# Optimizing a Trainium2 kernel written in Bass

```python
import jax, jax.numpy as jnp
from jax import lax
import numpy as np
import math

D_MODEL = 2048
BATCH = 1
SEQ = 256
DEPTH = 1

N_MEM = 256
EPS = 1e-6
CONV_WIDTH = D_MODEL
CONV_K = 31
GLA_HEADS = 4
GLA_DK = D_MODEL // 2
GLA_DV = D_MODEL
GLA_DKH = GLA_DK // GLA_HEADS
GLA_DVH = GLA_DV // GLA_HEADS
GLA_RANK = 16
GLA_TAU = 16.0
CHUNK = 64
MEM_HEADS = 4
MEM_HD = 128
MEM_WIDTH = MEM_HEADS * MEM_HD
N_BRANCH = 3

SPLIT_SIZES = [
    CONV_WIDTH,
    CONV_WIDTH,
    CONV_WIDTH,
    GLA_DK,
    GLA_DK,
    GLA_DV,
    GLA_DV,
    GLA_RANK,
    MEM_WIDTH,
    MEM_WIDTH,
    N_BRANCH * D_MODEL,
]
SPLITS = [int(s) for s in np.cumsum(SPLIT_SIZES)[:-1]]
D_IN = int(sum(SPLIT_SIZES))


def rmsnorm(x, g):
    xf = x.astype(jnp.float32)
    y = xf * lax.rsqrt(jnp.mean(xf * xf, axis=-1, keepdims=True) + EPS)
    return (y * g.astype(jnp.float32)).astype(x.dtype)

def layernorm(x, g, b):
    xf = x.astype(jnp.float32)
    mu = jnp.mean(xf, axis=-1, keepdims=True)
    var = jnp.mean(jnp.square(xf - mu), axis=-1, keepdims=True)
    y = (xf - mu) * lax.rsqrt(var + EPS)
    return (y * g.astype(jnp.float32) + b.astype(jnp.float32)).astype(x.dtype)

def causal_depthwise_conv(u, w, b):
    C = u.shape[-1]
    y = lax.conv_general_dilated(
        u, w[:, None, :].astype(u.dtype), window_strides=(1,),
        padding=[(CONV_K - 1, 0)],
        dimension_numbers=("NWC", "WIO", "NWC"),
        feature_group_count=C)
    return y + b.astype(u.dtype)

def gla_chunked(q, k, v, log_a):
    B, S, H, dk = q.shape
    dv = v.shape[-1]
    N = S // CHUNK

    def to_chunks(t):
        return t.astype(jnp.float32).reshape(B, N, CHUNK, H, t.shape[-1]).transpose(1, 0, 3, 2, 4)

    qc, kc, vc = to_chunks(q), to_chunks(k), to_chunks(v)
    bc = jnp.cumsum(to_chunks(log_a), axis=-2)
    mask = jnp.tril(jnp.ones((CHUNK, CHUNK), dtype=bool))[:, :, None]

    def step(state, inp):
        qi, ki, vi, bi = inp
        o_inter = jnp.einsum("bhtk,bhkv->bhtv", qi * jnp.exp(bi), state)
        diff = bi[:, :, :, None, :] - bi[:, :, None, :, :]
        decay = jnp.exp(jnp.where(mask, diff, -jnp.inf))
        scores = jnp.einsum("bhtk,bhsk,bhtsk->bhts", qi, ki, decay)
        o_intra = jnp.einsum("bhts,bhsv->bhtv", scores, vi)
        b_last = bi[:, :, -1, :]
        k_dec = ki * jnp.exp(b_last[:, :, None, :] - bi)
        state = jnp.exp(b_last)[..., None] * state + jnp.einsum("bhck,bhcv->bhkv", k_dec, vi)
        return state, o_inter + o_intra

    s0 = jnp.zeros((B, H, dk, dv), jnp.float32)
    _, o = lax.scan(step, s0, (qc, kc, vc, bc))
    return o.transpose(1, 0, 3, 2, 4).reshape(B, S, H, dv)

def first_inputs(seed: int = 0) -> dict:
    key = jax.random.key(seed)
    ks = jax.random.split(key, 24)
    f32 = jnp.float32
    L = DEPTH

    def nrm(k, shape, scale):
        return jax.random.normal(k, shape, f32) * scale

    return {
        "x": jax.random.normal(ks[0], (BATCH, SEQ, D_MODEL), f32),
        "mem": jax.random.normal(ks[1], (BATCH, N_MEM, D_MODEL), f32),
        "ln_in_g": 1.0 + nrm(ks[2], (L, D_MODEL), 0.02),
        "mem_ln_g": 1.0 + nrm(ks[3], (L, D_MODEL), 0.02),
        "w_in": nrm(ks[4], (L, D_MODEL, D_IN), D_MODEL ** -0.5),
        "b_gate": nrm(ks[5], (L, N_BRANCH * D_MODEL), 0.02),
        "dw_w": nrm(ks[6], (L, CONV_K, CONV_WIDTH), CONV_K ** -0.5),
        "dw_b": nrm(ks[7], (L, CONV_WIDTH), 0.02),
        "conv_ln_g": 1.0 + nrm(ks[8], (L, CONV_WIDTH), 0.02),
        "conv_ln_b": nrm(ks[9], (L, CONV_WIDTH), 0.02),
        "w_conv_out": nrm(ks[10], (L, CONV_WIDTH, D_MODEL), CONV_WIDTH ** -0.5),
        "b_conv_out": nrm(ks[11], (L, D_MODEL), 0.02),
        "w_alpha2": nrm(ks[12], (L, GLA_RANK, GLA_DK), GLA_RANK ** -0.5),
        "b_alpha": nrm(ks[13], (L, GLA_DK), 0.02),
        "gla_norm_g": 1.0 + nrm(ks[14], (L, GLA_DV), 0.02),
        "w_gla_out": nrm(ks[15], (L, GLA_DV, D_MODEL), GLA_DV ** -0.5),
        "w_mem_kv": nrm(ks[16], (L, D_MODEL, 2 * MEM_WIDTH), D_MODEL ** -0.5),
        "w_mem_out": nrm(ks[17], (L, MEM_WIDTH, D_MODEL), MEM_WIDTH ** -0.5),
        "w_out": nrm(ks[18], (L, D_MODEL, D_MODEL), D_MODEL ** -0.5),
        "final_g": 1.0 + nrm(ks[19], (D_MODEL,), 0.02),
    }

def first_block(x, mem, ln_in_g, mem_ln_g, w_in, b_gate, dw_w, dw_b, conv_ln_g, conv_ln_b,
              w_conv_out, b_conv_out, w_alpha2, b_alpha, gla_norm_g, w_gla_out,
              w_mem_kv, w_mem_out, w_out, final_g):
    B, S, D = x.shape
    M = mem.shape[1]
    for l in range(DEPTH):
        h = rmsnorm(x, ln_in_g[l])
        proj = h @ w_in[l]
        (conv_a, conv_b, conv_z, q, k, v, gla_z, alpha_lr, mq, mz, gate_pre) = jnp.split(proj, SPLITS, axis=-1)

        u = conv_a * jax.nn.sigmoid(conv_b)
        u = causal_depthwise_conv(u, dw_w[l], dw_b[l])
        u = jax.nn.silu(layernorm(u, conv_ln_g[l], conv_ln_b[l]))
        u = u * jax.nn.silu(conv_z)
        y_conv = u @ w_conv_out[l] + b_conv_out[l]

        log_a = jax.nn.log_sigmoid((alpha_lr @ w_alpha2[l] + b_alpha[l]).astype(jnp.float32)) / GLA_TAU
        qh = q.reshape(B, S, GLA_HEADS, GLA_DKH) * (GLA_DKH ** -0.5)
        kh = k.reshape(B, S, GLA_HEADS, GLA_DKH)
        vh = v.reshape(B, S, GLA_HEADS, GLA_DVH)
        o = gla_chunked(qh, kh, vh, log_a.reshape(B, S, GLA_HEADS, GLA_DKH)).astype(x.dtype)
        o = rmsnorm(o, gla_norm_g[l].reshape(GLA_HEADS, GLA_DVH)).reshape(B, S, GLA_DV)
        y_gla = (o * jax.nn.silu(gla_z)) @ w_gla_out[l]

        m = rmsnorm(mem, mem_ln_g[l])
        mk, mv = jnp.split(m @ w_mem_kv[l], 2, axis=-1)
        mk = mk.reshape(B, M, MEM_HEADS, MEM_HD)
        mv = mv.reshape(B, M, MEM_HEADS, MEM_HD)
        mqh = mq.reshape(B, S, MEM_HEADS, MEM_HD)
        sc = jnp.einsum("bshd,bmhd->bhsm", mqh.astype(jnp.float32), mk.astype(jnp.float32)) * (MEM_HD ** -0.5)
        p = jax.nn.softmax(sc, axis=-1).astype(x.dtype)
        om = jnp.einsum("bhsm,bmhd->bshd", p, mv).reshape(B, S, MEM_WIDTH)
        y_mem = (om * jax.nn.silu(mz)) @ w_mem_out[l]

        g = jax.nn.sigmoid(gate_pre + b_gate[l]).reshape(B, S, N_BRANCH, D)
        y = g[:, :, 0] * y_conv + g[:, :, 1] * y_gla + g[:, :, 2] * y_mem
        x = x + y @ w_out[l]
    return rmsnorm(x, final_g)


_first_inputs = first_inputs


def first_inputs(seed=0):
    import zlib

    import numpy as np

    out = dict(_first_inputs(seed))
    spreads = {}
    factors = {'ln_in_g': 3.97,
     'mem_ln_g': 8.0,
     'b_gate': 8.0,
     'dw_b': 7.159,
     'conv_ln_g': 8.0,
     'conv_ln_b': 8.0,
     'b_conv_out': 5.648,
     'b_alpha': 8.0,
     'gla_norm_g': 8.0,
     'final_g': 2.915}
    for name, (base, spread) in spreads.items():
        noise = np.random.default_rng([zlib.crc32(name.encode()), seed]).standard_normal(out[name].shape)
        drawn = base * np.exp(spread * noise) if base else spread * noise
        out[name] = __import__('jax').numpy.asarray(drawn.astype(out[name].dtype))
    for name, factor in factors.items():
        out[name] = (out[name] * factor).astype(out[name].dtype)
    return out


_narrow_inputs = first_inputs


def first_inputs(seed=0):

    out = dict(_narrow_inputs(seed))
    wider = {'conv_ln_g': 6.96,
     'conv_ln_b': 6.86,
     'b_conv_out': 12.0,
     'gla_norm_g': 4.89,
     'final_g': 3.27}
    for name, times in wider.items():
        mean = out[name].mean()
        out[name] = (mean + times * (out[name] - mean)).astype(out[name].dtype)
    return out


N_HEADS = 16
HEAD_DIM = 128
N_KV_HEADS = 4
KV_REP = N_HEADS // N_KV_HEADS
D_ATTN = N_HEADS * HEAD_DIM
D_KV = N_KV_HEADS * HEAD_DIM
IDX_HEADS = 8
IDX_DIM = 64
TOPK_MAX = 256
Q_BLOCK = 128
SGU_CHUNK = 128
SGU_GROUPS = 16
D_SGU = D_MODEL
SGU_GROUP_DIM = D_SGU // SGU_GROUPS
D_FF = 4 * D_MODEL
REL_BUCKETS = 32
REL_MAX_DIST = 128
N_BRANCHES = 2
COL_SIZES = (D_ATTN, D_KV, D_KV, IDX_HEADS * IDX_DIM, IDX_DIM, IDX_HEADS,
             D_SGU, D_SGU, D_MODEL, D_MODEL)
D_IN_2 = 2 * D_ATTN // 2 + 2 * D_KV + IDX_HEADS * IDX_DIM + IDX_DIM + IDX_HEADS + 2 * D_SGU + N_BRANCHES * D_MODEL


def rms_norm(x, g):
    xf = x.astype(jnp.float32)
    y = xf * lax.rsqrt(jnp.mean(xf * xf, axis=-1, keepdims=True) + EPS)
    return (y * g.astype(jnp.float32)).astype(x.dtype)

def layer_norm(x, g, b):
    xf = x.astype(jnp.float32)
    mu = jnp.mean(xf, axis=-1, keepdims=True)
    var = jnp.mean(jnp.square(xf - mu), axis=-1, keepdims=True)
    y = (xf - mu) * lax.rsqrt(var + EPS)
    return (y * g.astype(jnp.float32) + b.astype(jnp.float32)).astype(x.dtype)

def rel_bucket(dist):
    n = jnp.maximum(dist, 0)
    max_exact = REL_BUCKETS // 2
    nf = jnp.maximum(n, 1).astype(jnp.float32)
    large = max_exact + (jnp.log(nf / max_exact) / math.log(REL_MAX_DIST / max_exact)
                         * (REL_BUCKETS - max_exact)).astype(jnp.int32)
    large = jnp.minimum(large, REL_BUCKETS - 1)
    return jnp.where(n < max_exact, n, large)

def sparse_attention(q, k, v, qi, ki, wi, rel_bias):
    B, T = q.shape[0], q.shape[1]
    L = k.shape[1]
    top_k = min(TOPK_MAX, L // 4)
    nb = T // Q_BLOCK

    def to_blocks(a):
        return a.reshape((B, nb, Q_BLOCK) + a.shape[2:]).swapaxes(0, 1)

    starts = jnp.arange(nb, dtype=jnp.int32) * Q_BLOCK
    key_pos = jnp.arange(L, dtype=jnp.int32)
    ki32 = ki.astype(jnp.float32)
    idx_scale = (IDX_HEADS ** -0.5) * (IDX_DIM ** -0.5)

    def block(args):
        qb, qib, wib, start = args
        q_pos = start + jnp.arange(Q_BLOCK, dtype=jnp.int32)
        s = jnp.einsum('bqhd,bsd->bqhs', qib.astype(jnp.float32), ki32)
        score = jnp.einsum('bqh,bqhs->bqs', wib.astype(jnp.float32) * idx_scale, jax.nn.relu(s))
        causal = key_pos[None, :] <= q_pos[:, None]
        score = jnp.where(causal[None], score, -jnp.inf)
        _, idx = lax.top_k(score, top_k)
        valid = idx <= q_pos[None, :, None]
        k_sel = jax.vmap(lambda kb, ib: kb[ib])(k, idx)
        v_sel = jax.vmap(lambda vb, ib: vb[ib])(v, idx)
        qg = qb.reshape(B, Q_BLOCK, N_KV_HEADS, KV_REP, HEAD_DIM)
        logits = jnp.einsum('bqgrd,bqngd->bqgrn', qg, k_sel).astype(jnp.float32) * (HEAD_DIM ** -0.5)
        bucket = rel_bucket(q_pos[None, :, None] - idx)
        bias = rel_bias[bucket].astype(jnp.float32)
        bias = bias.reshape(B, Q_BLOCK, top_k, N_KV_HEADS, KV_REP).transpose(0, 1, 3, 4, 2)
        logits = jnp.where(valid[:, :, None, None, :], logits + bias, -1e30)
        p = jax.nn.softmax(logits, axis=-1).astype(v.dtype)
        o = jnp.einsum('bqgrn,bqngd->bqgrd', p, v_sel)
        return o.reshape(B, Q_BLOCK, D_ATTN)

    out = lax.map(block, (to_blocks(q), to_blocks(qi), to_blocks(wi), starts))
    return out.swapaxes(0, 1).reshape(B, T, D_ATTN)

def spatial_gating(u, v, ln_g, ln_b, w_s, b_s):
    B, T = v.shape[0], v.shape[1]
    nc = T // SGU_CHUNK
    vn = layer_norm(v, ln_g, ln_b)
    vc = vn.reshape(B, nc, SGU_CHUNK, SGU_GROUPS, SGU_GROUP_DIM)
    mask = jnp.tril(jnp.ones((SGU_CHUNK, SGU_CHUNK), dtype=bool))
    ws = jnp.where(mask[None], w_s, jnp.zeros_like(w_s))
    mixed = jnp.einsum('gts,bcsgd->bctgd', ws, vc) + b_s.T[None, None, :, :, None]
    return u * mixed.reshape(B, T, D_SGU)

def second_inputs(seed: int = 0) -> dict:
    key = jax.random.key(seed)
    ks = jax.random.split(key, 16)
    f32 = jnp.float32
    d_in = sum(COL_SIZES)
    x = jax.random.normal(ks[0], (BATCH, SEQ, D_MODEL), f32)
    rel_bias = 0.5 * jax.random.normal(ks[1], (REL_BUCKETS, N_HEADS), f32)
    norm1_g = 1.0 + 0.01 * jax.random.normal(ks[2], (DEPTH, D_MODEL), f32)
    w_in = jax.random.normal(ks[3], (DEPTH, D_MODEL, d_in), f32) * D_MODEL ** -0.5
    sgu_ln_g = 1.0 + 0.01 * jax.random.normal(ks[4], (DEPTH, D_SGU), f32)
    sgu_ln_b = 0.01 * jax.random.normal(ks[5], (DEPTH, D_SGU), f32)
    sgu_w = jax.random.normal(ks[6], (DEPTH, SGU_GROUPS, SGU_CHUNK, SGU_CHUNK), f32) * SGU_CHUNK ** -0.5
    sgu_b = 1.0 + 0.01 * jax.random.normal(ks[7], (DEPTH, SGU_GROUPS, SGU_CHUNK), f32)
    w_out = jax.random.normal(ks[8], (DEPTH, D_MODEL, D_MODEL), f32) * D_MODEL ** -0.5
    norm2_g = 1.0 + 0.01 * jax.random.normal(ks[9], (DEPTH, D_MODEL), f32)
    w_ff1 = jax.random.normal(ks[10], (DEPTH, D_MODEL, D_FF), f32) * D_MODEL ** -0.5
    w_ff2 = jax.random.normal(ks[11], (DEPTH, D_FF, D_MODEL), f32) * D_FF ** -0.5
    final_g = 1.0 + 0.01 * jax.random.normal(ks[12], (D_MODEL,), f32)
    return {"x": x, "rel_bias": rel_bias, "norm1_g": norm1_g, "w_in": w_in,
            "sgu_ln_g": sgu_ln_g, "sgu_ln_b": sgu_ln_b, "sgu_w": sgu_w, "sgu_b": sgu_b,
            "w_out": w_out, "norm2_g": norm2_g, "w_ff1": w_ff1, "w_ff2": w_ff2,
            "final_g": final_g}

def second_block(x, rel_bias, norm1_g, w_in, sgu_ln_g, sgu_ln_b, sgu_w, sgu_b,
              w_out, norm2_g, w_ff1, w_ff2, final_g):
    B, T, _ = x.shape
    split_pts = [int(p) for p in np.cumsum(COL_SIZES)[:-1]]
    for l in range(DEPTH):
        h = rms_norm(x, norm1_g[l])
        proj = jnp.einsum('btd,dc->btc', h, w_in[l])
        q, k, v, qi, ki, wi, u_s, v_s, ga, gb = jnp.split(proj, split_pts, axis=-1)
        q = q.reshape(B, T, N_HEADS, HEAD_DIM)
        k = k.reshape(B, T, N_KV_HEADS, HEAD_DIM)
        v = v.reshape(B, T, N_KV_HEADS, HEAD_DIM)
        qi = qi.reshape(B, T, IDX_HEADS, IDX_DIM)
        attn = sparse_attention(q, k, v, qi, ki, wi, rel_bias)
        sgu = spatial_gating(jax.nn.gelu(u_s), jax.nn.gelu(v_s),
                             sgu_ln_g[l], sgu_ln_b[l], sgu_w[l], sgu_b[l])
        merged = jax.nn.sigmoid(ga) * attn + jax.nn.sigmoid(gb) * sgu
        x = x + jnp.einsum('btc,cd->btd', merged, w_out[l])
        h2 = rms_norm(x, norm2_g[l])
        ff = jnp.square(jax.nn.relu(jnp.einsum('btd,df->btf', h2, w_ff1[l])))
        x = x + jnp.einsum('btf,fd->btd', ff, w_ff2[l])
    return rms_norm(x, final_g)


_first_inputs_2 = second_inputs


def second_inputs(seed=0):
    import zlib

    import numpy as np

    out = dict(_first_inputs_2(seed))
    spreads = {}
    factors = {}
    for name, (base, spread) in spreads.items():
        noise = np.random.default_rng([zlib.crc32(name.encode()), seed]).standard_normal(out[name].shape)
        drawn = base * np.exp(spread * noise) if base else spread * noise
        out[name] = __import__('jax').numpy.asarray(drawn.astype(out[name].dtype))
    for name, factor in factors.items():
        out[name] = (out[name] * factor).astype(out[name].dtype)
    return out


_narrow_inputs_2 = second_inputs


def second_inputs(seed=0):

    out = dict(_narrow_inputs_2(seed))
    wider = {'norm1_g': 5.01,
     'sgu_ln_g': 12.0,
     'sgu_ln_b': 12.0,
     'sgu_b': 12.0,
     'norm2_g': 7.29,
     'final_g': 6.55}
    for name, times in wider.items():
        mean = out[name].mean()
        out[name] = (mean + times * (out[name] - mean)).astype(out[name].dtype)
    return out


MLA_HEADS = 8
MLA_Q_RANK = 512
MLA_KV_RANK = 512
MLA_NOPE_DIM = 128
MLA_ROPE_DIM = 64
MLA_V_DIM = 128
MLA_WIDTH = MLA_HEADS * MLA_V_DIM
MLA_IN = MLA_Q_RANK + MLA_KV_RANK + MLA_ROPE_DIM
ROPE_THETA = 10000.0

RWKV_HEAD = 64
RWKV_HEADS = 16
RWKV_WIDTH = RWKV_HEADS * RWKV_HEAD
DECAY_RANK = 96
ICLR_RANK = 96
RWKV_SIZES = [RWKV_WIDTH, RWKV_WIDTH, RWKV_WIDTH, DECAY_RANK, DECAY_RANK, ICLR_RANK, ICLR_RANK]
RWKV_IN = sum(RWKV_SIZES)
GN_EPS = 64e-5
NORM_EPS = 1e-6

IN_SIZES = [MLA_IN, RWKV_IN, MLA_WIDTH, RWKV_WIDTH, D_MODEL, D_MODEL]
D_IN_3 = sum(IN_SIZES)


def _offsets(sizes):
    return [int(o) for o in np.cumsum(sizes)[:-1]]

def rms_norm_3(x, g, eps=NORM_EPS):
    xf = x.astype(jnp.float32)
    y = xf * lax.rsqrt(jnp.mean(xf * xf, axis=-1, keepdims=True) + eps)
    return (y * g.astype(jnp.float32)).astype(x.dtype)

def apply_rotary(t, cos, sin):
    tf = t.astype(jnp.float32)
    t1, t2 = jnp.split(tf, 2, axis=-1)
    return jnp.concatenate([t1 * cos - t2 * sin, t1 * sin + t2 * cos], axis=-1).astype(t.dtype)

def centred_shift(p):
    pad = jnp.pad(p, ((0, 0), (1, 1), (0, 0)))
    return 0.5 * (pad[:, :-2] + pad[:, 2:])

def mla_attention(q_nope, q_rope, k_nope, k_rope, v):
    B, S, H, _ = q_nope.shape
    nb = S // Q_BLOCK
    scale = (MLA_NOPE_DIM + MLA_ROPE_DIM) ** -0.5
    qn = q_nope.reshape(B, nb, Q_BLOCK, H, MLA_NOPE_DIM).transpose(1, 0, 2, 3, 4)
    qr = q_rope.reshape(B, nb, Q_BLOCK, H, MLA_ROPE_DIM).transpose(1, 0, 2, 3, 4)

    def block(args):
        qn_b, qr_b = args
        s = (jnp.einsum('bqhd,bkhd->bhqk', qn_b, k_nope, preferred_element_type=jnp.float32)
             + jnp.einsum('bqhr,bkr->bhqk', qr_b, k_rope, preferred_element_type=jnp.float32))
        p = jax.nn.softmax(s * scale, axis=-1)
        return jnp.einsum('bhqk,bkhd->bqhd', p.astype(v.dtype), v)

    o = lax.map(block, (qn, qr))
    return o.transpose(1, 0, 2, 3, 4).reshape(B, S, H * MLA_V_DIM)

def rwkv7_bidir_scan(r, w_f, w_b, k_f, k_b, v, kk, a_f, a_b):
    B, S, H, N = r.shape

    def tm(fwd, bwd):
        return jnp.stack([fwd, bwd[:, ::-1]], axis=0).transpose(2, 0, 1, 3, 4)

    xs = (tm(r, r), tm(w_f, w_b), tm(k_f, k_b), tm(v, v), tm(-kk, -kk), tm(kk * a_f, kk * a_b))

    def step(st, inp):
        r_t, w_t, k_t, v_t, a_t, b_t = inp
        sa = jnp.einsum('dbhij,dbhj->dbhi', st, a_t)
        st = st * w_t[..., None, :] + sa[..., None] * b_t[..., None, :] + v_t[..., None] * k_t[..., None, :]
        y = jnp.einsum('dbhij,dbhj->dbhi', st, r_t)
        return st, y

    s0 = jnp.zeros((2, B, H, N, N), jnp.float32)
    _, ys = lax.scan(step, s0, xs)
    y = ys[:, 0] + ys[::-1, 1]
    return y.transpose(1, 0, 2, 3)

def third_inputs(seed: int = 0) -> dict:
    key = jax.random.key(seed)
    ks = jax.random.split(key, 32)
    f32 = jnp.float32
    nrm = lambda k, shape, s: jax.random.normal(k, shape, f32) * s
    gain = lambda k, n: 1.0 + nrm(k, (n,), 0.02)
    return {
        "x": nrm(ks[0], (BATCH, SEQ, D_MODEL), 1.0),
        "g_pre": gain(ks[1], D_MODEL),
        "w_in": nrm(ks[2], (D_MODEL, D_IN_3), D_MODEL ** -0.5),
        "mla_q_norm": gain(ks[3], MLA_Q_RANK),
        "mla_wq_b": nrm(ks[4], (MLA_Q_RANK, MLA_HEADS * (MLA_NOPE_DIM + MLA_ROPE_DIM)), MLA_Q_RANK ** -0.5),
        "mla_kv_norm": gain(ks[5], MLA_KV_RANK),
        "mla_wkv_b": nrm(ks[6], (MLA_KV_RANK, MLA_HEADS * (MLA_NOPE_DIM + MLA_V_DIM)), MLA_KV_RANK ** -0.5),
        "rwkv_mu": jax.random.uniform(ks[7], (RWKV_IN,), f32),
        "rwkv_w0_f": nrm(ks[8], (RWKV_WIDTH,), 0.5),
        "rwkv_w2_f": nrm(ks[9], (DECAY_RANK, RWKV_WIDTH), 0.5 * DECAY_RANK ** -0.5),
        "rwkv_w0_b": nrm(ks[10], (RWKV_WIDTH,), 0.5),
        "rwkv_w2_b": nrm(ks[11], (DECAY_RANK, RWKV_WIDTH), 0.5 * DECAY_RANK ** -0.5),
        "rwkv_a0_f": nrm(ks[12], (RWKV_WIDTH,), 0.1),
        "rwkv_a2_f": nrm(ks[13], (ICLR_RANK, RWKV_WIDTH), 0.5 * ICLR_RANK ** -0.5),
        "rwkv_a0_b": nrm(ks[14], (RWKV_WIDTH,), 0.1),
        "rwkv_a2_b": nrm(ks[15], (ICLR_RANK, RWKV_WIDTH), 0.5 * ICLR_RANK ** -0.5),
        "rwkv_k_k": 0.85 + nrm(ks[16], (RWKV_WIDTH,), 0.02),
        "rwkv_k_a": gain(ks[17], RWKV_WIDTH),
        "rwkv_r_k": nrm(ks[18], (RWKV_HEADS, RWKV_HEAD), 0.1),
        "rwkv_gn_g": gain(ks[19], RWKV_WIDTH),
        "rwkv_gn_b": nrm(ks[20], (RWKV_WIDTH,), 0.01),
        "w_br_mla": nrm(ks[21], (MLA_WIDTH, D_MODEL), MLA_WIDTH ** -0.5),
        "w_br_rwkv": nrm(ks[22], (RWKV_WIDTH, D_MODEL), RWKV_WIDTH ** -0.5),
        "w_out": nrm(ks[23], (D_MODEL, D_MODEL), D_MODEL ** -0.5),
        "g_post": gain(ks[24], D_MODEL),
    }

def third_block(x, g_pre, w_in, mla_q_norm, mla_wq_b, mla_kv_norm, mla_wkv_b, rwkv_mu,
              rwkv_w0_f, rwkv_w2_f, rwkv_w0_b, rwkv_w2_b, rwkv_a0_f, rwkv_a2_f, rwkv_a0_b,
              rwkv_a2_b, rwkv_k_k, rwkv_k_a, rwkv_r_k, rwkv_gn_g, rwkv_gn_b, w_br_mla,
              w_br_rwkv, w_out, g_post):
    f32 = jnp.float32
    B, S, _ = x.shape
    pos = jnp.arange(S, dtype=f32)
    inv_freq = jnp.power(ROPE_THETA, -jnp.arange(0, MLA_ROPE_DIM, 2, dtype=f32) / MLA_ROPE_DIM)
    ang = pos[:, None] * inv_freq[None, :]
    cos, sin = jnp.cos(ang), jnp.sin(ang)

    for _layer in range(DEPTH):
        h = rms_norm_3(x, g_pre)
        proj = h @ w_in
        mla_in, rwkv_in, z_mla, z_rwkv, gate_mla, gate_rwkv = jnp.split(proj, _offsets(IN_SIZES), axis=-1)

        q_a, kv_a, k_rope = jnp.split(mla_in, _offsets([MLA_Q_RANK, MLA_KV_RANK, MLA_ROPE_DIM]), axis=-1)
        q = (rms_norm_3(q_a, mla_q_norm) @ mla_wq_b).reshape(B, S, MLA_HEADS, MLA_NOPE_DIM + MLA_ROPE_DIM)
        kv = (rms_norm_3(kv_a, mla_kv_norm) @ mla_wkv_b).reshape(B, S, MLA_HEADS, MLA_NOPE_DIM + MLA_V_DIM)
        q_nope, q_rope = q[..., :MLA_NOPE_DIM], q[..., MLA_NOPE_DIM:]
        k_nope, v_mla = kv[..., :MLA_NOPE_DIM], kv[..., MLA_NOPE_DIM:]
        q_rope = apply_rotary(q_rope, cos[:, None, :], sin[:, None, :])
        k_rope = apply_rotary(k_rope, cos, sin)
        y_mla = mla_attention(q_nope, q_rope, k_nope, k_rope, v_mla)

        rin = rwkv_in.astype(f32)
        rin = rin + rwkv_mu * (centred_shift(rin) - rin)
        r, k, v, wd_f, wd_b, ad_f, ad_b = jnp.split(rin, _offsets(RWKV_SIZES), axis=-1)

        def decay(w0, wd, w2):
            z = w0 + jnp.tanh(wd) @ w2
            return jnp.exp(-jnp.exp(-jax.nn.softplus(-z) - 0.5))

        w_f = decay(rwkv_w0_f.astype(f32), wd_f, rwkv_w2_f.astype(f32))
        w_b = decay(rwkv_w0_b.astype(f32), wd_b, rwkv_w2_b.astype(f32))
        a_f = jax.nn.sigmoid(rwkv_a0_f.astype(f32) + ad_f @ rwkv_a2_f.astype(f32))
        a_b = jax.nn.sigmoid(rwkv_a0_b.astype(f32) + ad_b @ rwkv_a2_b.astype(f32))

        hd = lambda t: t.reshape(B, S, RWKV_HEADS, RWKV_HEAD)
        kk = hd(k * rwkv_k_k.astype(f32))
        kk = kk / jnp.maximum(jnp.linalg.norm(kk, axis=-1, keepdims=True), 1e-12)
        k_a = rwkv_k_a.astype(f32)
        k_f = k * (1.0 + (a_f - 1.0) * k_a)
        k_b = k * (1.0 + (a_b - 1.0) * k_a)
        r_h, v_h, k_fh, k_bh = hd(r), hd(v), hd(k_f), hd(k_b)
        y = rwkv7_bidir_scan(r_h, hd(w_f), hd(w_b), k_fh, k_bh, v_h, kk, hd(a_f), hd(a_b))
        mu = jnp.mean(y, axis=-1, keepdims=True)
        var = jnp.mean(jnp.square(y - mu), axis=-1, keepdims=True)
        yn = ((y - mu) * lax.rsqrt(var + GN_EPS)).reshape(B, S, RWKV_WIDTH)
        yn = yn * rwkv_gn_g.astype(f32) + rwkv_gn_b.astype(f32)
        bonus = jnp.sum(r_h * (k_fh + k_bh) * rwkv_r_k.astype(f32), axis=-1, keepdims=True) * v_h
        y_rwkv = (yn + bonus.reshape(B, S, RWKV_WIDTH)).astype(x.dtype)

        u_mla = (y_mla * jax.nn.silu(z_mla)) @ w_br_mla
        u_rwkv = (y_rwkv * jax.nn.silu(z_rwkv)) @ w_br_rwkv
        merged = jax.nn.sigmoid(gate_mla) * u_mla + jax.nn.sigmoid(gate_rwkv) * u_rwkv
        out = merged @ w_out
        x = (x + rms_norm_3(out, g_post)).astype(x.dtype)
    return x


_first_inputs_3 = third_inputs


def third_inputs(seed=0):
    import zlib

    import numpy as np

    out = dict(_first_inputs_3(seed))
    spreads = {}
    factors = {'mla_q_norm': 8.0,
     'mla_kv_norm': 8.0,
     'rwkv_k_k': 64.0,
     'rwkv_k_a': 3.275,
     'rwkv_gn_g': 25.426,
     'rwkv_gn_b': 53.148,
     'g_post': 11.765,
     'rwkv_w2_f': 3.013,
     'rwkv_w2_b': 3.004}
    for name, (base, spread) in spreads.items():
        noise = np.random.default_rng([zlib.crc32(name.encode()), seed]).standard_normal(out[name].shape)
        drawn = base * np.exp(spread * noise) if base else spread * noise
        out[name] = __import__('jax').numpy.asarray(drawn.astype(out[name].dtype))
    for name, factor in factors.items():
        out[name] = (out[name] * factor).astype(out[name].dtype)
    return out


_narrow_inputs_3 = third_inputs


def third_inputs(seed=0):

    out = dict(_narrow_inputs_3(seed))
    wider = {'rwkv_k_k': 11.61, 'rwkv_r_k': 4.62, 'rwkv_gn_g': 3.35, 'rwkv_gn_b': 3.31, 'g_post': 3.21}
    for name, times in wider.items():
        mean = out[name].mean()
        out[name] = (mean + times * (out[name] - mean)).astype(out[name].dtype)
    return out


def setup_inputs(seed=0):
    out = dict(first_inputs(seed))
    for name, value in second_inputs(seed + 1).items():
        if name != "x":
            out[name + "_2"] = value
    for name, value in third_inputs(seed + 2).items():
        if name != "x":
            out[name + "_3"] = value
    return out


def reference(
    x, mem, ln_in_g, mem_ln_g, w_in, b_gate, dw_w, dw_b, conv_ln_g, conv_ln_b, w_conv_out,
    b_conv_out, w_alpha2, b_alpha, gla_norm_g, w_gla_out, w_mem_kv, w_mem_out, w_out, final_g,
    rel_bias_2, norm1_g_2, w_in_2, sgu_ln_g_2, sgu_ln_b_2, sgu_w_2, sgu_b_2, w_out_2, norm2_g_2,
    w_ff1_2, w_ff2_2, final_g_2, g_pre_3, w_in_3, mla_q_norm_3, mla_wq_b_3, mla_kv_norm_3,
    mla_wkv_b_3, rwkv_mu_3, rwkv_w0_f_3, rwkv_w2_f_3, rwkv_w0_b_3, rwkv_w2_b_3, rwkv_a0_f_3,
    rwkv_a2_f_3, rwkv_a0_b_3, rwkv_a2_b_3, rwkv_k_k_3, rwkv_k_a_3, rwkv_r_k_3, rwkv_gn_g_3,
    rwkv_gn_b_3, w_br_mla_3, w_br_rwkv_3, w_out_3, g_post_3,
):
    x = first_block(
        x, mem, ln_in_g, mem_ln_g, w_in, b_gate, dw_w, dw_b, conv_ln_g, conv_ln_b, w_conv_out,
        b_conv_out, w_alpha2, b_alpha, gla_norm_g, w_gla_out, w_mem_kv, w_mem_out, w_out,
        final_g,
    )
    x = second_block(
        x, rel_bias_2, norm1_g_2, w_in_2, sgu_ln_g_2, sgu_ln_b_2, sgu_w_2, sgu_b_2, w_out_2,
        norm2_g_2, w_ff1_2, w_ff2_2, final_g_2,
    )
    return third_block(
        x, g_pre_3, w_in_3, mla_q_norm_3, mla_wq_b_3, mla_kv_norm_3, mla_wkv_b_3, rwkv_mu_3,
        rwkv_w0_f_3, rwkv_w2_f_3, rwkv_w0_b_3, rwkv_w2_b_3, rwkv_a0_f_3, rwkv_a2_f_3,
        rwkv_a0_b_3, rwkv_a2_b_3, rwkv_k_k_3, rwkv_k_a_3, rwkv_r_k_3, rwkv_gn_g_3, rwkv_gn_b_3,
        w_br_mla_3, w_br_rwkv_3, w_out_3, g_post_3,
    )


_drawn_inputs = setup_inputs


def setup_inputs(seed=0):
    import zlib

    import numpy as np

    out = dict(_drawn_inputs(seed))
    spreads = {}
    factors = {}
    for name, (base, spread) in spreads.items():
        noise = np.random.default_rng([zlib.crc32(name.encode()), seed]).standard_normal(out[name].shape)
        drawn = base * np.exp(spread * noise) if base else spread * noise
        out[name] = __import__('jax').numpy.asarray(drawn.astype(out[name].dtype))
    for name, factor in factors.items():
        out[name] = (out[name] * factor).astype(out[name].dtype)
    return out
```

```python
from contextlib import ExitStack

import numpy as np
import concourse.bass as bass
from concourse import mybir

F32 = mybir.dt.float32
ACT = mybir.ActivationFunctionType
ALU = mybir.AluOpType
AX = mybir.AxisListType
P = 128
T = 256
TT = T // P
D = 2048
DC = D // P
EPS = 1e-6
GLA_HEADS, GLA_LEVELS = 4, 7
MEM_HEADS = 4
NEG = -1e30
BLOCKS = (1, 2, 3)


def stream_plan(blocks):
    plan = []

    def add(name, units, kc=DC, cols=256):
        plan.append((name, units, kc, cols))
    add("conv_a", 8); add("conv_b", 8); add("gla_q", 4); add("gla_k", 4); add("gla_v", 8)
    add("conv_z", 8); add("conv_out", 8); add("gate0", 8)
    add("alpha", 1, DC, 16); add("gla_z", 8); add("gla_out", 8); add("gate1", 8)
    add("mem_k", 2); add("mem_v", 2); add("mem_q", 2); add("mem_z", 2)
    add("mem_out", 8, 4); add("gate2", 8); add("w_out", 8)
    if 1 not in blocks:
        plan.clear()
    if 2 in blocks:
        add("sa_q", 8); add("sa_k", 2); add("sa_v", 2); add("sa_qi", 2); add("sa_ki", 1, DC, 128); add("sa_wi", 1, DC, 8)
        add("sgu_u", 8); add("sgu_v", 8); add("gate_a", 8); add("gate_b", 8); add("w_out_2", 8)
        for c in range(4):
            add(f"ff1_{c}", 8); add(f"ff2_{c}", 8)
    if 3 in blocks:
        add("rwkv_rk", 8); add("rwkv_v", 4); add("rwkv_da", 2, DC, 192)
        add("z_rwkv", 4); add("br_rwkv", 8, 8); add("gate_rwkv", 8)
        add("mla_qkv_a", 4); add("mla_k_rope", 1)
        add("mla_q_nope", 4, 4); add("mla_q_rope", 4, 4); add("mla_k_nope", 4, 4); add("mla_v", 4, 4)
        add("z_mla", 4); add("br_mla", 8, 8); add("gate_mla", 8); add("w_out_3", 8)
    return plan


VECS = [("ln_in_g", 16), ("mem_ln_g", 16), ("b_gate", 48), ("dw_b", 16), ("conv_ln_g", 16), ("conv_ln_b", 16),
        ("b_conv_out", 16), ("b_alpha", 8), ("gla_norm_g", 16), ("final_g", 16), ("dw_w", 16 * 31),
        ("g_pre_3", 16), ("mla_q_norm_3", 4), ("mla_kv_norm_3", 4), ("rwkv_mu_3", 28), ("rwkv_w0_f_3", 8), ("rwkv_w0_b_3", 8),
        ("rwkv_a0_f_3", 8), ("rwkv_a0_b_3", 8), ("rwkv_k_k_3", 8), ("rwkv_k_a_3", 8), ("rwkv_r_k_3", 8), ("rwkv_gn_g_3", 8),
        ("rwkv_gn_b_3", 8), ("g_post_3", 16), ("norm1_g_2", 16), ("norm2_g_2", 16), ("final_g_2", 16)]
VEC_AT = {}
_n = 0
for _name, _c in VECS:
    VEC_AT[_name] = _n
    _n += _c
NVEC = _n


class Stage:
    unit = 0
    gated = 0
    mids = 0


def build(nc, ins, out, blocks):
    plan = stream_plan(blocks)
    units = [(name, u, kc, cols) for name, n, kc, cols in plan for u in range(n)]

    with ExitStack() as ctx:
        def sb(name, shape):
            return ctx.enter_context(nc.sbuf_tensor(name, shape, F32))

        def sem(name):
            return ctx.enter_context(nc.semaphore(name))

        ring = [sb(f"ring{i}", [P, DC * 256]) for i in range(2)]
        arena = [sb(f"arena{i}", [P, DC, T]) for i in range(9)]
        X, H, Y, Tm = arena[0:4]
        tmp = [sb(f"act_tmp{i}", [P, 2, T]) for i in range(2)]
        tmp2 = [sb(f"dve_tmp{i}", [P, 2, T]) for i in range(2)]
        vecs = sb("vecs", [P, NVEC])
        ones = sb("ones", [P, P])
        ident = sb("ident", [P, P])
        stat = sb("stat", [P, 4, T])
        small = sb("small", [P, 64])
        psg = ctx.enter_context(nc.psum_tensor("ps_gemm", [P, 4, 512], F32))
        psa = ctx.enter_context(nc.psum_tensor("ps_aux", [P, 4, 512], F32))

        def vec(name, c):
            return vecs[:, bass.ds(c + VEC_AT[name], 1)]

        w_ready = [sem(f"w_ready{i}") for i in range(2)]
        units_done = sem("units_done")
        bank_free = sem("bank_free")
        act_ready = sem("act_ready")
        dve_mid = sem("dve_mid")
        const_in = sem("const_in")
        out_done = sem("out_done")
        st = Stage()

        def load_unit(sp, g, src_index=None):
            name, u, kc, cols = units[g]
            src = ins[name]
            ix = u if src_index is None else src_index
            sp.dma_start(ring[g % 2][:, 0:kc * cols],
                         src[bass.ds(ix, 1)].rearrange("a p n -> (a p) n")).then_inc(w_ready[g % 2], 16)

        def prefetch(sp, g0, n):
            g, end = g0 + 2, min(g0 + n + 2, len(units))
            while g < end:
                run = 1
                while g + run < end and units[g + run][0] == units[g][0]:
                    run += 1
                pairs = run // 2
                if pairs >= 2:
                    u0 = units[g][1]
                    with sp.Fori(0, pairs, 1) as i:
                        for j in range(2):
                            sp.wait_ge(units_done, 2 * i + (g + j - 1))
                            load_unit(sp, g + j, 2 * i + (u0 + j))
                    g += 2 * pairs
                    run -= 2 * pairs
                for _ in range(run):
                    sp.wait_ge(units_done, g - 1)
                    load_unit(sp, g)
                    g += 1

        def unit_loop(eng, n, body):
            if n >= 4:
                assert n % 2 == 0
                with eng.Fori(0, n // 2, 1) as i:
                    for j in range(2):
                        body(2 * i, j)
            else:
                for u in range(n):
                    body(u - u % 2, u % 2)

        def pe_product(pe, g0, n, rhs, natural):
            name, _, kc, cols = units[g0]
            cw = 96 if cols == 192 else min(cols, P)

            def body(i2, j):
                slot = (g0 + j) % 2
                w = ring[slot]
                pe.wait_ge(w_ready[slot], 16 * ((g0 + j) // 2 + 1) + 8 * i2)
                pe.wait_ge(bank_free, i2 + (g0 + j + 1))
                for c in range(TT if natural else cols // cw):
                    bank = psg[:, 2 * slot + c, :]
                    for k in range(kc):
                        if natural:
                            mm = nc.tensor.matmul(bank[:, 0:cols], rhs[:, k, c * P:(c + 1) * P],
                                                  w[:, k * cols:(k + 1) * cols], start=k == 0, stop=k == kc - 1)
                        else:
                            mm = nc.tensor.matmul(bank[0:cw, 0:T], w[:, k * cols + c * cw:k * cols + (c + 1) * cw],
                                                  rhs[:, k, :], start=k == 0, stop=k == kc - 1)
                mm.then_inc(units_done, 1)
            unit_loop(pe, n, body)

        class Prod:

            def __init__(s, name, rhs, kind, dst=None, src=None, bias=None, scale=1.0, natural=False, at=0, after=False, rows=P):
                s.g0 = st.unit
                assert units[s.g0][:2] == (name, 0), (units[s.g0], name)
                s.n = [x[1] for x in plan if x[0] == name][0]
                st.unit += s.n
                s.rhs, s.kind, s.dst, s.src, s.bias, s.scale, s.natural, s.at = rhs, kind, dst, src, bias, scale, natural, at
                s.after, s.rows = after, rows
                s.act0, s.mid0 = st.gated, st.mids
                if kind not in ("copy", "bias", "copy_small", "copy_narrow", "resid"):
                    st.gated += s.n
                if kind in ("silu_mul", "gate_add", "silu"):
                    st.mids += s.n * (0 if kind == "silu" else 1)

            def sp(s, sp):
                prefetch(sp, s.g0, s.n)

            def pe(s, pe):
                if s.after:
                    pe.wait_ge(bank_free, s.g0 + 2)
                pe_product(pe, s.g0, s.n, s.rhs, s.natural)

            def views(s, i2, j):
                slot = (s.g0 + j) % 2
                ps = psg[0:s.rows, 2 * slot:2 * slot + 2, 0:T]
                if s.kind == "copy_narrow":
                    return slot, psg[:, 2 * slot:2 * slot + 2, 0:s.dst.shape[2]], s.dst
                if s.natural:
                    d = s.dst[:, :, bass.ds(i2 * 256 + (j * 256 + s.at), 256)]
                elif s.kind != "copy_small":
                    d = s.dst[0:s.rows, bass.ds(2 * i2 + (2 * j + s.at), 2), :]
                else:
                    d = None
                return slot, ps, d

            def act(s, act):
                if s.kind == "resid":
                    return

                def body(i2, j):
                    slot, ps, d = s.views(i2, j)
                    act.wait_ge(units_done, i2 + (s.g0 + j + 1))
                    if s.kind in ("copy", "copy_narrow"):
                        nc.scalar.activation(d, ps, ACT.Copy, scale=s.scale).then_inc(bank_free, 1)
                        return
                    if s.kind == "copy_small":
                        nc.scalar.activation(s.dst, psg[0:s.dst.shape[0], 2 * slot, 0:T], ACT.Copy).then_inc(bank_free, 1)
                        return
                    if s.kind == "bias":
                        for c in range(2):
                            a = nc.scalar.activation(s.dst[:, bass.ds(2 * i2 + (2 * j + c), 1), :].rearrange("p a t -> p (a t)"),
                                                     ps[:, c, :], ACT.Identity, bias=vec(s.bias, 2 * i2 + (2 * j + c)))
                        a.then_inc(bank_free, 1)
                        return
                    act.wait_ge(bank_free, i2 + (s.g0 + j + 1))
                    if s.kind in ("gate_set", "gate_add") and s.bias:
                        for c in range(2):
                            a = nc.scalar.activation(tmp[slot][:, c, :], ps[:, c, :], ACT.Sigmoid,
                                                     bias=vec(s.bias[0], 2 * i2 + (2 * j + c + s.bias[1])))
                    else:
                        f = {"sig_mul": ACT.Sigmoid, "silu": ACT.Sigmoid, "silu_mul": ACT.Sigmoid, "gate_set": ACT.Sigmoid, "gate_add": ACT.Sigmoid, "relu2": ACT.Relu}[s.kind]
                        a = nc.scalar.activation(tmp[slot][:, :, :], ps, f)
                    a.then_inc(act_ready, 1)
                unit_loop(act, s.n, body)

            def dve(s, dve):
                if s.kind in ("copy", "bias", "copy_small", "copy_narrow"):
                    return
                dve.wait_ge(bank_free, s.g0 + 2)

                def body(i2, j):
                    slot, ps, d = s.views(i2, j)
                    if s.kind == "resid":
                        dve.wait_ge(units_done, i2 + (s.g0 + j + 1))
                        nc.vector.tensor_tensor(d, ps, d, ALU.add).then_inc(bank_free, 1)
                        return
                    dve.wait_ge(act_ready, i2 + (s.act0 + j + 1))
                    t = tmp[slot][:, :, :]
                    if s.kind == "sig_mul":
                        last = nc.vector.tensor_tensor(d, t, d, ALU.mult)
                    elif s.kind == "silu":
                        last = nc.vector.tensor_tensor(d, ps, t, ALU.mult)
                    elif s.kind == "relu2":
                        last = nc.vector.tensor_tensor(d, t, t, ALU.mult)
                    elif s.kind == "gate_set":
                        last = nc.vector.tensor_tensor(d, t, s.src[:, bass.ds(2 * i2 + 2 * j, 2), :], ALU.mult)
                    else:
                        if s.kind == "silu_mul":
                            a = nc.vector.tensor_tensor(tmp2[slot][:, :, :], ps, t, ALU.mult)
                        else:
                            a = nc.vector.tensor_tensor(tmp2[slot][:, :, :], t, s.src[:, bass.ds(2 * i2 + 2 * j, 2), :], ALU.mult)
                        a.then_inc(dve_mid, 1)
                        dve.wait_ge(dve_mid, i2 + (s.mid0 + j + 1))
                        last = nc.vector.tensor_tensor(d, tmp2[slot][:, :, :], d,
                                                       ALU.mult if s.kind == "silu_mul" else ALU.add)
                    last.then_inc(bank_free, 1)
                unit_loop(dve, s.n, body)

        def products(*args, dve_side=None):
            prods = [Prod(*a[0], **a[1]) for a in args]
            with nc.Block() as block:
                @block.sync
                def _(sp):
                    for p in prods:
                        p.sp(sp)

                @block.tensor
                def _(pe):
                    for p in prods:
                        p.pe(pe)

                @block.scalar
                def _(act):
                    for p in prods:
                        p.act(act)

                @block.vector
                def _(dve):
                    for p in prods:
                        p.dve(dve)
                    if dve_side:
                        dve_side(dve)

        def G(*a, **k):
            return (a, k)

        nstage = [0]

        def stage_sems(*names):
            nstage[0] += 1
            return [sem(f"s{nstage[0]}_{n}") for n in names]

        def linker(eng, chain):
            count = [0]

            def link(x):
                count[0] += 1
                x.then_inc(chain, 1)
                eng.wait_ge(chain, count[0])
            return link

        def vcol(name, c):
            return vecs[:, VEC_AT[name] + c:VEC_AT[name] + c + 1]

        def flat(buf, a, b):
            return buf[:, a:b, :].rearrange("p c t -> p (c t)")

        sq_ready, sums_done, root_in, root_done, chain, normed = [
            sem("norm_" + n) for n in ("sq_ready", "sums_done", "root_in", "root_done", "dve_chain", "normed")]
        norm_base = [0] * 6

        def norm(src, dst, n, gain, scratch, mean=False, bias=None, silu=False, gain_at=0, groups=1):
            b_sq, b_sums, b_in, b_root, b_chain, b_norm = norm_base
            tot = n * groups
            count = [0]
            with nc.Block() as block:
                @block.scalar
                def _(act):
                    h = max(tot // 4, 1)
                    for a in range(0, tot, h):
                        nc.scalar.activation(scratch[:, a:a + h, :], src[:, a:a + h, :], ACT.Square).then_inc(sq_ready, 1)
                    for g in range(groups):
                        act.wait_ge(root_in, b_in + g + 1)
                        nc.scalar.activation(stat[:, 2, :], stat[:, 1, :], ACT.Sqrt).then_inc(root_done, 1)
                    if silu:
                        for c in range(tot):
                            act.wait_ge(normed, b_norm + c + 1)
                            nc.scalar.activation(scratch[:, c, :], dst[:, c, :], ACT.Sigmoid).then_inc(root_done, 1)

                @block.tensor
                def _(pe):
                    h = max(tot // 4, 1)
                    for g in range(groups):
                        if g:
                            pe.wait_ge(root_in, b_in + g)
                        if mean:
                            for c in range(n):
                                nc.tensor.matmul(psa[:, 1, 0:T], ones[:, :], src[:, g * n + c, :], start=c == 0, stop=c == n - 1)
                        for c in range(n):
                            pe.wait_ge(sq_ready, b_sq + (g * n + c) // h + 1)
                            mm = nc.tensor.matmul(psa[:, 0, 0:T], ones[:, :], scratch[:, g * n + c, :], start=c == 0, stop=c == n - 1)
                        mm.then_inc(sums_done, 1)

                @block.vector
                def _(dve):
                    def link(x):
                        count[0] += 1
                        x.then_inc(chain, 1)
                        dve.wait_ge(chain, b_chain + count[0])
                    for g in range(groups):
                        dve.wait_ge(sums_done, b_sums + g + 1)
                        inv = 1.0 / (n * P)
                        if mean:
                            link(nc.vector.tensor_scalar(stat[:, 0, :], psa[:, 1, 0:T], inv, None, ALU.mult))
                            link(nc.vector.tensor_tensor(stat[:, 3, :], stat[:, 0, :], stat[:, 0, :], ALU.mult))
                            link(nc.vector.tensor_scalar(stat[:, 1, :], psa[:, 0, 0:T], inv, EPS, ALU.mult, ALU.add))
                            nc.vector.tensor_tensor(stat[:, 1, :], stat[:, 1, :], stat[:, 3, :], ALU.subtract).then_inc(root_in, 1)
                        else:
                            nc.vector.tensor_scalar(stat[:, 1, :], psa[:, 0, 0:T], inv, EPS, ALU.mult, ALU.add).then_inc(root_in, 1)
                        dve.wait_ge(root_done, b_root + g + 1)
                        link(nc.vector.reciprocal(stat[:, 3, :], stat[:, 2, :]))
                        if mean:
                            link(nc.vector.tensor_tensor(stat[:, 0, :], stat[:, 0, :], stat[:, 3, :], ALU.mult))
                        for c in range(g * n, g * n + n):
                            if not mean:
                                x = nc.vector.scalar_tensor_tensor(out=dst[:, c, :], in0=src[:, c, :], scalar=vecs[:, VEC_AT[gain] + gain_at + c:VEC_AT[gain] + gain_at + c + 1],
                                                                   in1=stat[:, 3, :], op0=ALU.mult, op1=ALU.mult)
                                if c == g * n + n - 1:
                                    link(x)
                            else:
                                link(nc.vector.tensor_tensor(dst[:, c, :], src[:, c, :], stat[:, 3, :], ALU.mult))
                                link(nc.vector.tensor_tensor(dst[:, c, :], dst[:, c, :], stat[:, 0, :], ALU.subtract))
                                x = nc.vector.tensor_scalar(dst[:, c, :], dst[:, c, :], vecs[:, VEC_AT[gain] + c:VEC_AT[gain] + c + 1],
                                                            vecs[:, VEC_AT[bias] + c:VEC_AT[bias] + c + 1], ALU.mult, ALU.add)
                                x.then_inc(normed, 1)
                    if silu:
                        for c in range(tot):
                            dve.wait_ge(root_done, b_root + groups + c + 1)
                            nc.vector.tensor_tensor(dst[:, c, :], dst[:, c, :], scratch[:, c, :], ALU.mult)
            for i, more in enumerate((-(-tot // max(tot // 4, 1)), groups, groups, groups + (tot if silu else 0), count[0], tot if mean else 0)):
                norm_base[i] += more

        def attention(nh, qk, v, o, pbuf, ptbuf, mask=None):
            (qk_done, mx_done, exp_done, p_done, chain, tr_done, trc_done, o_done, oc_done) = stage_sems(
                "qk_done", "mx_done", "exp_done", "p_done", "dve_chain", "tr_done", "trc_done", "o_done", "oc_done")
            with nc.Block() as block:
                @block.tensor
                def _(pe):
                    def scores(h):
                        if h >= 2:
                            pe.wait_ge(exp_done, h - 1)
                        mm = qk(h, psa[:, h % 2, :])
                        mm.then_inc(qk_done, 1)
                    scores(0)
                    for h in range(nh):
                        if h + 1 < nh:
                            scores(h + 1)
                        pe.wait_ge(p_done, h + 1)
                        if h:
                            pe.wait_ge(trc_done, h)
                        for s in range(TT):
                            for t in range(TT):
                                mm = nc.tensor.transpose(psa[:, 2, s * T + t * P:s * T + (t + 1) * P],
                                                         pbuf[:, h % 2, t, s * P:(s + 1) * P], ident[:, :])
                        mm.then_inc(tr_done, 1)
                        pe.wait_ge(trc_done, h + 1)
                        if h:
                            pe.wait_ge(oc_done, h)
                        for s in range(TT):
                            mm = nc.tensor.matmul(psa[:, 3, 0:T], v(h, s), ptbuf[:, h % 2, s, :], start=s == 0, stop=s == TT - 1)
                        mm.then_inc(o_done, 1)

                @block.vector
                def _(dve):
                    count = [0]

                    def link(x):
                        count[0] += 1
                        x.then_inc(chain, 1)
                        dve.wait_ge(chain, count[0])

                    def maximum(h):
                        dve.wait_ge(qk_done, h + 1)
                        ps = psa[:, h % 2, :].rearrange("p (t s) -> p t s", t=TT)
                        src = ps
                        if mask is not None:
                            if h >= 2:
                                dve.wait_ge(tr_done, h - 1)
                            link(nc.vector.tensor_tensor(pbuf[:, h % 2, :, :], ps, mask, ALU.add))
                            src = pbuf[:, h % 2, :, :]
                        nc.vector.tensor_reduce(small[:, 4 * (h % 2):4 * (h % 2) + 2], src, AX.X, ALU.max, negate=True).then_inc(mx_done, 1)
                    maximum(0)
                    for h in range(nh):
                        if h + 1 < nh:
                            maximum(h + 1)
                        b = 8 + 4 * (h % 2)
                        dve.wait_ge(exp_done, h + 1)
                        link(nc.vector.reciprocal(small[:, b + 2:b + 4], small[:, b:b + 2]))
                        for t in range(TT):
                            x = nc.vector.tensor_scalar(pbuf[:, h % 2, t, :], pbuf[:, h % 2, t, :], small[:, b + 2 + t:b + 3 + t], None, ALU.mult)
                        x.then_inc(p_done, 1)
                        dve.wait_ge(o_done, h + 1)
                        nc.vector.tensor_copy(o(h), psa[:, 3, 0:T]).then_inc(oc_done, 1)

                @block.scalar
                def _(act):
                    def exps(h):
                        act.wait_ge(mx_done, h + 1)
                        if h >= 2:
                            act.wait_ge(tr_done, h - 1)
                        for t in range(TT):
                            src = psa[:, h % 2, t * T:(t + 1) * T] if mask is None else pbuf[:, h % 2, t, :]
                            x = nc.scalar.activation(pbuf[:, h % 2, t, :], src, ACT.Exp, bias=small[:, 4 * (h % 2) + t:4 * (h % 2) + t + 1],
                                                     accum_out=small[:, 8 + 4 * (h % 2) + t:9 + 4 * (h % 2) + t])
                        x.then_inc(exp_done, 1)
                    exps(0)
                    for h in range(nh):
                        if h + 1 < nh:
                            exps(h + 1)
                        act.wait_ge(tr_done, h + 1)
                        if h >= 2:
                            act.wait_ge(o_done, h - 1)
                        nc.scalar.activation(ptbuf[:, h % 2, :, :], psa[:, 2, :].rearrange("p (s t) -> p s t", s=TT), ACT.Copy).then_inc(trc_done, 1)

        consts = [("x_t", X[:, :, :]), ("vecs", vecs[:, :]), ("ones", ones[:, :]), ("ident", ident[:, :])]
        with nc.Block() as block:
            @block.sync
            def _(sp):
                for name, dst in consts:
                    sp.dma_start(dst, ins[name]).then_inc(const_in, 16)
                for g in range(2):
                    load_unit(sp, g)
                sp.wait_ge(const_in, 16 * len(consts))

            @block.scalar
            def _(act):
                act.sem_inc(bank_free, 2)

        S = arena

        def load_consts(*pairs):
            (loaded,) = stage_sems("consts_in")
            with nc.Block() as block:
                @block.sync
                def _(sp):
                    for name, dst in pairs:
                        sp.dma_start(dst, ins[name]).then_inc(loaded, 16)
                    sp.wait_ge(loaded, 16 * len(pairs))

        def block_1(own):
            def sb(name, shape):
                return own.enter_context(nc.sbuf_tensor(name, shape, F32))
            masks = sb("level_masks", [P, 8, P])
            alpha_t = sb("alpha_t", [16, T])
            wal2 = sb("w_alpha2_sb", [16, 1024])
            sc = sb("gla_sc", [P, 8, P])
            stt = sb("gla_st", [P, 2, T])
            load_consts(("level_masks", masks[:, :, :]), ("w_alpha2", wal2[:, :]))
            norm(X, H, DC, "ln_in_g", S[4])
            U, CV = S[4], S[5]
            products(G("conv_a", H, "copy", dst=U), G("conv_b", H, "sig_mul", dst=U))

            (conv_step,) = stage_sems("conv_step")
            K31 = 31

            def conv_side(dve):
                with dve.Fori(0, DC, 1) as c:
                    w0 = VEC_AT["dw_w"]

                    def ch(buf, a, b):
                        return buf[:, bass.ds(c, 1), a:b].rearrange("p a t -> p (a t)")
                    nc.vector.tensor_scalar(ch(CV, 0, T), ch(U, 0, T), vecs[:, bass.ds(c * K31 + (w0 + K31 - 1), 1)],
                                            vec("dw_b", c), ALU.mult, ALU.add).then_inc(conv_step, 1)
                    for lag in range(1, K31):
                        dve.wait_ge(conv_step, c * K31 + lag)
                        nc.vector.scalar_tensor_tensor(out=ch(CV, lag, T), in0=ch(U, 0, T - lag),
                                                       scalar=vecs[:, bass.ds(c * K31 + (w0 + K31 - 1 - lag), 1)],
                                                       in1=ch(CV, lag, T), op0=ALU.mult, op1=ALU.add).then_inc(conv_step, 1)
            QK, V = S[6], S[7]
            Vn = V[:, :, :].rearrange("p c t -> p (c t)").rearrange("p (t n) -> p t n", t=TT)
            products(G("gla_q", H, "copy", dst=QK, scale=1.0 / 16), G("gla_k", H, "copy", dst=QK, at=8),
                     G("gla_v", H, "copy", dst=Vn, natural=True), dve_side=conv_side)
            norm(CV, CV, DC, "conv_ln_g", S[8], mean=True, bias="conv_ln_b", silu=True)
            products(G("conv_z", H, "silu_mul", dst=CV), G("conv_out", CV, "bias", after=True, dst=Tm, bias="b_conv_out"),
                     G("gate0", H, "gate_set", dst=Y, src=Tm, bias=("b_gate", 0)))
            products(G("alpha", H, "copy_small", dst=alpha_t[:, :]))

            B, LA = S[4], S[5]
            za, zb, zc, zd = stage_sems("z_done", "z_moved", "steps", "act_steps")
            with nc.Block() as block:
                @block.tensor
                def _(pe):
                    for c in range(8):
                        mm = nc.tensor.matmul(psa[:, c // 2, (c % 2) * T:(c % 2 + 1) * T], wal2[0:16, c * P:(c + 1) * P],
                                              alpha_t[0:16, :], start=True, stop=True)
                    mm.then_inc(za, 1)

                @block.vector
                def _(dve):
                    count = [0]

                    def link(x):
                        count[0] += 1
                        x.then_inc(zc, 1)
                        dve.wait_ge(zc, count[0])
                    dve.wait_ge(za, 1)
                    for c in range(8):
                        x = nc.vector.tensor_scalar(B[:, c, :], psa[:, c // 2, (c % 2) * T:(c % 2 + 1) * T], vecs[:, VEC_AT["b_alpha"] + c:VEC_AT["b_alpha"] + c + 1], None, ALU.add)
                    link(x)
                    nc.vector.scalar_tensor_tensor(out=LA[:, 0:8, :], in0=B[:, 0:8, :], scalar=-1.0, in1=B[:, 0:8, :], op0=ALU.mult, op1=ALU.min).then_inc(zb, 1)
                    link(nc.vector.tensor_scalar(B[:, 0:8, :], B[:, 0:8, :], 0.0, None, ALU.min))
                    dve.wait_ge(zd, 2)
                    link(nc.vector.tensor_tensor(LA[:, 0:8, :], B[:, 0:8, :], LA[:, 8:16, :], ALU.subtract))
                    link(nc.vector.tensor_scalar(LA[:, 0:8, :], LA[:, 0:8, :], 1.0 / 16, None, ALU.mult))
                    for c in range(8):
                        nc.vector.tensor_tensor_scan(B[:, c, :], LA[:, c, :], LA[:, c, :], 0.0, ALU.add, ALU.bypass)

                @block.scalar
                def _(act):
                    act.wait_ge(zb, 1)
                    nc.scalar.activation(LA[:, 0:8, :], LA[:, 0:8, :], ACT.Exp).then_inc(zd, 1)
                    act.wait_ge(zd, 1)
                    nc.scalar.activation(LA[:, 8:16, :], LA[:, 0:8, :], ACT.Ln, bias=1.0).then_inc(zd, 1)

            E, Q2 = S[8], S[5]
            O = S[3]
            e1, e2, ds_, es, qd, od, ev, oc = stage_sems("diff_ready", "exp_ready", "dve_steps", "top_done", "ops_ready", "levels_done", "scores_ready", "o_done")
            with nc.Block() as block:
                @block.vector
                def _(dve):
                    count = [0]

                    def link(x):
                        count[0] += 1
                        x.then_inc(ds_, 1)
                        dve.wait_ge(ds_, count[0])
                    for h in range(GLA_HEADS):
                        if h:
                            dve.wait_ge(es, h)
                        bh = B[:, 2 * h:2 * h + 2, :].rearrange("p c t -> p (c t)")
                        for m in range(8):
                            size = 2 << m
                            bv = bh.rearrange("p (n s) -> p n s", s=size)
                            r = bv[:, :, size // 2 - 1:size // 2].broadcast_to([P, 2 * T // size, size])
                            x = nc.vector.tensor_tensor(E[:, 2 * m:2 * m + 2, :].rearrange("p c t -> p (c t)").rearrange("p (n s) -> p n s", s=size),
                                                        bv, r, ALU.subtract)
                        x.then_inc(e1, 1)
                        dve.wait_ge(e2, 2 * h + 2)
                        Ev = E[:, :, :].rearrange("p (l c) t -> p l (c t)", l=8)
                        qh = QK[:, 2 * h:2 * h + 2, :].rearrange("p c t -> p (c t)")
                        kh = QK[:, 8 + 2 * h:10 + 2 * h, :].rearrange("p c t -> p (c t)")
                        link(nc.vector.tensor_tensor(Q2[:, :, :].rearrange("p (l c) t -> p l (c t)", l=8), Ev,
                                                     qh.rearrange("p (a n) -> p a n", a=1).broadcast_to([P, 8, 2 * T]), ALU.mult))
                        nc.vector.tensor_tensor(Ev, Ev, kh.rearrange("p (a n) -> p a n", a=1).broadcast_to([P, 8, 2 * T]), ALU.mult).then_inc(qd, 1)
                        for t in range(TT):
                            dve.wait_ge(od, 2 * h + t + 1)
                            ps = psa[:, 0:2, :].rearrange("p b (l t) -> p (b l) t", l=4)
                            link(nc.vector.tensor_tensor(sc[:, :, :], ps, masks[:, :, :], ALU.mult))
                            nc.vector.tensor_reduce(stt[:, t, t * P:(t + 1) * P], sc[:, :, :].rearrange("p l t -> p t l"), AX.X, ALU.add).then_inc(ev, 1)
                        dve.wait_ge(es, h + 1)
                        nc.vector.tensor_copy(stt[:, 0, P:T], psa[:, 2, 0:P]).then_inc(ev, 1)
                        for c in range(4):
                            dve.wait_ge(oc, 2 * (4 * h + c) + 1)
                            nc.vector.tensor_copy(O[:, 4 * h + c, :], psa[:, 3, 0:T]).then_inc(oc, 1)

                @block.scalar
                def _(act):
                    for h in range(GLA_HEADS):
                        act.wait_ge(e1, h + 1)
                        nc.scalar.activation(E[:, :, :], E[:, :, :], ACT.Abs).then_inc(e2, 1)
                        act.wait_ge(e2, 2 * h + 1)
                        nc.scalar.activation(E[:, :, :], E[:, :, :], ACT.Exp, scale=-1.0).then_inc(e2, 1)

                @block.tensor
                def _(pe):
                    for h in range(GLA_HEADS):
                        pe.wait_ge(qd, h + 1)
                        for t in range(TT):
                            if h or t:
                                pe.wait_ge(ev, 3 * h + t)
                            tk = slice(t * P, (t + 1) * P)
                            for l in range(8):
                                for c in range(2):
                                    kk = E[:, 2 * l + c, tk] if l < GLA_LEVELS else QK[:, 8 + 2 * h + c, tk]
                                    qq = Q2[:, 2 * l + c, tk] if l < GLA_LEVELS else QK[:, 2 * h + c, tk]
                                    mm = nc.tensor.matmul(psa[:, l // 4, (l % 4) * P:(l % 4 + 1) * P], kk, qq, start=c == 0, stop=c == 1)
                            mm.then_inc(od, 1)
                        for c in range(2):
                            mm = nc.tensor.matmul(psa[:, 2, 0:P], E[:, 14 + c, 0:P], Q2[:, 14 + c, P:T], start=c == 0, stop=c == 1)
                        mm.then_inc(es, 1)
                        pe.wait_ge(ev, 3 * h + 3)
                        for c in range(4):
                            if h or c:
                                pe.wait_ge(oc, 2 * (4 * h + c))
                            col = (4 * h + c) * P
                            nc.tensor.matmul(psa[:, 3, 0:T], Vn[:, 0, col:col + P], stt[:, 0, :], start=True, stop=False)
                            nc.tensor.matmul(psa[:, 3, P:T], Vn[:, 1, col:col + P], stt[:, 1, P:T], start=False, stop=True).then_inc(oc, 1)

            norm(O, CV, 4, "gla_norm_g", S[8], groups=4)
            products(G("gla_z", H, "silu_mul", dst=CV), G("gla_out", CV, "copy", after=True, dst=Tm),
                     G("gate1", H, "gate_add", dst=Y, src=Tm, bias=("b_gate", 16)))

            M, MH, MQ, MV = S[4], S[5], S[6], S[7]
            (mem_in,) = stage_sems("mem_in")
            with nc.Block() as block:
                @block.sync
                def _(sp):
                    sp.dma_start(M[:, :, :], ins["mem_t"]).then_inc(mem_in, 16)
                    sp.wait_ge(mem_in, 16)
            norm(M, MH, DC, "mem_ln_g", S[8])
            MVn = MV[:, 0:4, :].rearrange("p c t -> p (c t)").rearrange("p (t n) -> p t n", t=TT)
            products(G("mem_k", MH, "copy", dst=MQ), G("mem_v", MH, "copy", dst=MVn, natural=True),
                     G("mem_q", H, "copy", dst=MQ, at=4, scale=float(128 ** -0.5)))

            def mem_qk(h, ps):
                for t in range(TT):
                    mm = nc.tensor.matmul(ps[:, t * T:(t + 1) * T], MQ[:, 4 + h, t * P:(t + 1) * P], MQ[:, h, :], start=True, stop=True)
                return mm
            PB = S[8][:, 0:4, :].rearrange("p (b t) s -> p b t s", b=2)
            PT = S[8][:, 4:8, :].rearrange("p (b t) s -> p b t s", b=2)
            attention(MEM_HEADS, mem_qk, lambda h, s: MVn[:, s, h * P:(h + 1) * P], lambda h: MQ[:, 8 + h, :], PB, PT)
            products(G("mem_z", H, "silu_mul", dst=MQ, at=8), G("mem_out", MQ[:, 8:12, :], "copy", after=True, dst=Tm),
                     G("gate2", H, "gate_add", dst=Y, src=Tm, bias=("b_gate", 32)))
            products(G("w_out", Y, "resid", dst=X))
            norm(X, X, DC, "final_g", S[4])


        def block_3(own):
            norm(X, H, DC, "g_pre_3", S[4])
            with ExitStack() as rwkv_mem:
                rwkv(rwkv_mem)
            with ExitStack() as mla_mem:
                mla(mla_mem)
            products(G("w_out_3", Y, "copy", dst=Tm))
            norm(Tm, Tm, DC, "g_post_3", S[4])
            (added,) = stage_sems("added")
            with nc.Block() as block:
                @block.vector
                def _(dve):
                    nc.vector.tensor_tensor(X[:, :, :], X[:, :, :], Tm[:, :, :], ALU.add).then_inc(added, 1)

        NC8 = 8
        CH = 64
        NCH = T // CH

        def rwkv(own):
            def sb(name, shape):
                return own.enter_context(nc.sbuf_tensor(name, shape, F32))
            RK, VD, LW, AA = S[2], S[3], S[4], S[5]
            products(G("rwkv_rk", H, "copy", dst=RK), G("rwkv_v", H, "copy", dst=VD),
                     G("rwkv_da", H, "copy", dst=VD, at=8, rows=96))

            blk = sb("head_ones", [P, P])
            load_consts(("head_ones", blk[:, :]), ("rwkv_w2", S[6][0:96, :, :]))
            TS = S[7]
            steps, tanh_in, tanh_out = stage_sems("dve_steps", "tanh_in", "tanh_out")
            with nc.Block() as block:
                @block.vector
                def _(dve):
                    link = linker(dve, steps)
                    for buf, rows, a, b, mu in ((RK, P, 0, 16, 0), (VD, P, 0, 8, 16), (VD, 96, 8, 12, 24)):
                        x = buf[0:rows, a:b, :]
                        y = TS[0:rows, 0:b - a, :]
                        nc.vector.tensor_tensor(y[:, :, 1:T - 1], x[:, :, 0:T - 2], x[:, :, 2:T], ALU.add)
                        nc.vector.tensor_copy(y[:, :, 0:1], x[:, :, 1:2])
                        link(nc.vector.tensor_copy(y[:, :, T - 1:T], x[:, :, T - 2:T - 1]))
                        link(nc.vector.scalar_tensor_tensor(out=y, in0=y, scalar=0.5, in1=x, op0=ALU.mult, op1=ALU.subtract))
                        for c in range(b - a):
                            z = nc.vector.scalar_tensor_tensor(out=x[:, c, :], in0=y[:, c, :], scalar=vecs[0:rows, VEC_AT["rwkv_mu_3"] + mu + c:VEC_AT["rwkv_mu_3"] + mu + c + 1],
                                                               in1=x[:, c, :], op0=ALU.mult, op1=ALU.add)
                        link(z)
                    nc.vector.tensor_copy(small[:, 0:1], vecs[:, 0:1]).then_inc(tanh_in, 1)

                @block.scalar
                def _(act):
                    act.wait_ge(tanh_in, 1)
                    nc.scalar.activation(VD[0:96, 8:10, :], VD[0:96, 8:10, :], ACT.Tanh).then_inc(tanh_out, 1)

            za, zb = stage_sems("lowrank_done", "lowrank_used")
            with nc.Block() as block:
                @block.tensor
                def _(pe):
                    for n in range(32):
                        j, c = n // 8, n % 8
                        if n >= 4:
                            pe.wait_ge(zb, n - 3)
                        nc.tensor.matmul(psa[:, n % 4, 0:T], S[6][0:96, :, :].rearrange("p c t -> p (c t)")[:, j * 1024 + c * P:j * 1024 + (c + 1) * P],
                                         VD[0:96, 8 + j, :], start=True, stop=True).then_inc(za, 1)

                @block.scalar
                def _(act):
                    for n in range(32):
                        j, c = n // 8, n % 8
                        act.wait_ge(za, n + 1)
                        dst = (LW if j < 2 else AA)[:, (j % 2) * 8 + c, :]
                        nc.scalar.activation(dst, psa[:, n % 4, 0:T], ACT.Sigmoid,
                                             bias=vcol(("rwkv_w0_f_3", "rwkv_w0_b_3", "rwkv_a0_f_3", "rwkv_a0_b_3")[j], c)).then_inc(zb, 1)
            KK = VD[:, 8:16, :]
            sq_in, sq_out, s_done, s_used, r_out, steps = stage_sems("kk_ready", "kk_squared", "kk_sums", "kk_sums_used", "root_done", "dve_steps")
            with nc.Block() as block:
                @block.vector
                def _(dve):
                    link = linker(dve, steps)
                    nc.vector.tensor_scalar(LW[:, :, :], LW[:, :, :], -float(np.exp(-0.5)), None, ALU.mult)
                    for c in range(NC8):
                        x = nc.vector.tensor_scalar(KK[:, c, :], RK[:, 8 + c, :], vcol("rwkv_k_k_3", c), None, ALU.mult)
                    x.then_inc(sq_in, 1)
                    dve.wait_ge(r_out, NC8)
                    link(nc.vector.tensor_scalar(TS[:, 8:16, :], TS[:, 8:16, :], 1e-12, None, ALU.max))
                    link(nc.vector.reciprocal(TS[:, 8:16, :], TS[:, 8:16, :]))
                    nc.vector.tensor_tensor(KK, KK, TS[:, 8:16, :], ALU.mult)

                @block.scalar
                def _(act):
                    act.wait_ge(sq_in, 1)
                    nc.scalar.activation(TS[:, 0:8, :], KK, ACT.Square).then_inc(sq_out, 1)
                    for c in range(NC8):
                        act.wait_ge(s_done, c + 1)
                        nc.scalar.activation(TS[:, 8 + c, :], psa[:, c % 4, 0:T], ACT.Sqrt).then_inc(r_out, 1)

                @block.tensor
                def _(pe):
                    pe.wait_ge(sq_out, 1)
                    for c in range(NC8):
                        if c >= 4:
                            pe.wait_ge(r_out, c - 3)
                        nc.tensor.matmul(psa[:, c % 4, 0:T], blk[:, :], TS[:, c, :], start=True, stop=True).then_inc(s_done, 1)

            with ExitStack() as scan_mem:
                rwkv_scan(scan_mem, RK, VD, LW, AA)
            rwkv_out(own, blk, RK, VD, LW, AA)

        def rwkv_scan(own, RK, VD, LW, AA):
            def sb(name, shape):
                return own.enter_context(nc.sbuf_tensor(name, shape, F32))
            pool = {0: [[S[6], 0], [S[1], 0]], 1: [[S[7], 0], [S[8], 0]]}

            def carve(d, n):
                for slot in pool[d]:
                    if slot[1] + n <= DC * T:
                        slot[1] += n
                        return slot[0][:, :, :].rearrange("p c t -> p (c t)")[:, slot[1] - n:slot[1]]
                raise AssertionError("arena is full")
            masks64 = sb("chunk_masks", [P, 2, 2, P])
            m16_ts = sb("mask16_ts", [P, 2, P])
            m16_st = sb("mask16_st", [P, 2, P])
            reset = sb("chunk_reset", [P, T])
            load_consts(("chunk_masks", masks64[:, :, :, :]), ("mask16_ts", m16_ts[:, :, :]), ("mask16_st", m16_st[:, :, :]),
                        ("chunk_reset", reset[:, :]))

            def quad(ap):
                return ap.rearrange("p (i n) -> p i n", i=4)

            def per4(mask):
                return mask.rearrange("p (a n) -> p a n", a=1).broadcast_to([P, 4, mask.shape[-1]])

            class Dir:
                pass
            dirs = []
            for d in range(2):
                q = Dir()
                q.bank = [(psg, psa)[d][:, b, :] for b in range(4)]
                q.two = [(psg, psa)[d][:, 2 * b:2 * b + 2, :].rearrange("p b n -> p (b n)") for b in range(2)]
                q.M1 = carve(d, 1024).rearrange("p (i k t) -> p i k t", i=4, k=2)
                q.M2 = carve(d, 1024).rearrange("p (i k t) -> p i k t", i=4, k=2)
                q.SQ0 = carve(d, 1024).rearrange("p (k i t) -> p k i t", k=2, i=4)
                q.SQ1 = carve(d, 1024).rearrange("p (k i t) -> p k i t", k=2, i=4)
                q.RT = quad(carve(d, 512))
                q.B = [quad(carve(d, 512)) for _ in range(2)]
                q.TT = quad(carve(d, 512))
                q.AR = carve(d, 512).rearrange("p (t k n) -> p t k n", t=2, k=2)
                q.bk = carve(d, 512).rearrange("p (k n) -> p k n", k=2)
                q.bkp = tmp2[d][:, :, :]
                q.tok = sb(f"tok{d}", [P, 4, 2, P])[:, :, :, :]
                q.EX = carve(d, 1024).rearrange("p (k n) -> p k n", k=4) if d else stat
                q.GC = sb(f"gc{d}", [P, NCH])
                q.t1 = q.EX[:, 2, :]
                q.W1T = tmp[d][:, 1, :].rearrange("p (t n) -> p t n", t=2)
                q.Z = tmp[d][:, 0, :].rearrange("p (i n) -> p i n", i=4)
                q.W2 = q.bk[:, 0, :].rearrange("p (h t n) -> p h t n", h=2, t=2)
                q.U = q.W2
                q.S = carve(0, 256).rearrange("p (k n) -> p k n", k=NCH)
                q.ka, q.kf = tmp[d][:, 0, :], tmp[d][:, 1, :]
                q.order = range(NCH) if d == 0 else range(NCH - 1, -1, -1)
                dirs.append(q)
            prep_in, prep_exp, chain, y_done, y_copied, started, passed = stage_sems("exponents", "exponentials", "dve_chain", "y_done", "y_copied", "states_zero", "waits_passed")
            prepared = stage_sems("prepared0", "prepared1")
            pe_step = stage_sems("pe_step0", "pe_step1")
            act_step = stage_sems("act_step0", "act_step1")
            dve_step = stage_sems("dve_step0", "dve_step1")
            inst = [(hp, t) for hp in range(2) for t in range(TT)]

            STEPS = [("tok", 1, 1), ("gram", 0, 1), ("d2", 1, 0), ("d4", 1, 1), ("d8", 1, 1), ("b8", 0, 1), ("t16", 1, 0),
                     ("n1", 1, 0), ("n2", 1, 0), ("cz", 1, 1), ("tt", 0, 1), ("w", 1, 0)]
            for k in range(NCH):
                STEPS.append((("u", k), 0, 1))
                if k < NCH - 1:
                    STEPS.append((("s", k), 0, 1))
            NS = len(STEPS)
            NA = sum(x[1] for x in STEPS)
            ND = sum(x[2] for x in STEPS)

            def seen(n, col):
                return sum(x[col] for x in STEPS[:n])

            def rows(hp):
                return slice(CH * hp, CH * hp + CH)

            def pe_emit(q, name):
                b0, b1, b2, b3 = q.bank
                mm = nc.tensor.matmul
                tr = nc.tensor.transpose

                def four(bank, lhs, rhs):
                    for i in range(4):
                        x = mm(bank[:, i * P:(i + 1) * P], lhs[:, i, :], rhs[:, i, :], start=True, stop=True)
                    return x
                Dm, DT, E2, E2T = q.SQ0[:, 0], q.SQ0[:, 1], q.SQ1[:, 0], q.SQ1[:, 1]
                if name == "tok":
                    for t in range(TT):
                        tk = slice(t * P, (t + 1) * P)
                        tr(b0[:, tk], q.AR[:, t, 0, :], ident[:, :])
                        tr(b0[:, T + t * P:T + (t + 1) * P], q.bkp[:, 0, tk], ident[:, :])
                        tr(b1[:, tk], q.bkp[:, 1, tk], ident[:, :])
                        tr(b1[:, T + t * P:T + (t + 1) * P], vc_buf[:, tk], ident[:, :])
                    for i, (hp, t) in enumerate(inst):
                        x = mm(q.bank[2 + hp][:, t * P:(t + 1) * P], q.AR[rows(hp), t, 0, :], q.bk[rows(hp), 0, t * P:(t + 1) * P], start=True, stop=True)
                elif name == "gram":
                    for k in range(2):
                        for i, (hp, t) in enumerate(inst):
                            x = mm(q.two[k][:, i * T:(i + 1) * T], q.bk[rows(hp), k, t * P:(t + 1) * P],
                                   q.AR[rows(hp), t, :, :].rearrange("p k n -> p (k n)"), start=True, stop=True)
                elif name == "d2":
                    four(b0, DT, Dm)
                    x = four(b1, Dm, DT)
                elif name == "d4":
                    four(b0, E2T, E2)
                    four(b1, E2, E2T)
                    x = four(b2, E2, q.B[0])
                elif name == "d8":
                    four(b0, DT, Dm)
                    x = four(b2, Dm, q.B[1])
                elif name == "b8":
                    x = four(b2, E2, q.B[0])
                elif name == "t16":
                    for i in range(4):
                        x = tr(b0[:, i * P:(i + 1) * P], q.B[1][:, i, :], ident[:, :])
                elif name == "n1":
                    four(b0, q.RT, E2T)
                    x = four(b1, E2T, q.RT)
                elif name == "n2":
                    x = four(b0, DT, Dm)
                elif name == "cz":
                    four(b2, E2, q.B[1])
                    for i, (hp, t) in enumerate(inst):
                        x = mm(b3[:, i * CH:(i + 1) * CH], q.M2[:, i, 0, :], q.tok[:, 3, t, CH * hp:CH * hp + CH], start=True, stop=True)
                elif name == "tt":
                    x = four(b2, Dm, q.B[0])
                elif name == "w":
                    for i, (hp, t) in enumerate(inst):
                        mm(b0[rows(hp), t * P:(t + 1) * P], q.tok[:, 0, t, CH * hp:CH * hp + CH], q.TT[:, i, :], start=True, stop=True)
                        x = mm(b1[:, i * CH:(i + 1) * CH], q.TT[:, i, :], q.Z[:, i, :], start=True, stop=True)
                elif name[0] == "u":
                    c = q.order[name[1]]
                    half = rows(c % 2)
                    for hp in range(2):
                        x = mm(q.bank[hp][half, 0:CH], q.W1T[rows(hp), c // 2, CH * (c % 2):CH * (c % 2) + CH],
                               q.S[rows(hp), name[1], :], start=True, stop=True)
                elif name[0] == "s":
                    c = q.order[name[1]]
                    half = rows(c % 2)
                    for hp in range(2):
                        mm(b2[rows(hp), 0:CH], q.tok[half, 1, c // 2, CH * hp:CH * hp + CH], q.U[half, hp, c // 2, :], start=True, stop=False)
                        x = mm(b2[rows(hp), 0:CH], q.tok[half, 2, c // 2, CH * hp:CH * hp + CH],
                               q.tok[half, 3, c // 2, CH * hp:CH * hp + CH], start=False, stop=True)
                return x

            def act_emit(q, name):
                cp = lambda o, i: nc.scalar.activation(o, i, ACT.Copy)
                if name == "tok":
                    return cp(q.tok, q.two[0].rearrange("p (k t n) -> p k t n", k=4, t=2))
                if name in ("d2", "n1", "d4"):
                    src = q.two[0].rearrange("p (k i t) -> p k i t", k=2, i=4)
                    return cp(q.SQ1 if name == "d2" else q.SQ0, src)
                if name in ("d8", "n2"):
                    return cp(q.SQ1[:, 0], quad(q.bank[0]))
                if name == "t16":
                    return cp(q.SQ1[:, 1], quad(q.bank[0]))
                if name == "cz":
                    return cp(q.Z, quad(q.bank[3][:, 0:T]))
                if name == "w":
                    cp(q.W1T, q.bank[0][:, 0:T].rearrange("p (t n) -> p t n", t=2))
                    return cp(q.W2, q.bank[1][:, 0:T].rearrange("p (h t n) -> p h t n", h=2, t=2))

            def dve_emit(d, q, name, link):
                tt = nc.vector.tensor_tensor
                b2 = quad(q.bank[2])
                if name == "tok":
                    four = lambda ap: ap.rearrange("p (h t) n -> p h t n", h=2)
                    grams = q.two[1].rearrange("p (h x) -> p h x", h=2)[:, :, 0:T].rearrange("p h (t n) -> p h t n", t=TT)
                    return tt(four(q.SQ0[:, 0]), grams, four(per4(m16_ts[:, d, :])), ALU.mult)
                if name == "gram":
                    m = masks64[:, d, :, :].rearrange("p k t -> p (k t)")
                    for k, M in ((1, q.M2), (0, q.M1)):
                        x = tt(M.rearrange("p i k t -> p i (k t)"), q.two[k].rearrange("p (i n) -> p i n", i=4), per4(m), ALU.mult)
                    link(x)
                    link(tt(q.SQ0[:, 1], q.M1[:, :, 0, :], per4(m16_st[:, d, :]), ALU.mult))
                    tt(q.RT, q.M1[:, :, 0, :], q.SQ0[:, 1], ALU.subtract)
                    return tt(q.B[0], q.SQ0[:, 1], per4(ident[:, :]), ALU.add)
                if name == "d4":
                    return tt(q.B[1], b2, q.B[0], ALU.add)
                if name == "d8":
                    return tt(q.B[0], b2, q.B[1], ALU.add)
                if name == "b8":
                    return tt(q.B[1], b2, q.B[0], ALU.add)
                if name == "cz":
                    return tt(q.B[0], b2, q.B[1], ALU.add)
                if name == "tt":
                    return tt(q.TT, b2, q.B[0], ALU.add)
                c = q.order[name[1]]
                if name[0] == "u":
                    half = rows(c % 2)
                    return tt(q.U[half, :, c // 2, :], q.two[0].rearrange("p (h x) -> p h x", h=2)[half, :, 0:CH], q.W2[half, :, c // 2, :], ALU.add)
                return nc.vector.scalar_tensor_tensor(out=q.S[:, name[1] + 1, :], in0=q.S[:, name[1], :], scalar=q.GC[:, c:c + 1],
                                                      in1=q.bank[2][:, 0:CH], op0=ALU.mult, op1=ALU.add)

            vc_buf = carve(0, T)
            NCHAIN = 2 * (4 + 3 + 2)
            with nc.Block() as block:
                @block.tensor
                def _(pe):
                    pe.wait_ge(started, 1)
                    with pe.Fori(0, NC8, 1) as it:
                        for n, (name, _, _) in enumerate(STEPS):
                            for d, q in enumerate(dirs):
                                if n == 0:
                                    pe.wait_ge(prepared[d], it + 1)
                                else:
                                    pe.wait_ge(act_step[d], it * NA + seen(n, 1))
                                if seen(n, 2):
                                    pe.wait_ge(dve_step[d], it * ND + seen(n, 2))
                                if name[0] in ("u", "s"):
                                    pe.sem_inc(passed, 1)
                                pe_emit(q, name).then_inc(pe_step[d], 1)
                        for d in range(2):
                            pe.wait_ge(dve_step[d], it * ND + ND)
                        yb = dirs[0].bank[3]
                        for i, (hp, t) in enumerate(inst):
                            y = yb[rows(hp), t * P:(t + 1) * P]
                            for d, q in enumerate(dirs):
                                nc.tensor.matmul(y, q.tok[:, 3, t, CH * hp:CH * hp + CH], q.M2[:, i, 1, :], start=d == 0, stop=False)
                                nc.tensor.matmul(y, q.U[:, hp, t, :], q.M1[:, i, 1, :], start=False, stop=False)
                                for k in range(NCH):
                                    c = q.order[k]
                                    if c // 2 == t:
                                        mm = nc.tensor.matmul(yb[rows(hp), c * CH:(c + 1) * CH], q.S[rows(hp), k, :],
                                                              q.AR[rows(hp), t, 1, CH * (c % 2):CH * (c % 2) + CH],
                                                              start=False, stop=d == 1 and k == max(kk for kk in range(NCH) if q.order[kk] // 2 == t))
                        mm.then_inc(y_done, 1)

                @block.scalar
                def _(act):
                    with act.Fori(0, NC8, 1) as it:
                        for d, q in enumerate(dirs):
                            act.wait_ge(prep_in, 2 * it + (d + 1))
                            nc.scalar.activation(q.EX[:, 3, :], q.EX[:, 0, :], ACT.Exp, scale=-1.0).then_inc(prep_exp, 1)
                            act.wait_ge(prep_exp, it * 6 + (3 * d + 1))
                            nc.scalar.activation(q.EX[:, 0:3, :], q.EX[:, 0:3, :], ACT.Exp).then_inc(prep_exp, 1)
                            nc.scalar.activation(q.GC[:, :], q.GC[:, :], ACT.Exp).then_inc(prep_exp, 1)
                        for n, (name, a, _) in enumerate(STEPS):
                            if a:
                                for d, q in enumerate(dirs):
                                    act.wait_ge(pe_step[d], it * NS + (n + 1))
                                    act_emit(q, name).then_inc(act_step[d], 1)
                        act.wait_ge(y_done, it + 1)
                        nc.scalar.activation(LW[:, bass.ds(it, 1), :].rearrange("p a t -> p (a t)"), dirs[0].bank[3][:, 0:T], ACT.Copy).then_inc(y_copied, 1)

                @block.vector
                def _(dve):
                    for d, q in enumerate(dirs):
                        x = nc.vector.memset(q.S[:, 0, :], 0.0)
                    nc.vector.memset(small[:, :], 0.0).then_inc(started, 1)
                    dve.wait_ge(started, 1)
                    v = nc.vector
                    with dve.Fori(0, NC8, 1) as it:
                        count = [0]

                        def link(x):
                            count[0] += 1
                            x.then_inc(chain, 1)
                            dve.wait_ge(chain, it * NCHAIN + count[0])

                        def pair(buf, off):
                            return buf[:, bass.ds(it + off, 1), :].rearrange("p a t -> p (a t)")
                        v.tensor_copy(vc_buf[:, :], pair(VD, 0))
                        for d, q in enumerate(dirs):
                            lw = pair(LW, 8 * d)
                            by = lambda ap: ap.rearrange("p (c n) -> p c n", c=NCH)
                            link(v.tensor_tensor_scan(q.ka, reset[:, :], lw, 0.0, ALU.mult, ALU.add))
                            tot = by(q.ka)[:, :, CH - 1:CH]
                            incl, excl, tail = q.EX[:, 0, :], q.EX[:, 1, :], q.EX[:, 2, :]
                            link(v.tensor_tensor(by(excl if d else tail), tot.broadcast_to([P, NCH, CH]), by(q.ka), ALU.subtract))
                            link(v.tensor_tensor(tail if d else excl, q.ka, lw, ALU.subtract))
                            if d:
                                link(v.tensor_tensor(incl, excl, lw, ALU.add))
                            else:
                                link(v.tensor_copy(incl, q.ka))
                            v.tensor_copy(q.GC[:, :], q.ka.rearrange("p (c n) -> p c n", c=NCH)[:, :, CH - 1]).then_inc(prep_in, 1)
                        for d, q in enumerate(dirs):
                            aa = pair(AA, 8 * d)
                            link(v.tensor_tensor(q.ka, pair(VD, 8), aa, ALU.mult))
                            link(v.tensor_scalar(q.kf, aa, 1.0, vecs[:, bass.ds(it + VEC_AT["rwkv_k_a_3"], 1)], ALU.subtract, ALU.mult))
                            link(v.scalar_tensor_tensor(out=q.kf, in0=q.kf, scalar=1.0, in1=pair(RK, 8), op0=ALU.add, op1=ALU.mult))
                            dve.wait_ge(prep_exp, it * 6 + (3 * d + 3))
                            til = lambda ap: ap.rearrange("p (t n) -> p t n", t=TT)
                            v.scalar_tensor_tensor(out=q.AR[:, :, 0, :], in0=til(pair(VD, 8)), scalar=-1.0, in1=til(q.EX[:, 1, :]), op0=ALU.mult, op1=ALU.mult)
                            v.tensor_tensor(q.AR[:, :, 1, :], til(pair(RK, 0)), til(q.EX[:, 0, :]), ALU.mult)
                            v.tensor_tensor(q.bk[:, 0, :], q.ka, q.EX[:, 3, :], ALU.mult)
                            v.tensor_tensor(q.bk[:, 1, :], q.kf, q.EX[:, 3, :], ALU.mult)
                            v.tensor_tensor(q.bkp[:, 0, :], q.ka, q.EX[:, 2, :], ALU.mult)
                            v.tensor_tensor(q.bkp[:, 1, :], q.kf, q.EX[:, 2, :], ALU.mult).then_inc(prepared[d], 1)
                        for n, (name, _, a) in enumerate(STEPS):
                            if a:
                                for d, q in enumerate(dirs):
                                    dve.wait_ge(pe_step[d], it * NS + (n + 1))
                                    dve_emit(d, q, name, link).then_inc(dve_step[d], 1)
                        assert count[0] == NCHAIN
                        dve.wait_ge(y_copied, it + 1)

        def rwkv_out(own, blk, RK, VD, LW, AA):
            YR, G6, G7 = LW, S[6], S[7]
            a_in, a_out, p1, p2, steps = stage_sems("act_in", "act_out", "pe_done", "pe_used", "dve_steps")
            with nc.Block() as block:
                @block.vector
                def _(dve):
                    link = linker(dve, steps)
                    v = nc.vector
                    link(v.tensor_tensor(AA[:, 0:8, :], AA[:, 0:8, :], AA[:, 8:16, :], ALU.add))
                    for c in range(NC8):
                        x = v.tensor_scalar(AA[:, c, :], AA[:, c, :], 2.0, vcol("rwkv_k_a_3", c), ALU.subtract, ALU.mult)
                    link(x)
                    link(v.scalar_tensor_tensor(out=AA[:, 0:8, :], in0=AA[:, 0:8, :], scalar=2.0, in1=RK[:, 8:16, :], op0=ALU.add, op1=ALU.mult))
                    for c in range(NC8):
                        x = v.scalar_tensor_tensor(out=AA[:, c, :], in0=AA[:, c, :], scalar=vcol("rwkv_r_k_3", c), in1=RK[:, c, :], op0=ALU.mult, op1=ALU.mult)
                    x.then_inc(a_in, 1)
                    for c in range(NC8):
                        dve.wait_ge(p1, 2 * c + 2)
                        v.scalar_tensor_tensor(out=G6[:, c, :], in0=psa[:, 2 * (c % 2), 0:T], scalar=-1.0 / 64, in1=YR[:, c, :], op0=ALU.mult, op1=ALU.add)
                        v.tensor_tensor(G7[:, c, :], psa[:, 2 * (c % 2) + 1, 0:T], VD[:, c, :], ALU.mult).then_inc(p2, 1)
                    for c in range(NC8):
                        dve.wait_ge(p1, 16 + c + 1)
                        v.tensor_scalar(G6[:, 8 + c, :], psa[:, c % 4, 0:T], 1.0 / 64, 64e-5, ALU.mult, ALU.add).then_inc(p2, 1)
                    dve.wait_ge(a_out, 2)
                    link(v.reciprocal(G6[:, 8:16, :], G6[:, 8:16, :]))
                    link(v.tensor_tensor(G6[:, 0:8, :], G6[:, 0:8, :], G6[:, 8:16, :], ALU.mult))
                    for c in range(NC8):
                        x = v.tensor_scalar(G6[:, c, :], G6[:, c, :], vcol("rwkv_gn_g_3", c), vcol("rwkv_gn_b_3", c), ALU.mult, ALU.add)
                    link(x)
                    v.tensor_tensor(YR[:, 0:8, :], G6[:, 0:8, :], G7[:, 0:8, :], ALU.add)

                @block.tensor
                def _(pe):
                    pe.wait_ge(a_in, 1)
                    for c in range(NC8):
                        if c >= 2:
                            pe.wait_ge(p2, c - 1)
                        nc.tensor.matmul(psa[:, 2 * (c % 2), 0:T], blk[:, :], YR[:, c, :], start=True, stop=True).then_inc(p1, 1)
                        nc.tensor.matmul(psa[:, 2 * (c % 2) + 1, 0:T], blk[:, :], AA[:, c, :], start=True, stop=True).then_inc(p1, 1)
                    pe.wait_ge(a_out, 1)
                    for c in range(NC8):
                        if c >= 4:
                            pe.wait_ge(p2, 8 + c - 3)
                        nc.tensor.matmul(psa[:, c % 4, 0:T], blk[:, :], AA[:, 8 + c, :], start=True, stop=True).then_inc(p1, 1)

                @block.scalar
                def _(act):
                    act.wait_ge(p2, NC8)
                    nc.scalar.activation(AA[:, 8:16, :], G6[:, 0:8, :], ACT.Square).then_inc(a_out, 1)
                    act.wait_ge(p2, 2 * NC8)
                    nc.scalar.activation(G6[:, 8:16, :], G6[:, 8:16, :], ACT.Sqrt).then_inc(a_out, 1)
            norm(X, H, DC, "g_pre_3", S[6])
            products(G("z_rwkv", H, "silu_mul", dst=YR), G("br_rwkv", YR, "copy", after=True, dst=Tm),
                     G("gate_rwkv", H, "gate_set", dst=Y, src=Tm))

        def mla(own):
            QA, QN, RO, VA = S[4], S[5], S[6], S[7]
            rot = own.enter_context(nc.sbuf_tensor("rotary", [P, 2, T], F32))
            load_consts(("rotary", rot[:, :, :]))
            OA = S[3]
            products(G("mla_qkv_a", H, "copy", dst=QA), G("mla_k_rope", H, "copy", dst=QA, at=8))
            norm(QA[:, 0:4, :], QA[:, 0:4, :], 4, "mla_q_norm_3", S[7])
            norm(QA[:, 4:8, :], QA[:, 4:8, :], 4, "mla_kv_norm_3", S[7])
            VN = VA[:, 0:8, :].rearrange("p c t -> p (c t)").rearrange("p (t n) -> p t n", t=TT)
            scale = float((128 + 64) ** -0.5)
            products(G("mla_q_nope", QA[:, 0:4, :], "copy", dst=QN, scale=scale), G("mla_q_rope", QA[:, 0:4, :], "copy", dst=RO, scale=scale),
                     G("mla_k_nope", QA[:, 4:8, :], "copy", dst=QN, at=8), G("mla_v", QA[:, 4:8, :], "copy", dst=VN, natural=True))
            (steps,) = stage_sems("dve_steps")
            with nc.Block() as block:
                @block.vector
                def _(dve):
                    link = linker(dve, steps)

                    def table(k, n):
                        return rot[:, k:k + 1, :].broadcast_to([P, n, T])
                    for a, n, buf in ((0, 4, RO), (8, 1, QA)):
                        x, y = buf[:, a:a + n, :], buf[:, a + n:a + 2 * n, :]
                        nc.vector.tensor_tensor(x, x, table(0, n), ALU.mult)
                        link(nc.vector.tensor_tensor(y, y, table(1, n), ALU.mult))
                        link(nc.vector.tensor_tensor(x, x, y, ALU.add))

            def qk(h, ps):
                half = slice(64 * (h % 2), 64 * (h % 2) + 64)
                for t in range(TT):
                    tk = slice(t * P, (t + 1) * P)
                    nc.tensor.matmul(ps[:, t * T:(t + 1) * T], QN[:, h, tk], QN[:, 8 + h, :], start=True, stop=False)
                    mm = nc.tensor.matmul(ps[:, t * T:(t + 1) * T], RO[half, h // 2, tk], QA[half, 8, :], start=False, stop=True)
                return mm
            PB = S[8][:, 0:4, :].rearrange("p (b t) s -> p b t s", b=2)
            PT = S[8][:, 4:8, :].rearrange("p (b t) s -> p b t s", b=2)
            attention(8, qk, lambda h, s: VN[:, s, h * P:(h + 1) * P], lambda h: OA[:, h, :], PB, PT)
            products(G("z_mla", H, "silu_mul", dst=OA), G("br_mla", OA, "copy", after=True, dst=QN),
                     G("gate_mla", H, "gate_add", dst=Y, src=QN))

        IH, NH, NKV, TOPK, RB = 8, 16, 4, 64, 32

        def block_2(own):
            with ExitStack() as attn_mem:
                sparse_attention(attn_mem)
            with ExitStack() as sgu_mem:
                tri = sgu_mem.enter_context(nc.sbuf_tensor("causal_t", [P, P], F32))
                load_consts(("causal_t", tri[:, :]))
                sgu(tri)
            norm(X, H, DC, "norm2_g_2", S[4])
            for c in range(4):
                F = S[2 + c % 2]
                products(G(f"ff1_{c}", H, "relu2", dst=F), G(f"ff2_{c}", F, "resid", after=True, dst=X))
            norm(X, X, DC, "final_g_2", S[4])

        def sparse_attention(own):
            def sb(name, shape):
                return own.enter_context(nc.sbuf_tensor(name, shape, F32))
            Q, KI, V4 = S[2], S[3], S[4]
            norm(X, H, DC, "norm1_g_2", S[4])
            wi = sb("index_weights", [P, TT, IH])
            VN = V4[:, 0:4, :].rearrange("p c t -> p (c t)").rearrange("p (t n) -> p t n", t=TT)
            products(G("sa_q", H, "copy", dst=Q, scale=float(128 ** -0.5)), G("sa_k", H, "copy", dst=KI),
                     G("sa_v", H, "copy", dst=VN, natural=True), G("sa_qi", H, "copy", dst=KI, at=4),
                     G("sa_ki", H, "copy_small", dst=KI[:, 8, :]), G("sa_wi", H, "copy_narrow", dst=wi[:, :, :], natural=True))

            RBs = [S[5], S[6]]
            RBv = [r[:, 0:12, :].rearrange("p c t -> p (c t)").rearrange("p (h z) -> p h z", h=8) for r in RBs]
            onehot = sb("bucket_onehot", [RB, 512])
            rel = sb("rel_bias_sb", [RB, NH])
            exch = sb("exchange", [P, P])
            bvec = sb("bias_by_distance", [NH, 512])
            causal = sb("causal", [P, 2, TT, T])
            load_consts(("bucket_onehot", onehot[:, :]), ("rel_bias", rel[:, :]), ("exchange", exch[:, :]), ("causal", causal[:, :, :, :]))
            scratch = nc.dram_tensor("bias_scratch", (NH, 512), F32, kind="Internal").ap()
            pe_b, act_b, dma_b = stage_sems("bias_done", "bias_copied", "bias_moved")
            idx_done, relu_done, steps, scaled = stage_sems("index_done", "relu_done", "dve_steps", "scaled")
            RL = S[7][:, 0:2, :]
            SC = S[7][:, 2:4, :]
            WK = S[7][:, 4:6, :]
            MK = S[7][:, 6:8, :]
            m8 = small[:, 16:32]
            with nc.Block() as block:
                @block.sync
                def _(sp):
                    sp.wait_ge(act_b, 1)
                    sp.dma_start(scratch, bvec[:, :]).then_inc(dma_b, 16)
                    sp.wait_ge(dma_b, 16)
                    for k in range(2):
                        src = bass.AP(tensor=scratch.tensor, offset=scratch.offset + 8 * k * 512, ap=[[1, P], [512, 8], [1, 384]])
                        sp.dma_start(RBv[k], src).then_inc(dma_b, 16)
                    sp.wait_ge(dma_b, 48)

                @block.tensor
                def _(pe):
                    nc.tensor.matmul(psg[0:NH, 0, :], rel[:, :], onehot[:, :], start=True, stop=True).then_inc(pe_b, 1)
                    for t in range(TT):
                        for h in range(IH):
                            n = IH * t + h
                            if n >= 4:
                                pe.wait_ge(relu_done, n - 3)
                            half = slice(64 * (h % 2), 64 * (h % 2) + 64)
                            nc.tensor.matmul(psa[:, n % 4, 0:T], KI[half, 4 + h // 2, t * P:(t + 1) * P], KI[half, 8, :],
                                             start=True, stop=True).then_inc(idx_done, 1)

                @block.scalar
                def _(act):
                    act.wait_ge(pe_b, 1)
                    nc.scalar.activation(bvec[:, :], psg[0:NH, 0, :], ACT.Copy).then_inc(act_b, 1)
                    for n in range(TT * IH):
                        act.wait_ge(idx_done, n + 1)
                        if n >= 2:
                            act.wait_ge(scaled, n)
                        nc.scalar.activation(RL[:, n % 2, :], psa[:, n % 4, 0:T], ACT.Relu).then_inc(relu_done, 1)

                @block.vector
                def _(dve):
                    link = linker(dve, steps)
                    v = nc.vector
                    v.tensor_scalar(wi[:, :, :], wi[:, :, :], float(IH ** -0.5 * 64 ** -0.5), None, ALU.mult).then_inc(scaled, 1)
                    dve.wait_ge(scaled, 1)
                    for t in range(TT):
                        for h in range(IH):
                            n = IH * t + h
                            dve.wait_ge(relu_done, n + 1)
                            dve.wait_ge(scaled, n + 1)
                            w = wi[:, t, h:h + 1]
                            if h == 0:
                                v.tensor_scalar(SC[:, t, :], RL[:, n % 2, :], w, None, ALU.mult).then_inc(scaled, 1)
                            else:
                                v.scalar_tensor_tensor(out=SC[:, t, :], in0=RL[:, n % 2, :], scalar=w, in1=SC[:, t, :],
                                                       op0=ALU.mult, op1=ALU.add).then_inc(scaled, 1)
                    dve.wait_ge(scaled, TT * IH + 1)
                    link(v.tensor_tensor(SC, SC, causal[:, 1, :, :], ALU.add))
                    for r in range(TOPK // 8):
                        src = SC if r == 0 else WK
                        for t in range(TT):
                            x = v.max(m8[:, 8 * t:8 * t + 8], src[:, t, :])
                        link(x)
                        for t in range(TT):
                            x = v.match_replace(out=WK[:, t, :], in_to_replace=m8[:, 8 * t:8 * t + 8], in_values=src[:, t, :], imm_value=-3e38)
                        link(x)
                    link(v.tensor_tensor(WK, WK, SC, ALU.is_equal))
                    link(v.tensor_scalar(WK, WK, -1.0, 1.0, ALU.mult, ALU.add))
                    link(v.tensor_tensor(WK, WK, causal[:, 0, :, :], ALU.mult))
                    link(v.tensor_scalar(MK, WK, 1.0, -NEG, ALU.subtract, ALU.mult))

            def qk(h, ps):
                for t in range(TT):
                    nc.tensor.matmul(ps[:, t * T:(t + 1) * T], Q[:, h, t * P:(t + 1) * P], KI[:, h // (NH // NKV), :], start=True, stop=False)
                    off = P * (1 - t)
                    mm = nc.tensor.matmul(ps[:, t * T:(t + 1) * T], exch[:, :], RBv[h // 8][:, h % 8, off:off + T], start=False, stop=True)
                return mm
            PB = S[8][:, 0:4, :].rearrange("p (b t) s -> p b t s", b=2)
            PT = S[8][:, 4:8, :].rearrange("p (b t) s -> p b t s", b=2)
            attention(NH, qk, lambda h, s: VN[:, s, (h // (NH // NKV)) * P:(h // (NH // NKV) + 1) * P], lambda h: Q[:, h, :], PB, PT, mask=MK)

        def sgu(ones_tri):
            U, VS, M5, S6, GB, WB = S[3], S[4], S[5], S[6], S[7], S[8]
            VN = VS[:, :, :].rearrange("p c t -> p (c t)").rearrange("p (t n) -> p t n", t=TT)
            products(G("sgu_u", H, "copy", dst=U), G("sgu_v", H, "copy", dst=VN, natural=True))
            M5n = flat(M5, 0, DC).rearrange("p (t n) -> p t n", t=TT)
            gb = flat(GB, 0, DC).rearrange("p (k n) -> p k n", k=2)
            ws = flat(WB, 0, 8).rearrange("p (g t) -> p g t", g=16)
            bs = flat(WB, 8, 16).rearrange("p (g t) -> p g t", g=16)
            tri_t = ones_tri
            cub, sig, steps, ln_in, ln_out, mix, mixed, sq = stage_sems("cubes", "sigmoids", "dve_steps", "ln_in", "ln_sums", "mix_done", "mixed", "root")
            (loaded,) = stage_sems("loaded")
            with nc.Block() as block:
                @block.sync
                def _(sp):
                    for k, name in enumerate(("sgu_g", "sgu_b")):
                        sp.dma_start(gb[:, k, :], ins[name].broadcast_to([P, D])).then_inc(loaded, 16)
                    sp.dma_start(ws, ins["sgu_w"]).then_inc(loaded, 16)
                    sp.dma_start(bs, ins["sgu_bias"].broadcast_to([P, D]).rearrange("p (g t) -> p g t", g=16)).then_inc(loaded, 16)
                    sp.wait_ge(loaded, 64)

                @block.vector
                def _(dve):
                    link = linker(dve, steps)
                    v = nc.vector
                    for k, (x, tm) in enumerate(((VS, M5), (U, S6))):
                        x, tm = x[:, :, :], tm[:, :, :]
                        link(v.tensor_tensor(tm, x, x, ALU.mult))
                        link(v.tensor_scalar(tm, tm, 0.044715, 1.0, ALU.mult, ALU.add))
                        v.tensor_tensor(tm, tm, x, ALU.mult).then_inc(cub, 1)
                    for k, (x, tm) in enumerate(((VS, M5), (U, S6))):
                        dve.wait_ge(sig, k + 1)
                        z = v.tensor_tensor(x[:, :, :], x[:, :, :], tm[:, :, :], ALU.mult)
                        if k == 0:
                            z.then_inc(ln_in, 1)
                    dve.wait_ge(ln_out, 4)
                    mean, sums = small[:, 32:34], small[:, 34:36]
                    link(v.tensor_scalar(small[:, 32:36], small[:, 32:36], 1.0 / D, None, ALU.mult))
                    link(v.tensor_tensor(small[:, 36:38], mean, mean, ALU.mult))
                    link(v.tensor_tensor(sums, sums, small[:, 36:38], ALU.subtract))
                    v.tensor_scalar(sums, sums, EPS, None, ALU.add).then_inc(ln_in, 1)
                    dve.wait_ge(sq, 1)
                    link(v.reciprocal(sums, sums))
                    dve.wait_ge(loaded, 64)
                    for t in range(TT):
                        x = v.tensor_scalar(VN[:, t, :], VN[:, t, :], small[:, 32 + t:33 + t], small[:, 34 + t:35 + t], ALU.subtract, ALU.mult)
                    link(x)
                    gk = lambda k: gb[:, k:k + 1, :].broadcast_to([P, TT, D])
                    link(v.tensor_tensor(VN, VN, gk(0), ALU.mult))
                    v.tensor_tensor(VN, VN, gk(1), ALU.add)
                    v.tensor_tensor(ws, ws, tri_t[:, :].rearrange("p (a t) -> p a t", a=1).broadcast_to([P, 16, P]), ALU.mult).then_inc(ln_in, 1)
                    for g in range(16):
                        dve.wait_ge(mix, g + 1)
                        b = bs[:, g:g + 1, :].broadcast_to([P, TT, P])
                        v.tensor_tensor(M5[:, g, :].rearrange("p (c t) -> p c t", c=TT), psa[:, g % 4, 0:T].rearrange("p (c t) -> p c t", c=TT), b, ALU.add).then_inc(mixed, 1)
                    dve.wait_ge(mixed, 16)
                    v.tensor_tensor(M5[:, :, :], M5[:, :, :], U[:, :, :], ALU.mult)

                @block.scalar
                def _(act):
                    for k, tm in enumerate((M5, S6)):
                        act.wait_ge(cub, k + 1)
                        nc.scalar.activation(tm[:, :, :], tm[:, :, :], ACT.Sigmoid, scale=float(2 * np.sqrt(2 / np.pi))).then_inc(sig, 1)
                    act.wait_ge(ln_in, 1)
                    for t in range(TT):
                        junk = M5n[:, t, :]
                        nc.scalar.activation(junk, VN[:, t, :], ACT.Copy, accum_out=small[:, 32 + t:33 + t]).then_inc(ln_out, 1)
                        act.wait_ge(ln_out, 2 * t + 1)
                        nc.scalar.activation(junk, VN[:, t, :], ACT.Square, accum_out=small[:, 34 + t:35 + t]).then_inc(ln_out, 1)
                    act.wait_ge(ln_in, 2)
                    nc.scalar.activation(small[:, 34:36], small[:, 34:36], ACT.Sqrt).then_inc(sq, 1)

                @block.tensor
                def _(pe):
                    pe.wait_ge(ln_in, 3)
                    for g in range(16):
                        if g >= 4:
                            pe.wait_ge(mixed, g - 3)
                        for c in range(TT):
                            mm = nc.tensor.matmul(psa[:, g % 4, c * P:(c + 1) * P], VN[:, c, g * P:(g + 1) * P], ws[:, g, :], start=True, stop=True)
                        mm.then_inc(mix, 1)
            products(G("gate_a", H, "sig_mul", dst=S[2]), G("gate_b", H, "gate_add", dst=S[2], src=M5),
                     G("w_out_2", S[2], "resid", after=True, dst=X))

        for n, part in ((1, block_1), (2, block_2), (3, block_3)):
            if n in blocks:
                with ExitStack() as own:
                    part(own)

        with nc.Block() as block:
            @block.sync
            def _(sp):
                sp.dma_start(out, X[:, :, :]).then_inc(out_done, 16)
                sp.wait_ge(out_done, 16)


def to_units(w, cols=256):
    w = np.asarray(w)
    k, n = w.shape
    return np.ascontiguousarray(w.reshape(k // P, P, n // cols, cols).transpose(2, 1, 0, 3).reshape(n // cols, P, k // P * cols))


def channel_major(x):
    return np.ascontiguousarray(np.asarray(x).T.reshape(-1, P, x.shape[0]).transpose(1, 0, 2))


def per_channel(v):
    return np.asarray(v).reshape(-1, P).T


def layout(i):
    a = {}
    w = np.asarray(i["w_in"])[0]
    sizes = [("conv_a", 2048), ("conv_b", 2048), ("conv_z", 2048), ("gla_q", 1024), ("gla_k", 1024), ("gla_v", 2048),
             ("gla_z", 2048), ("alpha", 16), ("mem_q", 512), ("mem_z", 512), ("gate0", 2048), ("gate1", 2048), ("gate2", 2048)]
    at = 0
    for name, n in sizes:
        a[name] = to_units(w[:, at:at + n], min(n, 256))
        at += n
    a["conv_out"] = to_units(i["w_conv_out"][0])
    a["gla_out"] = to_units(i["w_gla_out"][0])
    a["mem_k"] = to_units(i["w_mem_kv"][0][:, :512])
    a["mem_v"] = to_units(i["w_mem_kv"][0][:, 512:])
    a["mem_out"] = to_units(i["w_mem_out"][0])
    a["w_out"] = to_units(i["w_out"][0])
    a["x_t"] = channel_major(np.asarray(i["x"])[0])
    a["mem_t"] = channel_major(np.asarray(i["mem"])[0])
    a["w_alpha2"] = np.ascontiguousarray(np.asarray(i["w_alpha2"])[0])
    cols = []
    for name, c in VECS:
        v = np.asarray(i[name])
        if name == "dw_w":
            cols.append(v[0].reshape(31, DC, P).transpose(2, 1, 0).reshape(P, -1))
        elif name == "rwkv_mu_3":
            cols.append(per_channel(v[:3072]))
            cols.append(np.concatenate([v[3072:].reshape(4, 96), np.zeros((4, 32), v.dtype)], 1).T)
        else:
            cols.append(per_channel(v))
    a["vecs"] = np.ascontiguousarray(np.concatenate(cols, 1))
    w = np.asarray(i["w_in_2"])[0]
    for name, lo, hi in (("sa_q", 0, 2048), ("sa_k", 2048, 2560), ("sa_v", 2560, 3072), ("sa_qi", 3072, 3584),
                         ("sgu_u", 3656, 5704), ("sgu_v", 5704, 7752), ("gate_a", 7752, 9800), ("gate_b", 9800, 11848)):
        a[name] = to_units(w[:, lo:hi])
    a["sa_ki"] = to_units(np.concatenate([w[:, 3584:3648]] * 2, 1), 128)
    a["sa_wi"] = to_units(w[:, 3648:3656], 8)
    a["w_out_2"] = to_units(i["w_out_2"][0])
    w1, w2 = np.asarray(i["w_ff1_2"])[0], np.asarray(i["w_ff2_2"])[0]
    for c in range(4):
        a[f"ff1_{c}"] = to_units(w1[:, c * D:(c + 1) * D])
        a[f"ff2_{c}"] = to_units(w2[c * D:(c + 1) * D])
    a["rel_bias"] = np.asarray(i["rel_bias_2"])
    a["sgu_g"], a["sgu_b"] = np.asarray(i["sgu_ln_g_2"]), np.asarray(i["sgu_ln_b_2"])
    a["sgu_w"] = np.ascontiguousarray(np.asarray(i["sgu_w_2"])[0].transpose(2, 0, 1))
    a["sgu_bias"] = np.asarray(i["sgu_b_2"]).reshape(1, D)
    w = np.asarray(i["w_in_3"])
    for name, lo, hi in (("rwkv_rk", 1088, 3136), ("rwkv_v", 3136, 4160), ("z_mla", 4544, 5568), ("z_rwkv", 5568, 6592),
                         ("gate_mla", 6592, 8640), ("gate_rwkv", 8640, 10688), ("mla_qkv_a", 0, 1024)):
        a[name] = to_units(w[:, lo:hi])
    a["rwkv_da"] = to_units(w[:, 4160:4544], 192)
    kr, krs = w[:, 1024:1088], np.concatenate([w[:, 1056:1088], w[:, 1024:1056]], 1)
    a["mla_k_rope"] = to_units(np.concatenate([kr, kr, krs, krs], 1))
    wq = np.asarray(i["mla_wq_b_3"]).reshape(512, 8, 192)
    a["mla_q_nope"] = to_units(wq[:, :, :128].reshape(512, 1024))
    a["mla_q_rope"] = to_units(np.concatenate([wq[:, :, 128:].reshape(512, 512),
                                               np.concatenate([wq[:, :, 160:], wq[:, :, 128:160]], 2).reshape(512, 512)], 1))
    wkv = np.asarray(i["mla_wkv_b_3"]).reshape(512, 8, 256)
    a["mla_k_nope"] = to_units(wkv[:, :, :128].reshape(512, 1024))
    a["mla_v"] = to_units(wkv[:, :, 128:].reshape(512, 1024))
    a["br_mla"] = to_units(i["w_br_mla_3"])
    a["br_rwkv"] = to_units(i["w_br_rwkv_3"])
    a["w_out_3"] = to_units(i["w_out_3"])
    a["rwkv_w2"] = np.ascontiguousarray(np.stack([np.asarray(i[n]) for n in ("rwkv_w2_f_3", "rwkv_w2_b_3", "rwkv_a2_f_3", "rwkv_a2_b_3")], 1)
                                        .reshape(96, DC, T))
    a["ones"] = np.ones((P, P), np.float32)
    a["ident"] = np.eye(P, dtype=np.float32)
    s, t = np.arange(P)[:, None], np.arange(P)[None, :]
    m = np.zeros((P, 8, P), np.float32)
    for l in range(GLA_LEVELS):
        m[:, l] = ((s >> (l + 1)) == (t >> (l + 1))) & (((s >> l) & 1) == 0) & (((t >> l) & 1) == 1)
    m[:, 7] = s == t
    a["level_masks"] = m
    a["exchange"] = (s + t == P - 1).astype(np.float32)
    a["causal_t"] = (s <= t).astype(np.float32)
    key, query = np.arange(T)[None, None, :], (np.arange(TT)[None, :, None] * P + np.arange(P)[:, None, None])
    a["causal"] = np.stack([key <= query, np.where(key <= query, 0, NEG)], 1).astype(np.float32)
    dist = np.maximum(T - 1 - np.arange(512), 0)
    large = 16 + (np.log(np.maximum(dist, 1).astype(np.float32) / np.float32(16)) / np.float32(np.log(8.0)) * np.float32(16)).astype(np.int32)
    bucket = np.where(dist < 16, dist, np.minimum(large, 31))
    a["bucket_onehot"] = (np.arange(32)[:, None] == bucket[None, :]).astype(np.float32)
    a["head_ones"] = ((s // 64) == (t // 64)).astype(np.float32)
    cm = np.zeros((P, 2, 2, P), np.float32)
    m_ts, m_st = np.zeros((P, 2, P), np.float32), np.zeros((P, 2, P), np.float32)
    same64, same16 = (s // 64) == (t // 64), (s // 16) == (t // 16)
    for d, strict in enumerate((s < t, s > t)):
        cm[:, d, 0], cm[:, d, 1] = same64 & strict, same64 & (strict | (s == t))
        m_st[:, d] = same16 & strict
        m_ts[:, d] = (same16 & strict).T
    a["chunk_masks"], a["mask16_ts"], a["mask16_st"] = cm, m_ts, m_st
    a["chunk_reset"] = np.tile((np.arange(T) % 64 != 0).astype(np.float32), (P, 1))
    freq = np.float32(10000.0) ** (-np.arange(0, 64, 2, dtype=np.float32) / np.float32(64))
    ang = (np.arange(T, dtype=np.float32)[:, None] * freq[None, :]).astype(np.float32).T
    rot = np.zeros((P, 2, T), np.float32)
    for r in range(4):
        rot[32 * r:32 * r + 32, 0] = np.cos(ang)
        rot[32 * r:32 * r + 32, 1] = np.sin(ang) * (1 if r % 2 else -1)
    a["rotary"] = rot
    return a


def kernel(**inputs):
    import concourse.bacc as bacc
    from concourse.bass_utils import run_bass_kernel_spmd
    nc = bacc.Bacc("TRN2", target_bir_lowering=False, num_devices=1)
    arrays = layout(inputs)
    ins = {k: nc.dram_tensor("in_" + k, v.shape, F32, kind="ExternalInput").ap() for k, v in arrays.items()}
    out = nc.dram_tensor("out", (P, DC, T), F32, kind="ExternalOutput").ap()
    build(nc, ins, out, BLOCKS)
    r = run_bass_kernel_spmd(nc, [{"in_" + k: v for k, v in arrays.items()}], core_ids=[0])
    y = r.results[0]["out"]
    return np.ascontiguousarray(y.transpose(1, 0, 2).reshape(D, T).T)[None]
```

```python
from contextlib import ExitStack

import numpy as np
import concourse.bass as bass
from concourse import mybir

F32 = mybir.dt.float32
F32R = mybir.dt.float32r
ACT = mybir.ActivationFunctionType
ALU = mybir.AluOpType
AX = mybir.AxisListType
P = 128
T = 256
TT = T // P
D = 2048
DC = D // P
EPS = 1e-6
GLA_HEADS, GLA_LEVELS = 4, 7
MEM_HEADS = 4
NEG = -1e30
BLOCKS = (1, 2, 3)


def stream_plan(blocks):
    plan = []

    def add(name, units, kc=DC, cols=256):
        plan.append((name, units, kc, cols))
    if 1 in blocks:
        add("conv_a", 8); add("conv_b", 8); add("gla_q", 4); add("gla_k", 4); add("gla_v", 8)
        add("gate0", 8); add("conv_z", 8); add("alpha", 1, DC, 16); add("conv_out", 8)
        add("gate1", 8); add("gla_z", 8); add("gla_out", 8)
        add("gate2a", 4); add("mem_k", 2); add("mem_v", 2); add("mem_q", 2); add("gate2b", 4); add("mem_z", 2)
        add("mem_out", 8, 4); add("w_out", 8)
    if 2 in blocks:
        add("sa_q", 8); add("sa_k", 2); add("sa_v", 2); add("sa_qi", 2); add("sa_ki", 1, DC, 128); add("sa_wi", 1, DC, 8)
        add("sgu_u", 8); add("sgu_v", 8); add("gate_a", 8); add("gate_b", 8); add("w_out_2", 8)
        for c in range(4):
            add(f"ff1_{c}", 8); add(f"ff2_{c}", 8)
    if 3 in blocks:
        add("rwkv_rk", 8); add("rwkv_v", 4); add("rwkv_da", 2, DC, 192)
        add("gate_rwkv", 8); add("z_rwkv", 4); add("br_rwkv", 8, 8)
        add("mla_qkv_a", 4); add("mla_k_rope", 1)
        add("mla_q_nope", 4, 4); add("mla_q_rope", 4, 4); add("mla_k_nope", 4, 4); add("mla_v", 4, 4)
        add("gate_mla", 8); add("z_mla", 4); add("br_mla", 8, 8); add("w_out_3", 8)
    return plan


VECS = [("ln_in_g", 16), ("mem_ln_g", 16), ("b_gate", 48), ("dw_b", 16), ("conv_ln_g", 16), ("conv_ln_b", 16),
        ("b_conv_out", 16), ("b_alpha", 8), ("gla_norm_g", 16), ("final_g", 16), ("dw_w", 16 * 31),
        ("g_pre_3", 16), ("mla_q_norm_3", 4), ("mla_kv_norm_3", 4), ("rwkv_mu_3", 28), ("rwkv_w0_f_3", 8), ("rwkv_w0_b_3", 8),
        ("rwkv_a0_f_3", 8), ("rwkv_a0_b_3", 8), ("rwkv_k_k_3", 8), ("rwkv_k_a_3", 8), ("rwkv_r_k_3", 8), ("rwkv_gn_g_3", 8),
        ("rwkv_gn_b_3", 8), ("g_post_3", 16), ("norm1_g_2", 16), ("norm2_g_2", 16), ("final_g_2", 16)]
VEC_AT = {}
_n = 0
for _name, _c in VECS:
    VEC_AT[_name] = _n
    _n += _c
NVEC = _n


class Stage:
    unit = 0
    gated = 0
    mids = 0
    made = 0
    splits = 0


def build(nc, ins, out, blocks):
    plan = stream_plan(blocks)
    units = [(name, u, kc, cols) for name, n, kc, cols in plan for u in range(n)]

    with ExitStack() as ctx:
        def sb(name, shape):
            return ctx.enter_context(nc.sbuf_tensor(name, shape, F32))

        def sem(name):
            return ctx.enter_context(nc.semaphore(name))

        def twin(name, shape):
            at = -(-nc.sbuf_base // 32) * 32
            return sb(name, shape), nc.alloc_sbuf_tensor_at(name + "_r", shape, F32R, offset=at)
        HALF = DC * 256 // 2
        ring, ring_lo = zip(*[twin(f"ring{i}", [P, HALF]) for i in range(4)])
        w_hi = [ctx.enter_context(nc.sbuf_tensor(f"w_hi{i}", [P, HALF // 2], F32R)) for i in range(2)]
        arena, arena_r = zip(*[twin(f"arena{i}", [P, DC, T]) for i in range(9)])
        Y, Tm = arena[2:4]
        tmp = [sb(f"act_tmp{i}", [P, 2, T]) for i in range(2)]
        tmp2 = [sb(f"dve_tmp{i}", [P, 2, T]) for i in range(2)]
        vecs = sb("vecs", [P, NVEC])
        ones = sb("ones", [P, P])
        ident = sb("ident", [P, P])
        stat = sb("stat", [P, 4, T])
        small = sb("small", [P, 64])
        psg = ctx.enter_context(nc.psum_tensor("ps_gemm", [P, 4, 512], F32))
        psa = ctx.enter_context(nc.psum_tensor("ps_aux", [P, 4, 512], F32))

        def vec(name, c):
            return vecs[:, bass.ds(c + VEC_AT[name], 1)]

        def pair(hi, lo, a=0, b=DC):
            return arena_r[hi][:, a:b, :], arena_r[lo][:, a:b, :]

        w_ready = [sem(f"w_ready{i}") for i in range(4)]
        hi_ready = sem("w_hi_ready")
        lo_ready = sem("w_lo_ready")
        hi_used = sem("w_hi_used")
        quarters_done = sem("quarters_done")
        split_in = sem("split_in")
        split_hi = sem("split_hi")
        split_done = sem("split_done")
        bank_free = sem("bank_free")
        act_ready = sem("act_ready")
        dve_mid = sem("dve_mid")
        const_in = sem("const_in")
        out_done = sem("out_done")
        st = Stage()

        def load_half(sp, g, h, src_index=None):
            name, u, kc, cols = units[g]
            ix = u if src_index is None else src_index
            n = kc * cols // 2
            slot = 2 * (g % 2) + h
            sp.dma_start(ring[slot][:, 0:n],
                         ins[name][bass.ds(ix, 1)].rearrange("a p n -> (a p) n")[:, h * n:(h + 1) * n]).then_inc(w_ready[slot], 16)

        def prefetch(sp, g0, n):
            g, end = g0 + 2, min(g0 + n + 2, len(units))
            while g < end:
                run = 1
                while g + run < end and units[g + run][0] == units[g][0]:
                    run += 1
                pairs = run // 2
                if pairs >= 2:
                    u0 = units[g][1]
                    with sp.Fori(0, pairs, 1) as i:
                        for j in range(2):
                            for h in range(2):
                                sp.wait_ge(quarters_done, 8 * i + (4 * (g + j) + 2 * h - 6))
                                load_half(sp, g + j, h, 2 * i + (u0 + j))
                    g += 2 * pairs
                    run -= 2 * pairs
                for _ in range(run):
                    for h in range(2):
                        sp.wait_ge(quarters_done, 4 * g + 2 * h - 6)
                        load_half(sp, g, h)
                    g += 1

        def quarter_of(g, q):
            n = units[g][2] * units[g][3] // 4
            return 2 * (g % 2) + q // 2, slice(q % 2 * n, (q % 2 + 1) * n), n, 4 * g + q

        def round_weights(act, i2, g, q):
            slot, part, size, n = quarter_of(g, q)
            act.wait_ge(w_ready[slot], 8 * i2 + 16 * (g // 2 + 1))
            if n >= 2:
                act.wait_ge(hi_used, 4 * i2 + (n - 1))
                act.wait_ge(lo_ready, 4 * i2 + (n - 1))
            nc.scalar.activation(w_hi[q % 2][:, 0:size], ring[slot][:, part], ACT.Copy).then_inc(hi_ready, 1)

        def rest_of_weights(dve, i2, g, q):
            slot, part, size, n = quarter_of(g, q)
            dve.wait_ge(hi_ready, 4 * i2 + (n + 1))
            nc.vector.tensor_tensor(ring_lo[slot][:, part], ring[slot][:, part], w_hi[q % 2][:, 0:size].bitcast(F32), ALU.subtract).then_inc(lo_ready, 1)

        def unit_work(eng, quarter, g0, i2, j, epilogue, split):
            more = g0 + j + 1 + (i2 if type(i2) is int else 0) < len(units)
            at, g = (0, g0 + j + i2) if type(i2) is int else (i2, g0 + j)
            quarter(eng, at, g, 2)
            quarter(eng, at, g, 3)
            if more:
                quarter(eng, at, g + 1, 0)
            epilogue(i2, j)
            if more:
                quarter(eng, at, g + 1, 1)
            split(i2, j)

        def all_units(eng, quarter, g0, n, epilogue, split):
            other = g0 + n >= len(units) or units[g0 + n][2:] != units[g0][2:]
            looped = n - 2 if other else n
            if looped >= 4:
                assert n % 2 == 0
                with eng.Fori(0, looped // 2, 1) as i:
                    for j in range(2):
                        unit_work(eng, quarter, g0, 2 * i, j, epilogue, split)
            else:
                looped = 0
            for u in range(looped, n):
                unit_work(eng, quarter, g0, u - u % 2, u % 2, epilogue, split)

        def unit_loop(eng, n, body):
            if n >= 4:
                assert n % 2 == 0
                with eng.Fori(0, n // 2, 1) as i:
                    for j in range(2):
                        body(2 * i, j)
            else:
                for u in range(n):
                    body(u - u % 2, u % 2)

        def pe_body(pe, g0, rhs, natural):
            name, _, kc, cols = units[g0]
            cw = 96 if cols == 192 else min(cols, P)
            r_hi, r_lo = rhs

            def body(i2, j):
                slot = (g0 + j) % 2
                pe.wait_ge(bank_free, i2 + (g0 + j + 1))
                for q in range(4):
                    ring_slot, part, _, n = quarter_of(g0 + j, q)
                    whi, wlo = w_hi[q % 2], ring_lo[ring_slot][:, part]

                    def sweep(passes, first, last):
                        for c in range(TT if natural else cols // cw):
                            bank = psg[:, 2 * slot + c, :]
                            for k in range(kc // 4):
                                kk = q * (kc // 4) + k
                                for m, (w, r) in enumerate(passes):
                                    start = first and q == 0 and k == 0 and m == 0
                                    stop = last and q == 3 and k == kc // 4 - 1
                                    if natural:
                                        mm = nc.tensor.matmul(bank[:, 0:cols], r[:, kk, c * P:(c + 1) * P],
                                                              w[:, k * cols:(k + 1) * cols], start=start, stop=stop)
                                    else:
                                        mm = nc.tensor.matmul(bank[0:cw, 0:T], w[:, k * cols + c * cw:k * cols + (c + 1) * cw],
                                                              r[:, kk, :], start=start, stop=stop)
                        return mm
                    pe.wait_ge(hi_ready, 4 * i2 + (n + 1))
                    sweep([(whi, r_hi), (whi, r_lo)], True, False).then_inc(hi_used, 1)
                    pe.wait_ge(lo_ready, 4 * i2 + (n + 1))
                    sweep([(wlo, r_hi)], False, True).then_inc(quarters_done, 1)
            return body

        ACT_ONLY = ("copy", "bias", "copy_small", "copy_narrow", "sig")
        DVE_ONLY = ("resid", "bias_mul", "mul_add")

        class Prod:

            def __init__(s, name, rhs, kind, dst=None, src=None, bias=None, scale=1.0, natural=False, at=0, after=False, rows=P, step=2, split=None, needs_loads=False):
                s.g0 = st.unit
                assert units[s.g0][:2] == (name, 0), (units[s.g0], name)
                s.n = [x[1] for x in plan if x[0] == name][0]
                st.unit += s.n
                s.rhs, s.kind, s.dst, s.src, s.bias, s.scale, s.natural, s.at = rhs, kind, dst, src, bias, scale, natural, at
                s.after, s.rows, s.step = after, rows, step
                s.split, s.needs_loads = split, needs_loads
                s.split_before = st.splits
                s.act0, s.mid0 = st.gated, st.mids
                s.split0 = st.splits
                if split:
                    st.splits += s.n
                if kind not in ACT_ONLY + DVE_ONLY:
                    st.gated += s.n
                if kind in ("silu_mul", "gate_add", "mul_add"):
                    st.mids += s.n

            def sp(s, sp):
                prefetch(sp, s.g0, s.n)

            def pe(s, pe):
                if s.after:
                    pe.wait_ge(split_done, s.split_before)
                unit_loop(pe, s.n, pe_body(pe, s.g0, s.rhs, s.natural))

            def chunks(s, buf, i2, j):
                return buf[0:s.rows, bass.ds(s.step * i2 + (s.step * j + s.at), 2), :]

            def views(s, i2, j):
                slot = (s.g0 + j) % 2
                ps = psg[0:s.rows, 2 * slot:2 * slot + 2, 0:T]
                if s.kind == "copy_narrow":
                    return slot, psg[:, 2 * slot:2 * slot + 2, 0:s.dst.shape[2]], s.dst
                if s.natural:
                    d = s.dst[:, :, bass.ds(i2 * 256 + (j * 256 + s.at), 256)]
                elif s.kind != "copy_small":
                    d = s.chunks(s.dst, i2, j)
                else:
                    d = None
                return slot, ps, d

            def act(s, act):
                all_units(act, round_weights, s.g0, s.n, lambda i2, j: s.act_epilogue(act, i2, j), lambda i2, j: s.act_split(act, i2, j))

            def act_part(s, act, u, part):
                s.part(round_weights, s.act_epilogue, act, u, part)

            def dve_part(s, dve, u, part):
                s.part(rest_of_weights, s.dve_epilogue, dve, u, part)

            def part(s, quarter, epilogue, eng, u, part):
                g = s.g0 + u
                if part == 3:
                    epilogue(eng, u - u % 2, u % 2)
                if part < 2:
                    quarter(eng, 0, g, part + 2)
                elif g + 1 < len(units):
                    quarter(eng, 0, g + 1, part - 2)

            def act_unit(s, act, u):
                for part in range(4):
                    s.act_part(act, u, part)

            def dve_unit(s, dve, u):
                for part in range(4):
                    s.dve_part(dve, u, part)

            def pe_unit(s, pe, u):
                pe_body(pe, s.g0, s.rhs, s.natural)(u - u % 2, u % 2)

            def act_split(s, act, i2, j):
                if s.split:
                    act.wait_ge(bank_free, i2 + (s.g0 + j + 3))
                    nc.scalar.activation(s.chunks(s.split[0], i2, j), s.chunks(s.dst, i2, j), ACT.Copy).then_inc(split_hi, 1)

            def dve_split(s, dve, i2, j):
                if s.split:
                    dve.wait_ge(split_hi, i2 + (s.split0 + j + 1))
                    hi, lo = (s.chunks(x, i2, j) for x in s.split)
                    nc.vector.tensor_tensor(lo, s.chunks(s.dst, i2, j), hi.bitcast(F32), ALU.subtract).then_inc(split_done, 1)

            def act_epilogue(s, act, i2, j):
                if s.kind in DVE_ONLY:
                    return
                slot, ps, d = s.views(i2, j)
                act.wait_ge(quarters_done, 4 * i2 + (4 * (s.g0 + j) + 4))
                if s.kind in ("copy", "copy_narrow"):
                    nc.scalar.activation(d, ps, ACT.Copy, scale=s.scale).then_inc(bank_free, 1)
                    return
                if s.kind == "copy_small":
                    nc.scalar.activation(s.dst, psg[0:s.dst.shape[0], 2 * slot, 0:T], ACT.Copy).then_inc(bank_free, 1)
                    return
                if s.kind == "sig":
                    for c in range(2):
                        o = s.dst[:, bass.ds(2 * i2 + (2 * j + c + s.at), 1), :].rearrange("p a t -> p (a t)")
                        a = nc.scalar.activation(o, ps[:, c, :], ACT.Sigmoid, bias=vec(s.bias[0], 2 * i2 + (2 * j + c + s.bias[1])) if s.bias else 0.0)
                    a.then_inc(bank_free, 1)
                    return
                if s.kind == "bias":
                    for c in range(2):
                        a = nc.scalar.activation(s.dst[:, bass.ds(2 * i2 + (2 * j + c), 1), :].rearrange("p a t -> p (a t)"),
                                                 ps[:, c, :], ACT.Identity, bias=vec(s.bias, 2 * i2 + (2 * j + c)))
                    a.then_inc(bank_free, 1)
                    return
                act.wait_ge(bank_free, i2 + (s.g0 + j + 1))
                if s.kind in ("gate_set", "gate_add") and s.bias:
                    for c in range(2):
                        a = nc.scalar.activation(tmp[slot][:, c, :], ps[:, c, :], ACT.Sigmoid,
                                                 bias=vec(s.bias[0], 2 * i2 + (2 * j + c + s.bias[1])))
                else:
                    f = {"sig_mul": ACT.Sigmoid, "silu": ACT.Sigmoid, "silu_mul": ACT.Sigmoid, "gate_set": ACT.Sigmoid, "gate_add": ACT.Sigmoid, "relu2": ACT.Relu}[s.kind]
                    a = nc.scalar.activation(tmp[slot][:, :, :], ps, f)
                a.then_inc(act_ready, 1)

            def dve(s, dve):
                if s.kind not in ACT_ONLY:
                    dve.wait_ge(bank_free, s.g0 + 2)
                all_units(dve, rest_of_weights, s.g0, s.n, lambda i2, j: s.dve_epilogue(dve, i2, j), lambda i2, j: s.dve_split(dve, i2, j))

            def dve_epilogue(s, dve, i2, j):
                if s.kind in ACT_ONLY:
                    return
                slot, ps, d = s.views(i2, j)
                if s.kind == "resid":
                    dve.wait_ge(quarters_done, 4 * i2 + (4 * (s.g0 + j) + 4))
                    nc.vector.tensor_tensor(d, ps, d, ALU.add).then_inc(bank_free, 1)
                    return
                if s.kind == "bias_mul":
                    dve.wait_ge(quarters_done, 4 * i2 + (4 * (s.g0 + j) + 4))
                    for c in range(2):
                        o = s.dst[:, bass.ds(2 * i2 + (2 * j + c), 1), :].rearrange("p a t -> p (a t)")
                        a = nc.vector.scalar_tensor_tensor(out=o, in0=ps[:, c, :], scalar=vec(s.bias, 2 * i2 + (2 * j + c)) if s.bias else 0.0,
                                                           in1=o, op0=ALU.add, op1=ALU.mult)
                    a.then_inc(bank_free, 1)
                    return
                if s.kind == "mul_add":
                    dve.wait_ge(quarters_done, 4 * i2 + (4 * (s.g0 + j) + 4))
                    nc.vector.tensor_tensor(tmp2[slot][:, :, :], ps, s.src[:, bass.ds(2 * i2 + 2 * j, 2), :], ALU.mult).then_inc(dve_mid, 1)
                    dve.wait_ge(dve_mid, i2 + (s.mid0 + j + 1))
                    nc.vector.tensor_tensor(d, tmp2[slot][:, :, :], d, ALU.add).then_inc(bank_free, 1)
                    return
                dve.wait_ge(act_ready, i2 + (s.act0 + j + 1))
                t = tmp[slot][:, :, :]
                if s.kind == "sig_mul":
                    last = nc.vector.tensor_tensor(d, t, d, ALU.mult)
                elif s.kind == "silu":
                    last = nc.vector.tensor_tensor(d, ps, t, ALU.mult)
                elif s.kind == "relu2":
                    last = nc.vector.tensor_tensor(d, t, t, ALU.mult)
                elif s.kind == "gate_set":
                    last = nc.vector.tensor_tensor(d, t, s.src[:, bass.ds(2 * i2 + 2 * j, 2), :], ALU.mult)
                else:
                    if s.kind == "silu_mul":
                        a = nc.vector.tensor_tensor(tmp2[slot][:, :, :], ps, t, ALU.mult)
                    else:
                        a = nc.vector.tensor_tensor(tmp2[slot][:, :, :], t, s.src[:, bass.ds(2 * i2 + 2 * j, 2), :], ALU.mult)
                    a.then_inc(dve_mid, 1)
                    dve.wait_ge(dve_mid, i2 + (s.mid0 + j + 1))
                    last = nc.vector.tensor_tensor(d, tmp2[slot][:, :, :], d,
                                                   ALU.mult if s.kind == "silu_mul" else ALU.add)
                last.then_inc(bank_free, 1)

        def products(*args, dve_body=None, loads=(), pre=None, dve_pre=None):
            prods = [Prod(*a[0], **a[1]) for a in args]
            (loaded,) = stage_sems("loaded") if loads else (None,)
            with nc.Block() as block:
                @block.sync
                def _(sp):
                    for src, dst in loads:
                        sp.dma_start(dst, ins[src] if type(src) is str else src).then_inc(loaded, 16)
                    for p in prods:
                        p.sp(sp)
                    if loads:
                        sp.wait_ge(loaded, 16 * len(loads))

                @block.tensor
                def _(pe):
                    for p in prods:
                        p.pe(pe)

                @block.scalar
                def _(act):
                    if pre:
                        pre.act(act)
                    for p in prods:
                        p.act(act)

                @block.vector
                def _(dve):
                    if pre:
                        pre.dve(dve)
                    if dve_pre:
                        dve_pre(dve)
                    if dve_body:
                        dve_body(dve, prods[0].g0)
                    else:
                        for p in prods:
                            if p.needs_loads:
                                dve.wait_ge(loaded, 16 * len(loads))
                            p.dve(dve)

        class Split:

            def __init__(s, groups, make, raw, hi, lo):
                s.groups, s.make, s.raw, s.hi, s.lo = groups, make, raw, hi, lo
                s.made0, s.split0 = st.made, st.splits
                st.made += groups
                st.splits += groups

            def act(s, act):
                for q in range(s.groups):
                    act.wait_ge(split_in, s.made0 + q + 1)
                    nc.scalar.activation(s.hi(q), s.raw(q), ACT.Copy).then_inc(split_hi, 1)

            def dve(s, dve):
                s.make(dve, 0).then_inc(split_in, 1)
                for q in range(s.groups):
                    if q + 1 < s.groups:
                        s.make(dve, q + 1).then_inc(split_in, 1)
                    dve.wait_ge(split_hi, s.split0 + q + 1)
                    nc.vector.tensor_tensor(s.lo(q), s.raw(q), s.hi(q).bitcast(F32), ALU.subtract).then_inc(split_done, 1)

        def G(*a, **k):
            return (a, k)

        nstage = [0]

        def stage_sems(*names):
            nstage[0] += 1
            return [sem(f"s{nstage[0]}_{n}") for n in names]

        def linker(eng, chain):
            count = [0]

            def link(x):
                count[0] += 1
                x.then_inc(chain, 1)
                eng.wait_ge(chain, count[0])
            return link

        def vcol(name, c):
            return vecs[:, VEC_AT[name] + c:VEC_AT[name] + c + 1]

        def flat(buf, a, b):
            return buf[:, a:b, :].rearrange("p c t -> p (c t)")

        sq_ready, sums_done, root_in, root_done, chain, normed = [
            sem("norm_" + n) for n in ("sq_ready", "sums_done", "root_in", "root_done", "dve_chain", "normed")]
        norm_base = [0] * 6

        def norm(src, dst, n, gain, scratch, mean=False, bias=None, silu=False, gain_at=0, groups=1, side=None, split=None, spill=None):
            b_sq, b_sums, b_in, b_root, b_chain, b_norm = norm_base
            tot = n * groups
            count = [0]
            first = st.unit == 0
            side = Prod(*side[0], **side[1]) if side else None
            per = tot // side.n if side else 0
            (spilled,) = stage_sems("spilled") if spill is not None else (None,)

            def gained(c):
                return nc.vector.scalar_tensor_tensor(out=dst[:, c, :], in0=src[:, c, :], scalar=vecs[:, VEC_AT[gain] + gain_at + c:VEC_AT[gain] + gain_at + c + 1],
                                                      in1=stat[:, 3, :], op0=ALU.mult, op1=ALU.mult)

            def make(dve, q):
                for c in range(q * n // 4, (q + 1) * n // 4):
                    x = gained(c)
                return x
            if split:
                part = lambda buf: (lambda q: buf[:, q * n // 4:(q + 1) * n // 4, :])
                parts = Split(4, make, part(dst), part(split[0]), part(split[1]))
            with nc.Block() as block:
                @block.sync
                def _(sp):
                    if spill is not None:
                        sp.dma_start(spill, src[:, :, :]).then_inc(spilled, 16)
                    if side:
                        side.sp(sp)
                    if spill is not None:
                        sp.wait_ge(spilled, 16)

                @block.scalar
                def _(act):
                    h = max(tot // 4, 1)
                    for a in range(0, tot, h):
                        nc.scalar.activation(scratch[:, a:a + h, :], src[:, a:a + h, :], ACT.Square).then_inc(sq_ready, 1)
                    if first:
                        for q in range(2):
                            round_weights(act, 0, 0, q)
                    for g in range(groups):
                        act.wait_ge(root_in, b_in + g + 1)
                        nc.scalar.activation(stat[:, 2, :], stat[:, 1, :], ACT.Sqrt).then_inc(root_done, 1)
                    if split:
                        parts.act(act)
                    if silu:
                        for c in range(tot):
                            act.wait_ge(normed, b_norm + c + 1)
                            nc.scalar.activation(scratch[:, c, :], dst[:, c, :], ACT.Sigmoid).then_inc(root_done, 1)
                            if side and (c + 1) % per == 0:
                                side.act_unit(act, c // per)
                    elif side:
                        for u in range(side.n):
                            side.act_unit(act, u)

                @block.tensor
                def _(pe):
                    h = max(tot // 4, 1)
                    for g in range(groups):
                        if g:
                            pe.wait_ge(root_in, b_in + g)
                        if mean:
                            for c in range(n):
                                nc.tensor.matmul(psa[:, 1, 0:T], ones[:, :], src[:, g * n + c, :], start=c == 0, stop=c == n - 1)
                        for c in range(n):
                            pe.wait_ge(sq_ready, b_sq + (g * n + c) // h + 1)
                            mm = nc.tensor.matmul(psa[:, 0, 0:T], ones[:, :], scratch[:, g * n + c, :], start=c == 0, stop=c == n - 1)
                        mm.then_inc(sums_done, 1)
                    for u in range(side.n if side else 0):
                        side.pe_unit(pe, u)

                @block.vector
                def _(dve):
                    def link(x):
                        count[0] += 1
                        x.then_inc(chain, 1)
                        dve.wait_ge(chain, b_chain + count[0])
                    if first:
                        for q in range(2):
                            rest_of_weights(dve, 0, 0, q)
                    for g in range(groups):
                        dve.wait_ge(sums_done, b_sums + g + 1)
                        inv = 1.0 / (n * P)
                        if mean:
                            link(nc.vector.tensor_scalar(stat[:, 0, :], psa[:, 1, 0:T], inv, None, ALU.mult))
                            link(nc.vector.tensor_tensor(stat[:, 3, :], stat[:, 0, :], stat[:, 0, :], ALU.mult))
                            link(nc.vector.tensor_scalar(stat[:, 1, :], psa[:, 0, 0:T], inv, EPS, ALU.mult, ALU.add))
                            nc.vector.tensor_tensor(stat[:, 1, :], stat[:, 1, :], stat[:, 3, :], ALU.subtract).then_inc(root_in, 1)
                        else:
                            nc.vector.tensor_scalar(stat[:, 1, :], psa[:, 0, 0:T], inv, EPS, ALU.mult, ALU.add).then_inc(root_in, 1)
                        dve.wait_ge(root_done, b_root + g + 1)
                        link(nc.vector.reciprocal(stat[:, 3, :], stat[:, 2, :]))
                        if mean:
                            link(nc.vector.tensor_tensor(stat[:, 0, :], stat[:, 0, :], stat[:, 3, :], ALU.mult))
                        if split:
                            if spill is not None:
                                dve.wait_ge(spilled, 16)
                            parts.dve(dve)
                            continue
                        for c in range(g * n, g * n + n):
                            if not mean:
                                x = gained(c)
                                if c == g * n + n - 1:
                                    link(x)
                                continue
                            link(nc.vector.tensor_tensor(dst[:, c, :], src[:, c, :], stat[:, 3, :], ALU.mult))
                            link(nc.vector.tensor_tensor(dst[:, c, :], dst[:, c, :], stat[:, 0, :], ALU.subtract))
                            x = nc.vector.tensor_scalar(dst[:, c, :], dst[:, c, :], vecs[:, VEC_AT[gain] + c:VEC_AT[gain] + c + 1],
                                                        vecs[:, VEC_AT[bias] + c:VEC_AT[bias] + c + 1], ALU.mult, ALU.add)
                            x.then_inc(normed, 1)
                            if silu and (c + 1) % per == 0:
                                side.dve_unit(dve, c // per)
                                for cc in range(c + 1 - per, c + 1):
                                    dve.wait_ge(root_done, b_root + groups + cc + 1)
                                    nc.vector.tensor_tensor(dst[:, cc, :], dst[:, cc, :], scratch[:, cc, :], ALU.mult)
                    if side and not silu:
                        for u in range(side.n):
                            side.dve_unit(dve, u)
            for i, more in enumerate((-(-tot // max(tot // 4, 1)), groups, groups, groups + (tot if silu else 0), count[0], tot if mean else 0)):
                norm_base[i] += more

        def attention(nh, qk, v, o, pbuf, ptbuf, mask=None, side=None):
            (qk_done, mx_done, exp_done, p_done, chain, tr_done, trc_done, o_done, oc_done) = stage_sems(
                "qk_done", "mx_done", "exp_done", "p_done", "dve_chain", "tr_done", "trc_done", "o_done", "oc_done")
            side = Prod(*side[0], **side[1]) if side else None
            m = side.n if side else 0
            share = [range(h * m // nh, (h + 1) * m // nh) for h in range(nh)]
            assert m <= nh
            with nc.Block() as block:
                @block.sync
                def _(sp):
                    if side:
                        side.sp(sp)

                @block.tensor
                def _(pe):
                    def scores(h):
                        if h >= 2:
                            pe.wait_ge(exp_done, h - 1)
                        mm = qk(h, psa[:, h % 2, :])
                        mm.then_inc(qk_done, 1)
                    scores(0)
                    for h in range(nh):
                        if h + 1 < nh:
                            scores(h + 1)
                        for u in share[h]:
                            side.pe_unit(pe, u)
                        pe.wait_ge(p_done, h + 1)
                        if h:
                            pe.wait_ge(trc_done, h)
                        for s in range(TT):
                            for t in range(TT):
                                mm = nc.tensor.transpose(psa[:, 2, s * T + t * P:s * T + (t + 1) * P],
                                                         pbuf[:, h % 2, t, s * P:(s + 1) * P], ident[:, :])
                        mm.then_inc(tr_done, 1)
                        pe.wait_ge(trc_done, h + 1)
                        if h:
                            pe.wait_ge(oc_done, h)
                        for s in range(TT):
                            mm = nc.tensor.matmul(psa[:, 3, 0:T], v(h, s), ptbuf[:, h % 2, s, :], start=s == 0, stop=s == TT - 1)
                        mm.then_inc(o_done, 1)

                @block.vector
                def _(dve):
                    count = [0]

                    def link(x):
                        count[0] += 1
                        x.then_inc(chain, 1)
                        dve.wait_ge(chain, count[0])

                    def maximum(h):
                        dve.wait_ge(qk_done, h + 1)
                        ps = psa[:, h % 2, :].rearrange("p (t s) -> p t s", t=TT)
                        src = ps
                        if mask is not None:
                            if h >= 2:
                                dve.wait_ge(tr_done, h - 1)
                            link(nc.vector.tensor_tensor(pbuf[:, h % 2, :, :], ps, mask, ALU.add))
                            src = pbuf[:, h % 2, :, :]
                        nc.vector.tensor_reduce(small[:, 4 * (h % 2):4 * (h % 2) + 2], src, AX.X, ALU.max, negate=True).then_inc(mx_done, 1)
                    maximum(0)
                    for h in range(nh):
                        if h + 1 < nh:
                            maximum(h + 1)
                        b = 8 + 4 * (h % 2)
                        dve.wait_ge(exp_done, h + 1)
                        link(nc.vector.reciprocal(small[:, b + 2:b + 4], small[:, b:b + 2]))
                        for t in range(TT):
                            x = nc.vector.tensor_scalar(pbuf[:, h % 2, t, :], pbuf[:, h % 2, t, :], small[:, b + 2 + t:b + 3 + t], None, ALU.mult)
                        x.then_inc(p_done, 1)
                        for u in share[h]:
                            side.dve_unit(dve, u)
                        dve.wait_ge(o_done, h + 1)
                        nc.vector.tensor_copy(o(h), psa[:, 3, 0:T]).then_inc(oc_done, 1)

                @block.scalar
                def _(act):
                    def exps(h):
                        act.wait_ge(mx_done, h + 1)
                        if h >= 2:
                            act.wait_ge(tr_done, h - 1)
                        for t in range(TT):
                            src = psa[:, h % 2, t * T:(t + 1) * T] if mask is None else pbuf[:, h % 2, t, :]
                            x = nc.scalar.activation(pbuf[:, h % 2, t, :], src, ACT.Exp, bias=small[:, 4 * (h % 2) + t:4 * (h % 2) + t + 1],
                                                     accum_out=small[:, 8 + 4 * (h % 2) + t:9 + 4 * (h % 2) + t])
                        x.then_inc(exp_done, 1)
                    exps(0)
                    for h in range(nh):
                        if h + 1 < nh:
                            exps(h + 1)
                        for u in share[h]:
                            side.act_unit(act, u)
                        act.wait_ge(tr_done, h + 1)
                        if h >= 2:
                            act.wait_ge(o_done, h - 1)
                        nc.scalar.activation(ptbuf[:, h % 2, :, :], psa[:, 2, :].rearrange("p (s t) -> p s t", s=TT), ACT.Copy).then_inc(trc_done, 1)

        consts = [("x_t", arena[0][:, :, :]), ("vecs", vecs[:, :]), ("ones", ones[:, :]), ("ident", ident[:, :])]
        with nc.Block() as block:
            @block.sync
            def _(sp):
                for name, dst in consts:
                    sp.dma_start(dst, ins[name]).then_inc(const_in, 16)
                for g in range(2):
                    for h in range(2):
                        load_half(sp, g, h)
                sp.wait_ge(const_in, 16 * len(consts))

            @block.scalar
            def _(act):
                act.sem_inc(bank_free, 2)

        S = arena
        H = pair(1, 0)
        spill_x = nc.dram_tensor("residual", (P, DC, T), F32, kind="Internal").ap()

        def block_1(own):
            def sb(name, shape):
                return own.enter_context(nc.sbuf_tensor(name, shape, F32))
            masks = sb("level_masks", [P, 8, P])
            alpha_t, wal2 = S[3][0:16, 0, :], S[3][0:16, 4:8, :].rearrange("p c t -> p (c t)")
            sc = S[4][:, 8:12, :].rearrange("p c (k t) -> p (c k) t", k=2)
            stt = S[4][:, 12:14, :]
            norm(S[0], S[0], DC, "ln_in_g", S[4], split=(arena_r[1], arena_r[0]))
            U, CV = S[4], S[5]

            (conv_step,) = stage_sems("conv_step")
            K31 = 31

            CONV_UNITS = 24

            def conv_body(dve, g0):
                w0 = VEC_AT["dw_w"]
                rounds = DC // 4
                count = 4 * CONV_UNITS // rounds
                taps = [(lag, cc) for lag in range(K31) for cc in range(4)]
                with dve.Fori(0, rounds, 1) as c4:
                    def ch(buf, cc, a, b):
                        return buf[:, bass.ds(4 * c4 + cc, 1), a:b].rearrange("p a t -> p (a t)")
                    for n in range(count):
                        rest_of_weights(dve, (count // 4) * c4, g0 + (n + 2) // 4, (n + 2) % 4)
                        for lag, cc in taps[n * len(taps) // count:(n + 1) * len(taps) // count]:
                            w = vecs[:, bass.ds(c4 * (4 * K31) + (w0 + cc * K31 + K31 - 1 - lag), 1)]
                            if lag == 0:
                                x = nc.vector.tensor_scalar(ch(CV, cc, 0, T), ch(U, cc, 0, T), w, vec("dw_b", 4 * c4 + cc), ALU.mult, ALU.add)
                            else:
                                dve.wait_ge(conv_step, c4 * (4 * K31) + (4 * (lag - 1) + cc + 1))
                                x = nc.vector.scalar_tensor_tensor(out=ch(CV, cc, lag, T), in0=ch(U, cc, 0, T - lag), scalar=w,
                                                                   in1=ch(CV, cc, lag, T), op0=ALU.mult, op1=ALU.add)
                            x.then_inc(conv_step, 1)
            QK, V = S[6], S[7]
            Vn = V[:, :, :].rearrange("p c t -> p (c t)").rearrange("p (t n) -> p t n", t=TT)
            products(G("conv_a", H, "copy", dst=U), G("conv_b", H, "sig_mul", dst=U))
            products(G("gla_q", H, "copy", dst=QK, scale=1.0 / 16, step=4), G("gla_k", H, "copy", dst=QK, at=2, step=4),
                     G("gla_v", H, "copy", dst=Vn, natural=True), G("gate0", H, "sig", dst=Y, bias=("b_gate", 0)), dve_body=conv_body,
                     loads=(("level_masks", masks[:, :, :]), ("w_alpha2", wal2)))
            norm(CV, CV, DC, "conv_ln_g", S[8], mean=True, bias="conv_ln_b", silu=True,
                 side=G("conv_z", H, "silu", dst=U))
            quarter = lambda buf: (lambda q: buf[:, 4 * q:4 * q + 4, :])
            gated = Split(4, lambda dve, q: nc.vector.tensor_tensor(quarter(CV)(q), quarter(CV)(q), quarter(U)(q), ALU.mult),
                          quarter(CV), quarter(arena_r[8]), quarter(arena_r[5]))
            products(G("alpha", H, "copy_small", dst=alpha_t), pre=gated)
            products(G("conv_out", pair(8, 5), "bias_mul", dst=Y, bias="b_conv_out"))

            B, LA = S[4], S[5]
            za, zb, zc, zd = stage_sems("z_done", "z_moved", "steps", "act_steps")
            with nc.Block() as block:
                @block.tensor
                def _(pe):
                    for c in range(8):
                        mm = nc.tensor.matmul(psa[:, c // 2, (c % 2) * T:(c % 2 + 1) * T], wal2[0:16, c * P:(c + 1) * P],
                                              alpha_t, start=True, stop=True)
                    mm.then_inc(za, 1)

                @block.vector
                def _(dve):
                    count = [0]

                    def link(x):
                        count[0] += 1
                        x.then_inc(zc, 1)
                        dve.wait_ge(zc, count[0])
                    dve.wait_ge(za, 1)
                    for c in range(8):
                        x = nc.vector.tensor_scalar(B[:, c, :], psa[:, c // 2, (c % 2) * T:(c % 2 + 1) * T], vecs[:, VEC_AT["b_alpha"] + c:VEC_AT["b_alpha"] + c + 1], None, ALU.add)
                    link(x)
                    nc.vector.scalar_tensor_tensor(out=LA[:, 0:8, :], in0=B[:, 0:8, :], scalar=-1.0, in1=B[:, 0:8, :], op0=ALU.mult, op1=ALU.min).then_inc(zb, 1)
                    link(nc.vector.tensor_scalar(B[:, 0:8, :], B[:, 0:8, :], 0.0, None, ALU.min))
                    dve.wait_ge(zd, 2)
                    link(nc.vector.tensor_tensor(LA[:, 0:8, :], B[:, 0:8, :], LA[:, 8:16, :], ALU.subtract))
                    link(nc.vector.tensor_scalar(LA[:, 0:8, :], LA[:, 0:8, :], 1.0 / 16, None, ALU.mult))
                    for c in range(8):
                        nc.vector.tensor_tensor_scan(B[:, c, :], LA[:, c, :], LA[:, c, :], 0.0, ALU.add, ALU.bypass)

                @block.scalar
                def _(act):
                    act.wait_ge(zb, 1)
                    nc.scalar.activation(LA[:, 0:8, :], LA[:, 0:8, :], ACT.Exp).then_inc(zd, 1)
                    act.wait_ge(zd, 1)
                    nc.scalar.activation(LA[:, 8:16, :], LA[:, 0:8, :], ACT.Ln, bias=1.0).then_inc(zd, 1)

            E, Q2 = S[8], S[5]
            O = QK
            side = Prod("gate1", H, "sig", dst=Tm, bias=("b_gate", 16))
            e1, e2, ds_, es, qd, od, ev, oc = stage_sems("diff_ready", "exp_ready", "dve_steps", "top_done", "ops_ready", "levels_done", "scores_ready", "o_done")
            with nc.Block() as block:
                @block.sync
                def _(sp):
                    side.sp(sp)

                @block.vector
                def _(dve):
                    count = [0]

                    def link(x):
                        count[0] += 1
                        x.then_inc(ds_, 1)
                        dve.wait_ge(ds_, count[0])
                    Ev = E[:, :, :].rearrange("p (l c) t -> p l (c t)", l=8)
                    Q2v = Q2[:, :, :].rearrange("p (l c) t -> p l (c t)", l=8)

                    def differences(h, levels):
                        bh = B[:, 2 * h:2 * h + 2, :].rearrange("p c t -> p (c t)")
                        for m in levels:
                            size = 2 << m
                            bv = bh.rearrange("p (n s) -> p n s", s=size)
                            r = bv[:, :, size // 2 - 1:size // 2].broadcast_to([P, 2 * T // size, size])
                            x = nc.vector.tensor_tensor(E[:, 2 * m:2 * m + 2, :].rearrange("p c t -> p (c t)").rearrange("p (n s) -> p n s", s=size),
                                                        bv, r, ALU.subtract)
                        return x

                    def decayed(out, qk, l):
                        x = qk.rearrange("p c t -> p (c t)").rearrange("p (a n) -> p a n", a=1).broadcast_to([P, 2, 2 * T])
                        return nc.vector.tensor_tensor(out[:, l:l + 2, :], Ev[:, l:l + 2, :], x, ALU.mult)
                    differences(0, range(8)).then_inc(e1, 1)
                    for h in range(GLA_HEADS):
                        q_h, k_h = QK[:, 4 * h:4 * h + 2, :], QK[:, 4 * h + 2:4 * h + 4, :]
                        for half in range(2):
                            l = 4 * half
                            dve.wait_ge(e2, 4 * h + 3 + half)
                            decayed(Q2v, q_h, l)
                            side.dve_part(dve, 2 * h, 2 * half)
                            link(decayed(Q2v, q_h, l + 2))
                            decayed(Ev, k_h, l)
                            side.dve_part(dve, 2 * h, 2 * half + 1)
                            x = decayed(Ev, k_h, l + 2)
                        x.then_inc(qd, 1)
                        for t in range(TT):
                            dve.wait_ge(od, 2 * h + t + 1)
                            ps = psa[:, 0:2, :].rearrange("p b (l t) -> p (b l) t", l=4)
                            link(nc.vector.tensor_tensor(sc[:, :, :], ps, masks[:, :, :], ALU.mult))
                            nc.vector.tensor_reduce(stt[:, t, t * P:(t + 1) * P], sc[:, :, :].rearrange("p l t -> p t l"), AX.X, ALU.add).then_inc(ev, 1)
                        dve.wait_ge(es, h + 1)
                        nc.vector.tensor_copy(stt[:, 0, P:T], psa[:, 2, 0:P]).then_inc(ev, 1)
                        more = h + 1 < GLA_HEADS
                        if more:
                            differences(h + 1, range(4))
                        side.dve_part(dve, 2 * h + 1, 0)
                        if more:
                            differences(h + 1, range(4, 8)).then_inc(e1, 1)
                        for part in (1, 2, 3):
                            side.dve_part(dve, 2 * h + 1, part)
                        for c in range(4):
                            dve.wait_ge(oc, 2 * (4 * h + c) + 1)
                            nc.vector.tensor_copy(O[:, 4 * h + c, :], psa[:, 3, 0:T]).then_inc(oc, 1)

                @block.scalar
                def _(act):
                    def absolute(half):
                        nc.scalar.activation(E[:, 8 * half:8 * half + 8, :], E[:, 8 * half:8 * half + 8, :], ACT.Abs).then_inc(e2, 1)
                    act.wait_ge(e1, 1)
                    absolute(0)
                    absolute(1)
                    for h in range(GLA_HEADS):
                        act.wait_ge(e2, 4 * h + 2)
                        for half in range(2):
                            side.act_part(act, 2 * h, half)
                            nc.scalar.activation(E[:, 8 * half:8 * half + 8, :], E[:, 8 * half:8 * half + 8, :], ACT.Exp, scale=-1.0).then_inc(e2, 1)
                        side.act_part(act, 2 * h, 2)
                        side.act_part(act, 2 * h, 3)
                        side.act_part(act, 2 * h + 1, 0)
                        side.act_part(act, 2 * h + 1, 1)
                        if h + 1 < GLA_HEADS:
                            act.wait_ge(e1, h + 2)
                            absolute(0)
                        side.act_part(act, 2 * h + 1, 2)
                        if h + 1 < GLA_HEADS:
                            absolute(1)
                        side.act_part(act, 2 * h + 1, 3)

                @block.tensor
                def _(pe):
                    for h in range(GLA_HEADS):
                        side.pe_unit(pe, 2 * h)
                        pe.wait_ge(qd, h + 1)
                        for t in range(TT):
                            if h or t:
                                pe.wait_ge(ev, 3 * h + t)
                            tk = slice(t * P, (t + 1) * P)
                            for l in range(8):
                                for c in range(2):
                                    kk = E[:, 2 * l + c, tk] if l < GLA_LEVELS else QK[:, 4 * h + 2 + c, tk]
                                    qq = Q2[:, 2 * l + c, tk] if l < GLA_LEVELS else QK[:, 4 * h + c, tk]
                                    mm = nc.tensor.matmul(psa[:, l // 4, (l % 4) * P:(l % 4 + 1) * P], kk, qq, start=c == 0, stop=c == 1)
                            mm.then_inc(od, 1)
                        for c in range(2):
                            mm = nc.tensor.matmul(psa[:, 2, 0:P], E[:, 14 + c, 0:P], Q2[:, 14 + c, P:T], start=c == 0, stop=c == 1)
                        mm.then_inc(es, 1)
                        side.pe_unit(pe, 2 * h + 1)
                        pe.wait_ge(ev, 3 * h + 3)
                        for c in range(4):
                            if h or c:
                                pe.wait_ge(oc, 2 * (4 * h + c))
                            col = (4 * h + c) * P
                            nc.tensor.matmul(psa[:, 3, 0:T], Vn[:, 0, col:col + P], stt[:, 0, :], start=True, stop=False)
                            nc.tensor.matmul(psa[:, 3, P:T], Vn[:, 1, col:col + P], stt[:, 1, P:T], start=False, stop=True).then_inc(oc, 1)

            norm(O, CV, 4, "gla_norm_g", S[8], groups=4)
            products(G("gla_z", H, "silu_mul", dst=CV, split=(arena_r[8], arena_r[5])),
                     G("gla_out", pair(8, 5), "mul_add", after=True, dst=Y, src=Tm),
                     loads=(("mem_t", S[4][:, :, :]),))

            M, MH, MQ, MV = S[4], pair(5, 4), S[6], S[7]
            norm(M, M, DC, "mem_ln_g", S[8], split=MH, side=G("gate2a", H, "sig", dst=Tm, bias=("b_gate", 32)))
            MVn = MV[:, 0:4, :].rearrange("p c t -> p (c t)").rearrange("p (t n) -> p t n", t=TT)
            products(G("mem_k", MH, "copy", dst=MQ), G("mem_v", MH, "copy", dst=MVn, natural=True),
                     G("mem_q", H, "copy", dst=MQ, at=4, scale=float(128 ** -0.5)))

            def mem_qk(h, ps):
                for t in range(TT):
                    mm = nc.tensor.matmul(ps[:, t * T:(t + 1) * T], MQ[:, 4 + h, t * P:(t + 1) * P], MQ[:, h, :], start=True, stop=True)
                return mm
            PB = S[8][:, 0:4, :].rearrange("p (b t) s -> p b t s", b=2)
            PT = S[8][:, 4:8, :].rearrange("p (b t) s -> p b t s", b=2)
            attention(MEM_HEADS, mem_qk, lambda h, s: MVn[:, s, h * P:(h + 1) * P], lambda h: MQ[:, 8 + h, :], PB, PT,
                      side=G("gate2b", H, "sig", dst=Tm, at=8, bias=("b_gate", 40)))
            X = S[5]
            products(G("mem_z", H, "silu_mul", dst=MQ, at=8, split=(arena_r[8], arena_r[6])),
                     G("mem_out", pair(8, 6, 8, 12), "mul_add", after=True, dst=Y, src=Tm, split=(arena_r[4], arena_r[2])),
                     G("w_out", pair(4, 2), "resid", after=True, dst=X, needs_loads=True), loads=(("x_t", X[:, :, :]),))
            norm(X, S[0], DC, "final_g", S[4])

        def block_3(own):
            norm(S[0], S[0], DC, "g_pre_3", S[4], split=(arena_r[1], arena_r[0]), spill=spill_x)
            with ExitStack() as rwkv_mem:
                rwkv(rwkv_mem)
            with ExitStack() as mla_mem:
                mla(mla_mem)
            X = S[6]
            products(G("w_out_3", pair(5, 8), "copy", dst=Tm), loads=((spill_x, X[:, :, :]),))
            norm(Tm, Tm, DC, "g_post_3", S[4])
            (added,) = stage_sems("added")
            with nc.Block() as block:
                @block.vector
                def _(dve):
                    nc.vector.tensor_tensor(S[0][:, :, :], X[:, :, :], Tm[:, :, :], ALU.add).then_inc(added, 1)

        NC8 = 8
        CH = 64
        NCH = T // CH

        def rwkv(own):
            def sb(name, shape):
                return own.enter_context(nc.sbuf_tensor(name, shape, F32))
            RK, VD, LW, AA = S[2], S[3], S[4], S[5]
            spill_h = [nc.dram_tensor("normed_" + n, (P, DC, T), F32, kind="Internal").ap() for n in ("hi", "lo")]
            blk = sb("head_ones", [P, P])
            masks64 = sb("chunk_masks", [P, 2, 2, P])
            m16_ts = sb("mask16_ts", [P, 2, P])
            m16_st = sb("mask16_st", [P, 2, P])
            reset = sb("chunk_reset", [P, T])
            products(G("rwkv_rk", H, "copy", dst=RK), G("rwkv_v", H, "copy", dst=VD),
                     G("rwkv_da", H, "copy", dst=VD, at=8, rows=96),
                     loads=(("head_ones", blk[:, :]), ("rwkv_w2", S[6][0:96, :, :]), ("chunk_masks", masks64[:, :, :, :]),
                            ("mask16_ts", m16_ts[:, :, :]), ("mask16_st", m16_st[:, :, :]), ("chunk_reset", reset[:, :]),
                            (arena_r[1][:, :, :].bitcast(F32), spill_h[0]), (arena_r[0][:, 8:16, :].bitcast(F32), spill_h[1][:, 8:16, :])))

            TS = S[7]
            steps, tanh_in, tanh_out = stage_sems("dve_steps", "tanh_in", "tanh_out")
            with nc.Block() as block:
                @block.vector
                def _(dve):
                    link = linker(dve, steps)
                    for buf, rows, a, b, mu in ((RK, P, 0, 16, 0), (VD, P, 0, 8, 16), (VD, 96, 8, 12, 24)):
                        x = buf[0:rows, a:b, :]
                        y = TS[0:rows, 0:b - a, :]
                        nc.vector.tensor_tensor(y[:, :, 1:T - 1], x[:, :, 0:T - 2], x[:, :, 2:T], ALU.add)
                        nc.vector.tensor_copy(y[:, :, 0:1], x[:, :, 1:2])
                        link(nc.vector.tensor_copy(y[:, :, T - 1:T], x[:, :, T - 2:T - 1]))
                        link(nc.vector.scalar_tensor_tensor(out=y, in0=y, scalar=0.5, in1=x, op0=ALU.mult, op1=ALU.subtract))
                        for c in range(b - a):
                            z = nc.vector.scalar_tensor_tensor(out=x[:, c, :], in0=y[:, c, :], scalar=vecs[0:rows, VEC_AT["rwkv_mu_3"] + mu + c:VEC_AT["rwkv_mu_3"] + mu + c + 1],
                                                               in1=x[:, c, :], op0=ALU.mult, op1=ALU.add)
                        link(z)
                    nc.vector.tensor_copy(small[:, 0:1], vecs[:, 0:1]).then_inc(tanh_in, 1)

                @block.scalar
                def _(act):
                    act.wait_ge(tanh_in, 1)
                    nc.scalar.activation(VD[0:96, 8:10, :], VD[0:96, 8:10, :], ACT.Tanh).then_inc(tanh_out, 1)

            za, zb = stage_sems("lowrank_done", "lowrank_used")
            with nc.Block() as block:
                @block.tensor
                def _(pe):
                    for n in range(32):
                        j, c = n // 8, n % 8
                        if n >= 4:
                            pe.wait_ge(zb, n - 3)
                        nc.tensor.matmul(psa[:, n % 4, 0:T], S[6][0:96, :, :].rearrange("p c t -> p (c t)")[:, j * 1024 + c * P:j * 1024 + (c + 1) * P],
                                         VD[0:96, 8 + j, :], start=True, stop=True).then_inc(za, 1)

                @block.scalar
                def _(act):
                    for n in range(32):
                        j, c = n // 8, n % 8
                        act.wait_ge(za, n + 1)
                        dst = (LW if j < 2 else AA)[:, (j % 2) * 8 + c, :]
                        nc.scalar.activation(dst, psa[:, n % 4, 0:T], ACT.Sigmoid,
                                             bias=vcol(("rwkv_w0_f_3", "rwkv_w0_b_3", "rwkv_a0_f_3", "rwkv_a0_b_3")[j], c)).then_inc(zb, 1)
            KK = VD[:, 8:16, :]
            sq_in, sq_out, s_done, s_used, r_out, steps = stage_sems("kk_ready", "kk_squared", "kk_sums", "kk_sums_used", "root_done", "dve_steps")
            with nc.Block() as block:
                @block.vector
                def _(dve):
                    link = linker(dve, steps)
                    nc.vector.tensor_scalar(LW[:, :, :], LW[:, :, :], -float(np.exp(-0.5)), None, ALU.mult)
                    for c in range(NC8):
                        x = nc.vector.tensor_scalar(KK[:, c, :], RK[:, 8 + c, :], vcol("rwkv_k_k_3", c), None, ALU.mult)
                    x.then_inc(sq_in, 1)
                    dve.wait_ge(r_out, NC8)
                    link(nc.vector.tensor_scalar(TS[:, 8:16, :], TS[:, 8:16, :], 1e-12, None, ALU.max))
                    link(nc.vector.reciprocal(TS[:, 8:16, :], TS[:, 8:16, :]))
                    nc.vector.tensor_tensor(KK, KK, TS[:, 8:16, :], ALU.mult)

                @block.scalar
                def _(act):
                    act.wait_ge(sq_in, 1)
                    nc.scalar.activation(TS[:, 0:8, :], KK, ACT.Square).then_inc(sq_out, 1)
                    for c in range(NC8):
                        act.wait_ge(s_done, c + 1)
                        nc.scalar.activation(TS[:, 8 + c, :], psa[:, c % 4, 0:T], ACT.Sqrt).then_inc(r_out, 1)

                @block.tensor
                def _(pe):
                    pe.wait_ge(sq_out, 1)
                    for c in range(NC8):
                        if c >= 4:
                            pe.wait_ge(r_out, c - 3)
                        nc.tensor.matmul(psa[:, c % 4, 0:T], blk[:, :], TS[:, c, :], start=True, stop=True).then_inc(s_done, 1)

            with ExitStack() as scan_mem:
                rwkv_scan(scan_mem, RK, VD, LW, AA, (masks64, m16_ts, m16_st, reset))
            rwkv_out(own, blk, RK, VD, LW, AA, spill_h)

        def rwkv_scan(own, RK, VD, LW, AA, scan_masks):
            def sb(name, shape):
                return own.enter_context(nc.sbuf_tensor(name, shape, F32))
            pool = {0: [[S[6], 0], [S[1], 0]], 1: [[S[7], 0], [S[8], 0]]}

            def carve(d, n):
                for slot in pool[d]:
                    if slot[1] + n <= DC * T:
                        slot[1] += n
                        return slot[0][:, :, :].rearrange("p c t -> p (c t)")[:, slot[1] - n:slot[1]]
                raise AssertionError("arena is full")
            masks64, m16_ts, m16_st, reset = scan_masks

            def quad(ap):
                return ap.rearrange("p (i n) -> p i n", i=4)

            def per4(mask):
                return mask.rearrange("p (a n) -> p a n", a=1).broadcast_to([P, 4, mask.shape[-1]])

            class Dir:
                pass
            dirs = []
            for d in range(2):
                q = Dir()
                q.bank = [(psg, psa)[d][:, b, :] for b in range(4)]
                q.two = [(psg, psa)[d][:, 2 * b:2 * b + 2, :].rearrange("p b n -> p (b n)") for b in range(2)]
                q.M1 = carve(d, 1024).rearrange("p (i k t) -> p i k t", i=4, k=2)
                q.M2 = carve(d, 1024).rearrange("p (i k t) -> p i k t", i=4, k=2)
                q.SQ0 = carve(d, 1024).rearrange("p (k i t) -> p k i t", k=2, i=4)
                q.SQ1 = carve(d, 1024).rearrange("p (k i t) -> p k i t", k=2, i=4)
                q.RT = quad(carve(d, 512))
                q.B = [quad(carve(d, 512)) for _ in range(2)]
                q.TT = quad(carve(d, 512))
                q.AR = carve(d, 512).rearrange("p (t k n) -> p t k n", t=2, k=2)
                q.bk = carve(d, 512).rearrange("p (k n) -> p k n", k=2)
                q.bkp = tmp2[d][:, :, :]
                q.tok = flat(S[0], 8 + 4 * d, 12 + 4 * d).rearrange("p (k t n) -> p k t n", k=4, t=2)
                q.EX = carve(d, 1024).rearrange("p (k n) -> p k n", k=4) if d else stat
                q.GC = sb(f"gc{d}", [P, NCH])
                q.t1 = q.EX[:, 2, :]
                q.W1T = tmp[d][:, 1, :].rearrange("p (t n) -> p t n", t=2)
                q.Z = tmp[d][:, 0, :].rearrange("p (i n) -> p i n", i=4)
                q.W2 = q.bk[:, 0, :].rearrange("p (h t n) -> p h t n", h=2, t=2)
                q.U = q.W2
                q.S = carve(0, 256).rearrange("p (k n) -> p k n", k=NCH)
                q.ka, q.kf = tmp[d][:, 0, :], tmp[d][:, 1, :]
                q.order = range(NCH) if d == 0 else range(NCH - 1, -1, -1)
                dirs.append(q)
            prep_in, prep_exp, chain, y_done, y_copied, started, passed = stage_sems("exponents", "exponentials", "dve_chain", "y_done", "y_copied", "states_zero", "waits_passed")
            prepared = stage_sems("prepared0", "prepared1")
            pe_step = stage_sems("pe_step0", "pe_step1")
            act_step = stage_sems("act_step0", "act_step1")
            dve_step = stage_sems("dve_step0", "dve_step1")
            inst = [(hp, t) for hp in range(2) for t in range(TT)]

            STEPS = [("tok", 1, 1), ("gram", 0, 1), ("d2", 1, 0), ("d4", 1, 1), ("d8", 1, 1), ("b8", 0, 1), ("t16", 1, 0),
                     ("n1", 1, 0), ("n2", 1, 0), ("cz", 1, 1), ("tt", 0, 1), ("w", 1, 0)]
            for k in range(NCH):
                STEPS.append((("u", k), 0, 1))
                if k < NCH - 1:
                    STEPS.append((("s", k), 0, 1))
            NS = len(STEPS)
            NA = sum(x[1] for x in STEPS)
            ND = sum(x[2] for x in STEPS)

            def seen(n, col):
                return sum(x[col] for x in STEPS[:n])

            def rows(hp):
                return slice(CH * hp, CH * hp + CH)

            def pe_emit(q, name):
                b0, b1, b2, b3 = q.bank
                mm = nc.tensor.matmul
                tr = nc.tensor.transpose

                def four(bank, lhs, rhs):
                    for i in range(4):
                        x = mm(bank[:, i * P:(i + 1) * P], lhs[:, i, :], rhs[:, i, :], start=True, stop=True)
                    return x
                Dm, DT, E2, E2T = q.SQ0[:, 0], q.SQ0[:, 1], q.SQ1[:, 0], q.SQ1[:, 1]
                if name == "tok":
                    for t in range(TT):
                        tk = slice(t * P, (t + 1) * P)
                        tr(b0[:, tk], q.AR[:, t, 0, :], ident[:, :])
                        tr(b0[:, T + t * P:T + (t + 1) * P], q.bkp[:, 0, tk], ident[:, :])
                        tr(b1[:, tk], q.bkp[:, 1, tk], ident[:, :])
                        tr(b1[:, T + t * P:T + (t + 1) * P], vc_buf[:, tk], ident[:, :])
                    for i, (hp, t) in enumerate(inst):
                        x = mm(q.bank[2 + hp][:, t * P:(t + 1) * P], q.AR[rows(hp), t, 0, :], q.bk[rows(hp), 0, t * P:(t + 1) * P], start=True, stop=True)
                elif name == "gram":
                    for k in range(2):
                        for i, (hp, t) in enumerate(inst):
                            x = mm(q.two[k][:, i * T:(i + 1) * T], q.bk[rows(hp), k, t * P:(t + 1) * P],
                                   q.AR[rows(hp), t, :, :].rearrange("p k n -> p (k n)"), start=True, stop=True)
                elif name == "d2":
                    four(b0, DT, Dm)
                    x = four(b1, Dm, DT)
                elif name == "d4":
                    four(b0, E2T, E2)
                    four(b1, E2, E2T)
                    x = four(b2, E2, q.B[0])
                elif name == "d8":
                    four(b0, DT, Dm)
                    x = four(b2, Dm, q.B[1])
                elif name == "b8":
                    x = four(b2, E2, q.B[0])
                elif name == "t16":
                    for i in range(4):
                        x = tr(b0[:, i * P:(i + 1) * P], q.B[1][:, i, :], ident[:, :])
                elif name == "n1":
                    four(b0, q.RT, E2T)
                    x = four(b1, E2T, q.RT)
                elif name == "n2":
                    x = four(b0, DT, Dm)
                elif name == "cz":
                    four(b2, E2, q.B[1])
                    for i, (hp, t) in enumerate(inst):
                        x = mm(b3[:, i * CH:(i + 1) * CH], q.M2[:, i, 0, :], q.tok[:, 3, t, CH * hp:CH * hp + CH], start=True, stop=True)
                elif name == "tt":
                    x = four(b2, Dm, q.B[0])
                elif name == "w":
                    for i, (hp, t) in enumerate(inst):
                        mm(b0[rows(hp), t * P:(t + 1) * P], q.tok[:, 0, t, CH * hp:CH * hp + CH], q.TT[:, i, :], start=True, stop=True)
                        x = mm(b1[:, i * CH:(i + 1) * CH], q.TT[:, i, :], q.Z[:, i, :], start=True, stop=True)
                elif name[0] == "u":
                    c = q.order[name[1]]
                    half = rows(c % 2)
                    for hp in range(2):
                        x = mm(q.bank[hp][half, 0:CH], q.W1T[rows(hp), c // 2, CH * (c % 2):CH * (c % 2) + CH],
                               q.S[rows(hp), name[1], :], start=True, stop=True)
                elif name[0] == "s":
                    c = q.order[name[1]]
                    half = rows(c % 2)
                    for hp in range(2):
                        mm(b2[rows(hp), 0:CH], q.tok[half, 1, c // 2, CH * hp:CH * hp + CH], q.U[half, hp, c // 2, :], start=True, stop=False)
                        x = mm(b2[rows(hp), 0:CH], q.tok[half, 2, c // 2, CH * hp:CH * hp + CH],
                               q.tok[half, 3, c // 2, CH * hp:CH * hp + CH], start=False, stop=True)
                return x

            def act_emit(q, name):
                cp = lambda o, i: nc.scalar.activation(o, i, ACT.Copy)
                if name == "tok":
                    return cp(q.tok, q.two[0].rearrange("p (k t n) -> p k t n", k=4, t=2))
                if name in ("d2", "n1", "d4"):
                    src = q.two[0].rearrange("p (k i t) -> p k i t", k=2, i=4)
                    return cp(q.SQ1 if name == "d2" else q.SQ0, src)
                if name in ("d8", "n2"):
                    return cp(q.SQ1[:, 0], quad(q.bank[0]))
                if name == "t16":
                    return cp(q.SQ1[:, 1], quad(q.bank[0]))
                if name == "cz":
                    return cp(q.Z, quad(q.bank[3][:, 0:T]))
                if name == "w":
                    cp(q.W1T, q.bank[0][:, 0:T].rearrange("p (t n) -> p t n", t=2))
                    return cp(q.W2, q.bank[1][:, 0:T].rearrange("p (h t n) -> p h t n", h=2, t=2))

            def dve_emit(d, q, name, link):
                tt = nc.vector.tensor_tensor
                b2 = quad(q.bank[2])
                if name == "tok":
                    four = lambda ap: ap.rearrange("p (h t) n -> p h t n", h=2)
                    grams = q.two[1].rearrange("p (h x) -> p h x", h=2)[:, :, 0:T].rearrange("p h (t n) -> p h t n", t=TT)
                    return tt(four(q.SQ0[:, 0]), grams, four(per4(m16_ts[:, d, :])), ALU.mult)
                if name == "gram":
                    m = masks64[:, d, :, :].rearrange("p k t -> p (k t)")
                    for k, M in ((1, q.M2), (0, q.M1)):
                        x = tt(M.rearrange("p i k t -> p i (k t)"), q.two[k].rearrange("p (i n) -> p i n", i=4), per4(m), ALU.mult)
                    link(x)
                    link(tt(q.SQ0[:, 1], q.M1[:, :, 0, :], per4(m16_st[:, d, :]), ALU.mult))
                    tt(q.RT, q.M1[:, :, 0, :], q.SQ0[:, 1], ALU.subtract)
                    return tt(q.B[0], q.SQ0[:, 1], per4(ident[:, :]), ALU.add)
                if name == "d4":
                    return tt(q.B[1], b2, q.B[0], ALU.add)
                if name == "d8":
                    return tt(q.B[0], b2, q.B[1], ALU.add)
                if name == "b8":
                    return tt(q.B[1], b2, q.B[0], ALU.add)
                if name == "cz":
                    return tt(q.B[0], b2, q.B[1], ALU.add)
                if name == "tt":
                    return tt(q.TT, b2, q.B[0], ALU.add)
                c = q.order[name[1]]
                if name[0] == "u":
                    half = rows(c % 2)
                    return tt(q.U[half, :, c // 2, :], q.two[0].rearrange("p (h x) -> p h x", h=2)[half, :, 0:CH], q.W2[half, :, c // 2, :], ALU.add)
                return nc.vector.scalar_tensor_tensor(out=q.S[:, name[1] + 1, :], in0=q.S[:, name[1], :], scalar=q.GC[:, c:c + 1],
                                                      in1=q.bank[2][:, 0:CH], op0=ALU.mult, op1=ALU.add)

            vc_buf = carve(0, T)
            NCHAIN = 2 * (4 + 3 + 2)
            with nc.Block() as block:
                @block.tensor
                def _(pe):
                    pe.wait_ge(started, 1)
                    with pe.Fori(0, NC8, 1) as it:
                        for n, (name, _, _) in enumerate(STEPS):
                            for d, q in enumerate(dirs):
                                if n == 0:
                                    pe.wait_ge(prepared[d], it + 1)
                                else:
                                    pe.wait_ge(act_step[d], it * NA + seen(n, 1))
                                if seen(n, 2):
                                    pe.wait_ge(dve_step[d], it * ND + seen(n, 2))
                                if name[0] in ("u", "s"):
                                    pe.sem_inc(passed, 1)
                                pe_emit(q, name).then_inc(pe_step[d], 1)
                        for d in range(2):
                            pe.wait_ge(dve_step[d], it * ND + ND)
                        yb = dirs[0].bank[3]
                        for i, (hp, t) in enumerate(inst):
                            y = yb[rows(hp), t * P:(t + 1) * P]
                            for d, q in enumerate(dirs):
                                nc.tensor.matmul(y, q.tok[:, 3, t, CH * hp:CH * hp + CH], q.M2[:, i, 1, :], start=d == 0, stop=False)
                                nc.tensor.matmul(y, q.U[:, hp, t, :], q.M1[:, i, 1, :], start=False, stop=False)
                                for k in range(NCH):
                                    c = q.order[k]
                                    if c // 2 == t:
                                        mm = nc.tensor.matmul(yb[rows(hp), c * CH:(c + 1) * CH], q.S[rows(hp), k, :],
                                                              q.AR[rows(hp), t, 1, CH * (c % 2):CH * (c % 2) + CH],
                                                              start=False, stop=d == 1 and k == max(kk for kk in range(NCH) if q.order[kk] // 2 == t))
                        mm.then_inc(y_done, 1)

                @block.scalar
                def _(act):
                    act.sem_inc(y_copied, 1)
                    with act.Fori(0, NC8, 1) as it:
                        for d, q in enumerate(dirs):
                            act.wait_ge(prep_in, 2 * it + (d + 1))
                            nc.scalar.activation(q.EX[:, 3, :], q.EX[:, 0, :], ACT.Exp, scale=-1.0).then_inc(prep_exp, 1)
                            act.wait_ge(prep_exp, it * 6 + (3 * d + 1))
                            nc.scalar.activation(q.EX[:, 0:3, :], q.EX[:, 0:3, :], ACT.Exp).then_inc(prep_exp, 1)
                            nc.scalar.activation(q.GC[:, :], q.GC[:, :], ACT.Exp).then_inc(prep_exp, 1)
                        for n, (name, a, _) in enumerate(STEPS):
                            if a:
                                for d, q in enumerate(dirs):
                                    act.wait_ge(pe_step[d], it * NS + (n + 1))
                                    act_emit(q, name).then_inc(act_step[d], 1)
                        act.wait_ge(y_done, it + 1)
                        nc.scalar.activation(LW[:, bass.ds(it, 1), :].rearrange("p a t -> p (a t)"), dirs[0].bank[3][:, 0:T], ACT.Copy).then_inc(y_copied, 1)

                @block.vector
                def _(dve):
                    for d, q in enumerate(dirs):
                        x = nc.vector.memset(q.S[:, 0, :], 0.0)
                    nc.vector.memset(small[:, :], 0.0).then_inc(started, 1)
                    dve.wait_ge(started, 1)
                    v = nc.vector
                    with dve.Fori(0, NC8, 1) as it:
                        count = [0]

                        def link(x):
                            count[0] += 1
                            x.then_inc(chain, 1)
                            dve.wait_ge(chain, it * NCHAIN + count[0])

                        def pair(buf, off):
                            return buf[:, bass.ds(it + off, 1), :].rearrange("p a t -> p (a t)")
                        v.tensor_copy(vc_buf[:, :], pair(VD, 0))
                        for d, q in enumerate(dirs):
                            lw = pair(LW, 8 * d)
                            by = lambda ap: ap.rearrange("p (c n) -> p c n", c=NCH)
                            link(v.tensor_tensor_scan(q.ka, reset[:, :], lw, 0.0, ALU.mult, ALU.add))
                            tot = by(q.ka)[:, :, CH - 1:CH]
                            incl, excl, tail = q.EX[:, 0, :], q.EX[:, 1, :], q.EX[:, 2, :]
                            link(v.tensor_tensor(by(excl if d else tail), tot.broadcast_to([P, NCH, CH]), by(q.ka), ALU.subtract))
                            link(v.tensor_tensor(tail if d else excl, q.ka, lw, ALU.subtract))
                            if d:
                                link(v.tensor_tensor(incl, excl, lw, ALU.add))
                            else:
                                link(v.tensor_copy(incl, q.ka))
                            v.tensor_copy(q.GC[:, :], q.ka.rearrange("p (c n) -> p c n", c=NCH)[:, :, CH - 1]).then_inc(prep_in, 1)
                        for d, q in enumerate(dirs):
                            aa = pair(AA, 8 * d)
                            link(v.tensor_tensor(q.ka, pair(VD, 8), aa, ALU.mult))
                            link(v.tensor_scalar(q.kf, aa, 1.0, vecs[:, bass.ds(it + VEC_AT["rwkv_k_a_3"], 1)], ALU.subtract, ALU.mult))
                            link(v.scalar_tensor_tensor(out=q.kf, in0=q.kf, scalar=1.0, in1=pair(RK, 8), op0=ALU.add, op1=ALU.mult))
                            dve.wait_ge(prep_exp, it * 6 + (3 * d + 3))
                            til = lambda ap: ap.rearrange("p (t n) -> p t n", t=TT)
                            dve.wait_ge(y_copied, it + 1)
                            v.scalar_tensor_tensor(out=q.AR[:, :, 0, :], in0=til(pair(VD, 8)), scalar=-1.0, in1=til(q.EX[:, 1, :]), op0=ALU.mult, op1=ALU.mult)
                            v.tensor_tensor(q.AR[:, :, 1, :], til(pair(RK, 0)), til(q.EX[:, 0, :]), ALU.mult)
                            v.tensor_tensor(q.bk[:, 0, :], q.ka, q.EX[:, 3, :], ALU.mult)
                            v.tensor_tensor(q.bk[:, 1, :], q.kf, q.EX[:, 3, :], ALU.mult)
                            v.tensor_tensor(q.bkp[:, 0, :], q.ka, q.EX[:, 2, :], ALU.mult)
                            v.tensor_tensor(q.bkp[:, 1, :], q.kf, q.EX[:, 2, :], ALU.mult).then_inc(prepared[d], 1)
                        for n, (name, _, a) in enumerate(STEPS):
                            if a:
                                for d, q in enumerate(dirs):
                                    dve.wait_ge(pe_step[d], it * NS + (n + 1))
                                    dve_emit(d, q, name, link).then_inc(dve_step[d], 1)
                        assert count[0] == NCHAIN

        def rwkv_out(own, blk, RK, VD, LW, AA, spill_h):
            YR, G6, G7 = LW, S[6], S[7]
            side = Prod("gate_rwkv", H, "sig", dst=S[8])
            a_in, a_out, p1, p2, steps, back, again = stage_sems("act_in", "act_out", "pe_done", "pe_used", "dve_steps", "h_back", "h_again")
            with nc.Block() as block:
                @block.sync
                def _(sp):
                    for a, b, k in ((0, 8, 1), (8, 16, 1), (8, 16, 0)):
                        sp.dma_start(S[k][:, a:b, :], spill_h[1 - k][:, a:b, :]).then_inc(back, 16)
                    side.sp(sp)

                @block.vector
                def _(dve):
                    link = linker(dve, steps)
                    v = nc.vector
                    link(v.tensor_tensor(AA[:, 0:8, :], AA[:, 0:8, :], AA[:, 8:16, :], ALU.add))
                    for c in range(NC8):
                        x = v.tensor_scalar(AA[:, c, :], AA[:, c, :], 2.0, vcol("rwkv_k_a_3", c), ALU.subtract, ALU.mult)
                    link(x)
                    link(v.scalar_tensor_tensor(out=AA[:, 0:8, :], in0=AA[:, 0:8, :], scalar=2.0, in1=RK[:, 8:16, :], op0=ALU.add, op1=ALU.mult))
                    for c in range(NC8):
                        x = v.scalar_tensor_tensor(out=AA[:, c, :], in0=AA[:, c, :], scalar=vcol("rwkv_r_k_3", c), in1=RK[:, c, :], op0=ALU.mult, op1=ALU.mult)
                    x.then_inc(a_in, 1)
                    side.dve_unit(dve, 0)
                    side.dve_unit(dve, 1)
                    for c in range(NC8):
                        dve.wait_ge(p1, 2 * c + 2)
                        v.scalar_tensor_tensor(out=G6[:, c, :], in0=psa[:, 2 * (c % 2), 0:T], scalar=-1.0 / 64, in1=YR[:, c, :], op0=ALU.mult, op1=ALU.add)
                        v.tensor_tensor(G7[:, c, :], psa[:, 2 * (c % 2) + 1, 0:T], VD[:, c, :], ALU.mult).then_inc(p2, 1)
                    side.dve_unit(dve, 2)
                    for c in range(NC8):
                        dve.wait_ge(p1, 16 + c + 1)
                        v.tensor_scalar(G6[:, 8 + c, :], psa[:, c % 4, 0:T], 1.0 / 64, 64e-5, ALU.mult, ALU.add).then_inc(p2, 1)
                    dve.wait_ge(a_out, 2)
                    link(v.reciprocal(G6[:, 8:16, :], G6[:, 8:16, :]))
                    side.dve_unit(dve, 3)
                    link(v.tensor_tensor(G6[:, 0:8, :], G6[:, 0:8, :], G6[:, 8:16, :], ALU.mult))
                    side.dve_unit(dve, 4)
                    for c in range(NC8):
                        x = v.tensor_scalar(G6[:, c, :], G6[:, c, :], vcol("rwkv_gn_g_3", c), vcol("rwkv_gn_b_3", c), ALU.mult, ALU.add)
                    link(x)
                    side.dve_unit(dve, 5)
                    v.tensor_tensor(YR[:, 0:8, :], G6[:, 0:8, :], G7[:, 0:8, :], ALU.add)
                    for u in range(6, side.n):
                        side.dve_unit(dve, u)

                @block.tensor
                def _(pe):
                    pe.wait_ge(again, 2)
                    side.pe_unit(pe, 0)
                    side.pe_unit(pe, 1)
                    pe.wait_ge(a_in, 1)
                    for c in range(NC8):
                        if c >= 2:
                            pe.wait_ge(p2, c - 1)
                        nc.tensor.matmul(psa[:, 2 * (c % 2), 0:T], blk[:, :], YR[:, c, :], start=True, stop=True).then_inc(p1, 1)
                        nc.tensor.matmul(psa[:, 2 * (c % 2) + 1, 0:T], blk[:, :], AA[:, c, :], start=True, stop=True).then_inc(p1, 1)
                    side.pe_unit(pe, 2)
                    pe.wait_ge(a_out, 1)
                    for c in range(NC8):
                        if c >= 4:
                            pe.wait_ge(p2, 8 + c - 3)
                        nc.tensor.matmul(psa[:, c % 4, 0:T], blk[:, :], AA[:, 8 + c, :], start=True, stop=True).then_inc(p1, 1)
                    for u in range(3, side.n):
                        side.pe_unit(pe, u)

                @block.scalar
                def _(act):
                    act.wait_ge(back, 48)
                    nc.scalar.activation(arena_r[1][:, :, :], S[1][:, :, :], ACT.Copy).then_inc(again, 1)
                    nc.scalar.activation(arena_r[0][:, 8:16, :], S[0][:, 8:16, :], ACT.Copy).then_inc(again, 1)
                    side.act_unit(act, 0)
                    side.act_unit(act, 1)
                    act.wait_ge(p2, NC8)
                    nc.scalar.activation(AA[:, 8:16, :], G6[:, 0:8, :], ACT.Square).then_inc(a_out, 1)
                    side.act_unit(act, 2)
                    act.wait_ge(p2, 2 * NC8)
                    nc.scalar.activation(G6[:, 8:16, :], G6[:, 8:16, :], ACT.Sqrt).then_inc(a_out, 1)
                    for u in range(3, side.n):
                        side.act_unit(act, u)
            products(G("z_rwkv", H, "silu_mul", dst=YR, split=(arena_r[5], arena_r[4])),
                     G("br_rwkv", pair(5, 4), "bias_mul", after=True, dst=S[8]))

        def mla(own):
            QA, QN, RO = S[4], S[5], S[6]
            rot = own.enter_context(nc.sbuf_tensor("rotary", [P, 2, T], F32))
            OA = S[3]
            products(G("mla_qkv_a", H, "copy", dst=QA), G("mla_k_rope", H, "copy", dst=QA, at=8),
                     loads=(("rotary", rot[:, :, :]),))
            QL, KL = pair(3, 4, 0, 4), pair(3, 4, 4, 8)
            norm(QA[:, 0:4, :], QA[:, 0:4, :], 4, "mla_q_norm_3", S[7], split=QL)
            norm(QA[:, 4:8, :], QA[:, 4:8, :], 4, "mla_kv_norm_3", S[7], split=KL)
            VN = RO[:, 8:16, :].rearrange("p c t -> p (c t)").rearrange("p (t n) -> p t n", t=TT)
            scale = float((128 + 64) ** -0.5)
            products(G("mla_q_nope", QL, "copy", dst=QN, scale=scale), G("mla_q_rope", QL, "copy", dst=RO, scale=scale),
                     G("mla_k_nope", KL, "copy", dst=QN, at=8), G("mla_v", KL, "copy", dst=VN, natural=True))
            (steps,) = stage_sems("dve_steps")
            with nc.Block() as block:
                @block.vector
                def _(dve):
                    link = linker(dve, steps)

                    def table(k, n):
                        return rot[:, k:k + 1, :].broadcast_to([P, n, T])
                    for a, n, buf in ((0, 4, RO), (8, 1, QA)):
                        x, y = buf[:, a:a + n, :], buf[:, a + n:a + 2 * n, :]
                        nc.vector.tensor_tensor(x, x, table(0, n), ALU.mult)
                        link(nc.vector.tensor_tensor(y, y, table(1, n), ALU.mult))
                        link(nc.vector.tensor_tensor(x, x, y, ALU.add))

            def qk(h, ps):
                half = slice(64 * (h % 2), 64 * (h % 2) + 64)
                for t in range(TT):
                    tk = slice(t * P, (t + 1) * P)
                    nc.tensor.matmul(ps[:, t * T:(t + 1) * T], QN[:, h, tk], QN[:, 8 + h, :], start=True, stop=False)
                    mm = nc.tensor.matmul(ps[:, t * T:(t + 1) * T], RO[half, h // 2, tk], QA[half, 8, :], start=False, stop=True)
                return mm
            PB = S[2][:, 0:4, :].rearrange("p (b t) s -> p b t s", b=2)
            PT = S[2][:, 4:8, :].rearrange("p (b t) s -> p b t s", b=2)
            attention(8, qk, lambda h, s: VN[:, s, h * P:(h + 1) * P], lambda h: OA[:, h, :], PB, PT,
                      side=G("gate_mla", H, "sig", dst=S[7]))
            products(G("z_mla", H, "silu_mul", dst=OA, split=(arena_r[4], arena_r[3])),
                     G("br_mla", pair(4, 3), "mul_add", after=True, dst=S[8], src=S[7], split=(arena_r[5], arena_r[8])))

        IH, NH, NKV, TOPK, RB = 8, 16, 4, 64, 32

        def block_2(own):
            tri = own.enter_context(nc.sbuf_tensor("causal_t", [P, P], F32))
            with ExitStack() as attn_mem:
                sparse_attention(attn_mem, tri)
            X = S[6]
            sgu(tri, X)
            norm(X, S[5], DC, "norm2_g_2", S[4], split=(arena_r[1], arena_r[5]))
            for c in range(4):
                F, hi = 2 + c % 2, 7 + c % 2
                products(G(f"ff1_{c}", pair(1, 5), "relu2", dst=S[F], split=(arena_r[hi], arena_r[F])),
                         G(f"ff2_{c}", pair(hi, F), "resid", after=True, dst=X))
            norm(X, S[0], DC, "final_g_2", S[4])

        def sparse_attention(own, tri):
            def sb(name, shape):
                return own.enter_context(nc.sbuf_tensor(name, shape, F32))
            Q, KI, V4 = S[2], S[3], S[3]
            norm(S[0], S[0], DC, "norm1_g_2", S[4], split=(arena_r[1], arena_r[0]), spill=spill_x)
            wi = sb("index_weights", [P, TT, IH])
            onehot = flat(S[7][0:RB], 8, 10)
            rel = sb("rel_bias_sb", [RB, NH])
            exch = sb("exchange", [P, P])
            bvec = flat(S[7][0:NH], 10, 12)
            causal = sb("causal", [P, 2, TT, T])
            VN = V4[:, 12:16, :].rearrange("p c t -> p (c t)").rearrange("p (t n) -> p t n", t=TT)
            products(G("sa_q", H, "copy", dst=Q, scale=float(128 ** -0.5)), G("sa_k", H, "copy", dst=KI),
                     G("sa_v", H, "copy", dst=VN, natural=True), G("sa_qi", H, "copy", dst=KI, at=4),
                     G("sa_ki", H, "copy_small", dst=KI[:, 8, :]), G("sa_wi", H, "copy_narrow", dst=wi[:, :, :], natural=True),
                     loads=(("bucket_onehot", onehot), ("rel_bias", rel[:, :]), ("exchange", exch[:, :]),
                            ("causal", causal[:, :, :, :]), ("causal_t", tri[:, :])))

            RBs = [S[5], S[6]]
            RBv = [r[:, 0:12, :].rearrange("p c t -> p (c t)").rearrange("p (h z) -> p h z", h=8) for r in RBs]
            scratch = nc.dram_tensor("bias_scratch", (NH, 512), F32, kind="Internal").ap()
            pe_b, act_b, dma_b = stage_sems("bias_done", "bias_copied", "bias_moved")
            idx_done, relu_done, steps, scaled = stage_sems("index_done", "relu_done", "dve_steps", "scaled")
            RL = S[7][:, 0:2, :]
            SC = S[7][:, 2:4, :]
            WK = S[7][:, 4:6, :]
            MK = S[8][:, 8:10, :]
            m8 = small[:, 16:32]
            side = Prod("sgu_u", H, "copy", dst=S[4])
            with nc.Block() as block:
                @block.sync
                def _(sp):
                    side.sp(sp)
                    sp.wait_ge(act_b, 1)
                    sp.dma_start(scratch, bvec).then_inc(dma_b, 16)
                    sp.wait_ge(dma_b, 16)
                    for k in range(2):
                        src = bass.AP(tensor=scratch.tensor, offset=scratch.offset + 8 * k * 512, ap=[[1, P], [512, 8], [1, 384]])
                        sp.dma_start(RBv[k], src).then_inc(dma_b, 16)
                    sp.wait_ge(dma_b, 48)

                @block.tensor
                def _(pe):
                    nc.tensor.matmul(psa[0:NH, 3, :], rel[:, :], onehot, start=True, stop=True).then_inc(pe_b, 1)
                    for t in range(TT):
                        for h in range(IH):
                            n = IH * t + h
                            if n == 3:
                                pe.wait_ge(act_b, 1)
                            if n in (4, 10):
                                side.pe_unit(pe, n // 10)
                            if n >= 4:
                                pe.wait_ge(relu_done, n - 3)
                            half = slice(64 * (h % 2), 64 * (h % 2) + 64)
                            nc.tensor.matmul(psa[:, n % 4, 0:T], KI[half, 4 + h // 2, t * P:(t + 1) * P], KI[half, 8, :],
                                             start=True, stop=True).then_inc(idx_done, 1)

                    for u in range(2, side.n):
                        side.pe_unit(pe, u)

                @block.scalar
                def _(act):
                    act.wait_ge(pe_b, 1)
                    nc.scalar.activation(bvec, psa[0:NH, 3, :], ACT.Copy).then_inc(act_b, 1)
                    for n in range(TT * IH):
                        act.wait_ge(idx_done, n + 1)
                        if n >= 2:
                            act.wait_ge(scaled, n)
                        nc.scalar.activation(RL[:, n % 2, :], psa[:, n % 4, 0:T], ACT.Relu).then_inc(relu_done, 1)
                        if n in (3, 9):
                            side.act_unit(act, n // 9)
                    for u in range(2, side.n):
                        side.act_unit(act, u)

                @block.vector
                def _(dve):
                    link = linker(dve, steps)
                    v = nc.vector
                    v.tensor_scalar(wi[:, :, :], wi[:, :, :], float(IH ** -0.5 * 64 ** -0.5), None, ALU.mult).then_inc(scaled, 1)
                    dve.wait_ge(scaled, 1)
                    for t in range(TT):
                        for h in range(IH):
                            n = IH * t + h
                            dve.wait_ge(relu_done, n + 1)
                            dve.wait_ge(scaled, n + 1)
                            w = wi[:, t, h:h + 1]
                            if h == 0:
                                v.tensor_scalar(SC[:, t, :], RL[:, n % 2, :], w, None, ALU.mult).then_inc(scaled, 1)
                            else:
                                v.scalar_tensor_tensor(out=SC[:, t, :], in0=RL[:, n % 2, :], scalar=w, in1=SC[:, t, :],
                                                       op0=ALU.mult, op1=ALU.add).then_inc(scaled, 1)
                            if n in (3, 9):
                                side.dve_unit(dve, n // 9)
                    dve.wait_ge(scaled, TT * IH + 1)
                    link(v.tensor_tensor(SC, SC, causal[:, 1, :, :], ALU.add))
                    for r in range(TOPK // 8):
                        src = SC if r == 0 else WK
                        for t in range(TT):
                            x = v.max(m8[:, 8 * t:8 * t + 8], src[:, t, :])
                        link(x)
                        for t in range(TT):
                            x = v.match_replace(out=WK[:, t, :], in_to_replace=m8[:, 8 * t:8 * t + 8], in_values=src[:, t, :], imm_value=-3e38)
                        link(x)
                        if r % 2:
                            side.dve_unit(dve, 2 + r // 2)
                    link(v.tensor_tensor(WK, WK, SC, ALU.is_equal))
                    link(v.tensor_scalar(WK, WK, -1.0, 1.0, ALU.mult, ALU.add))
                    link(v.tensor_tensor(WK, WK, causal[:, 0, :, :], ALU.mult))
                    link(v.tensor_scalar(MK, WK, 1.0, -NEG, ALU.subtract, ALU.mult))
                    for u in range(6, side.n):
                        side.dve_unit(dve, u)

            def qk(h, ps):
                for t in range(TT):
                    nc.tensor.matmul(ps[:, t * T:(t + 1) * T], Q[:, h, t * P:(t + 1) * P], KI[:, h // (NH // NKV), :], start=True, stop=False)
                    off = P * (1 - t)
                    mm = nc.tensor.matmul(ps[:, t * T:(t + 1) * T], exch[:, :], RBv[h // 8][:, h % 8, off:off + T], start=False, stop=True)
                return mm
            PB = S[8][:, 0:4, :].rearrange("p (b t) s -> p b t s", b=2)
            PT = S[8][:, 4:8, :].rearrange("p (b t) s -> p b t s", b=2)
            attention(NH, qk, lambda h, s: VN[:, s, (h // (NH // NKV)) * P:(h // (NH // NKV) + 1) * P], lambda h: Q[:, h, :], PB, PT, mask=MK,
                      side=G("sgu_v", H, "copy", natural=True, dst=flat(S[7], 0, DC).rearrange("p (t n) -> p t n", t=TT)))

        def sgu(ones_tri, X):
            U, VS, M5, S6, GB, WB = S[4], S[7], S[5], S[6], S[3], S[8]
            VN = VS[:, :, :].rearrange("p c t -> p (c t)").rearrange("p (t n) -> p t n", t=TT)
            gb = flat(GB, 0, DC).rearrange("p (k n) -> p k n", k=2)
            ws = flat(WB, 0, 8).rearrange("p (g t) -> p g t", g=16)
            bs = flat(WB, 8, 16).rearrange("p (g t) -> p g t", g=16)
            tri_t = ones_tri
            cub, sig, steps, ln_in, ln_out, mix, mixed, sq = stage_sems("cubes", "sigmoids", "dve_steps", "ln_in", "ln_sums", "mix_done", "mixed", "root")
            (loaded,) = stage_sems("loaded")
            side = Prod("gate_a", H, "sig", dst=S6)
            with nc.Block() as block:
                @block.sync
                def _(sp):
                    for k, name in enumerate(("sgu_g", "sgu_b")):
                        sp.dma_start(gb[:, k, :], ins[name].broadcast_to([P, D])).then_inc(loaded, 16)
                    sp.dma_start(ws, ins["sgu_w"]).then_inc(loaded, 16)
                    sp.dma_start(bs, ins["sgu_bias"].broadcast_to([P, D]).rearrange("p (g t) -> p g t", g=16)).then_inc(loaded, 16)
                    side.sp(sp)
                    sp.wait_ge(loaded, 64)

                @block.vector
                def _(dve):
                    link = linker(dve, steps)
                    v = nc.vector
                    for k, x in enumerate((VS, U)):
                        x, tm = x[:, :, :], M5[:, :, :]
                        link(v.tensor_tensor(tm, x, x, ALU.mult))
                        link(v.tensor_scalar(tm, tm, 0.044715, 1.0, ALU.mult, ALU.add))
                        v.tensor_tensor(tm, tm, x, ALU.mult).then_inc(cub, 1)
                        if k:
                            side.dve_unit(dve, 1)
                        dve.wait_ge(sig, k + 1)
                        v.tensor_tensor(x, x, tm, ALU.mult).then_inc(ln_in, 1)
                        dve.wait_ge(ln_in, k + 1)
                        side.dve_unit(dve, 2 * k)
                    dve.wait_ge(ln_out, 4)
                    mean, sums = small[:, 32:34], small[:, 34:36]
                    link(v.tensor_scalar(small[:, 32:36], small[:, 32:36], 1.0 / D, None, ALU.mult))
                    link(v.tensor_tensor(small[:, 36:38], mean, mean, ALU.mult))
                    link(v.tensor_tensor(sums, sums, small[:, 36:38], ALU.subtract))
                    v.tensor_scalar(sums, sums, EPS, None, ALU.add).then_inc(ln_in, 1)
                    dve.wait_ge(sq, 1)
                    link(v.reciprocal(sums, sums))
                    dve.wait_ge(loaded, 64)
                    for t in range(TT):
                        x = v.tensor_scalar(VN[:, t, :], VN[:, t, :], small[:, 32 + t:33 + t], small[:, 34 + t:35 + t], ALU.subtract, ALU.mult)
                    link(x)
                    gk = lambda k: gb[:, k:k + 1, :].broadcast_to([P, TT, D])
                    link(v.tensor_tensor(VN, VN, gk(0), ALU.mult))
                    side.dve_unit(dve, 3)
                    v.tensor_tensor(VN, VN, gk(1), ALU.add)
                    v.tensor_tensor(ws, ws, tri_t[:, :].rearrange("p (a t) -> p a t", a=1).broadcast_to([P, 16, P]), ALU.mult).then_inc(ln_in, 1)
                    for g in range(16):
                        if g and g % 4 == 0:
                            side.dve_unit(dve, 3 + g // 4)
                        dve.wait_ge(mix, g + 1)
                        b = bs[:, g:g + 1, :].broadcast_to([P, TT, P])
                        v.tensor_tensor(M5[:, g, :].rearrange("p (c t) -> p c t", c=TT), psa[:, g % 4, 0:T].rearrange("p (c t) -> p c t", c=TT), b, ALU.add).then_inc(mixed, 1)
                    side.dve_unit(dve, side.n - 1)

                @block.scalar
                def _(act):
                    def gate(k):
                        act.wait_ge(cub, k + 1)
                        nc.scalar.activation(M5[:, :, :], M5[:, :, :], ACT.Sigmoid, scale=float(2 * np.sqrt(2 / np.pi))).then_inc(sig, 1)
                    gate(0)
                    side.act_unit(act, 0)
                    act.wait_ge(ln_in, 1)
                    for t in range(TT):
                        junk = psa[:, :, :].rearrange("p b n -> p (b n)")
                        if t:
                            act.wait_ge(ln_out, 2)
                        nc.scalar.activation(junk, VN[:, t, :], ACT.Copy, accum_out=small[:, 32 + t:33 + t]).then_inc(ln_out, 1)
                        if t == 0:
                            side.act_unit(act, 1)
                        act.wait_ge(ln_out, 2 * t + 1)
                        nc.scalar.activation(junk, VN[:, t, :], ACT.Square, accum_out=small[:, 34 + t:35 + t]).then_inc(ln_out, 1)
                    gate(1)
                    side.act_unit(act, 2)
                    act.wait_ge(ln_in, 3)
                    nc.scalar.activation(small[:, 34:36], small[:, 34:36], ACT.Sqrt).then_inc(sq, 1)
                    for u in range(3, side.n):
                        side.act_unit(act, u)

                @block.tensor
                def _(pe):
                    for u in range(4):
                        side.pe_unit(pe, u)
                    pe.wait_ge(ln_in, 4)
                    for g in range(16):
                        if g >= 4:
                            pe.wait_ge(mixed, g - 3)
                        for c in range(TT):
                            mm = nc.tensor.matmul(psa[:, g % 4, c * P:(c + 1) * P], VN[:, c, g * P:(g + 1) * P], ws[:, g, :], start=True, stop=True)
                        mm.then_inc(mix, 1)
                        if g % 4 == 3:
                            side.pe_unit(pe, 4 + g // 4)
            (gated,) = stage_sems("gated")

            def gate_branches(dve):
                v.tensor_tensor(M5[:, :, :], M5[:, :, :], U[:, :, :], ALU.mult).then_inc(gated, 1)
                v.tensor_tensor(S[2][:, :, :], S[2][:, :, :], S6[:, :, :], ALU.mult).then_inc(gated, 1)
                dve.wait_ge(gated, 2)
            v = nc.vector
            products(G("gate_b", H, "gate_add", dst=S[2], src=M5, split=(arena_r[3], arena_r[2])), dve_pre=gate_branches)
            products(G("w_out_2", pair(3, 2), "resid", dst=X, needs_loads=True), loads=((spill_x, X[:, :, :]),))

        for n, part in ((1, block_1), (2, block_2), (3, block_3)):
            if n in blocks:
                with ExitStack() as own:
                    part(own)

        with nc.Block() as block:
            @block.sync
            def _(sp):
                sp.dma_start(out, arena[0][:, :, :]).then_inc(out_done, 16)
                sp.wait_ge(out_done, 16)


def to_units(w, cols=256):
    w = np.asarray(w)
    k, n = w.shape
    return np.ascontiguousarray(w.reshape(k // P, P, n // cols, cols).transpose(2, 1, 0, 3).reshape(n // cols, P, k // P * cols))


def channel_major(x):
    return np.ascontiguousarray(np.asarray(x).T.reshape(-1, P, x.shape[0]).transpose(1, 0, 2))


def per_channel(v):
    return np.asarray(v).reshape(-1, P).T


def layout(i):
    a = {}
    w = np.asarray(i["w_in"])[0]
    sizes = [("conv_a", 2048), ("conv_b", 2048), ("conv_z", 2048), ("gla_q", 1024), ("gla_k", 1024), ("gla_v", 2048),
             ("gla_z", 2048), ("alpha", 16), ("mem_q", 512), ("mem_z", 512), ("gate0", 2048), ("gate1", 2048), ("gate2", 2048)]
    at = 0
    for name, n in sizes:
        a[name] = to_units(w[:, at:at + n], min(n, 256))
        at += n
    a["gate2a"], a["gate2b"] = a["gate2"][:4], a.pop("gate2")[4:]
    a["conv_out"] = to_units(i["w_conv_out"][0])
    a["gla_out"] = to_units(i["w_gla_out"][0])
    a["mem_k"] = to_units(i["w_mem_kv"][0][:, :512])
    a["mem_v"] = to_units(i["w_mem_kv"][0][:, 512:])
    a["mem_out"] = to_units(i["w_mem_out"][0])
    a["w_out"] = to_units(i["w_out"][0])
    a["x_t"] = channel_major(np.asarray(i["x"])[0])
    a["mem_t"] = channel_major(np.asarray(i["mem"])[0])
    a["w_alpha2"] = np.ascontiguousarray(np.asarray(i["w_alpha2"])[0])
    cols = []
    for name, c in VECS:
        v = np.asarray(i[name])
        if name == "dw_w":
            cols.append(v[0].reshape(31, DC, P).transpose(2, 1, 0).reshape(P, -1))
        elif name == "rwkv_mu_3":
            cols.append(per_channel(v[:3072]))
            cols.append(np.concatenate([v[3072:].reshape(4, 96), np.zeros((4, 32), v.dtype)], 1).T)
        else:
            cols.append(per_channel(v))
    a["vecs"] = np.ascontiguousarray(np.concatenate(cols, 1))
    w = np.asarray(i["w_in_2"])[0]
    for name, lo, hi in (("sa_q", 0, 2048), ("sa_k", 2048, 2560), ("sa_v", 2560, 3072), ("sa_qi", 3072, 3584),
                         ("sgu_u", 3656, 5704), ("sgu_v", 5704, 7752), ("gate_a", 7752, 9800), ("gate_b", 9800, 11848)):
        a[name] = to_units(w[:, lo:hi])
    a["sa_ki"] = to_units(np.concatenate([w[:, 3584:3648]] * 2, 1), 128)
    a["sa_wi"] = to_units(w[:, 3648:3656], 8)
    a["w_out_2"] = to_units(i["w_out_2"][0])
    w1, w2 = np.asarray(i["w_ff1_2"])[0], np.asarray(i["w_ff2_2"])[0]
    for c in range(4):
        a[f"ff1_{c}"] = to_units(w1[:, c * D:(c + 1) * D])
        a[f"ff2_{c}"] = to_units(w2[c * D:(c + 1) * D])
    a["rel_bias"] = np.asarray(i["rel_bias_2"])
    a["sgu_g"], a["sgu_b"] = np.asarray(i["sgu_ln_g_2"]), np.asarray(i["sgu_ln_b_2"])
    a["sgu_w"] = np.ascontiguousarray(np.asarray(i["sgu_w_2"])[0].transpose(2, 0, 1))
    a["sgu_bias"] = np.asarray(i["sgu_b_2"]).reshape(1, D)
    w = np.asarray(i["w_in_3"])
    for name, lo, hi in (("rwkv_rk", 1088, 3136), ("rwkv_v", 3136, 4160), ("z_mla", 4544, 5568), ("z_rwkv", 5568, 6592),
                         ("gate_mla", 6592, 8640), ("gate_rwkv", 8640, 10688), ("mla_qkv_a", 0, 1024)):
        a[name] = to_units(w[:, lo:hi])
    a["rwkv_da"] = to_units(w[:, 4160:4544], 192)
    kr, krs = w[:, 1024:1088], np.concatenate([w[:, 1056:1088], w[:, 1024:1056]], 1)
    a["mla_k_rope"] = to_units(np.concatenate([kr, kr, krs, krs], 1))
    wq = np.asarray(i["mla_wq_b_3"]).reshape(512, 8, 192)
    a["mla_q_nope"] = to_units(wq[:, :, :128].reshape(512, 1024))
    a["mla_q_rope"] = to_units(np.concatenate([wq[:, :, 128:].reshape(512, 512),
                                               np.concatenate([wq[:, :, 160:], wq[:, :, 128:160]], 2).reshape(512, 512)], 1))
    wkv = np.asarray(i["mla_wkv_b_3"]).reshape(512, 8, 256)
    a["mla_k_nope"] = to_units(wkv[:, :, :128].reshape(512, 1024))
    a["mla_v"] = to_units(wkv[:, :, 128:].reshape(512, 1024))
    a["br_mla"] = to_units(i["w_br_mla_3"])
    a["br_rwkv"] = to_units(i["w_br_rwkv_3"])
    a["w_out_3"] = to_units(i["w_out_3"])
    a["rwkv_w2"] = np.ascontiguousarray(np.stack([np.asarray(i[n]) for n in ("rwkv_w2_f_3", "rwkv_w2_b_3", "rwkv_a2_f_3", "rwkv_a2_b_3")], 1)
                                        .reshape(96, DC, T))
    a["ones"] = np.ones((P, P), np.float32)
    a["ident"] = np.eye(P, dtype=np.float32)
    s, t = np.arange(P)[:, None], np.arange(P)[None, :]
    m = np.zeros((P, 8, P), np.float32)
    for l in range(GLA_LEVELS):
        m[:, l] = ((s >> (l + 1)) == (t >> (l + 1))) & (((s >> l) & 1) == 0) & (((t >> l) & 1) == 1)
    m[:, 7] = s == t
    a["level_masks"] = m
    a["exchange"] = (s + t == P - 1).astype(np.float32)
    a["causal_t"] = (s <= t).astype(np.float32)
    key, query = np.arange(T)[None, None, :], (np.arange(TT)[None, :, None] * P + np.arange(P)[:, None, None])
    a["causal"] = np.stack([key <= query, np.where(key <= query, 0, NEG)], 1).astype(np.float32)
    dist = np.maximum(T - 1 - np.arange(512), 0)
    large = 16 + (np.log(np.maximum(dist, 1).astype(np.float32) / np.float32(16)) / np.float32(np.log(8.0)) * np.float32(16)).astype(np.int32)
    bucket = np.where(dist < 16, dist, np.minimum(large, 31))
    a["bucket_onehot"] = (np.arange(32)[:, None] == bucket[None, :]).astype(np.float32)
    a["head_ones"] = ((s // 64) == (t // 64)).astype(np.float32)
    cm = np.zeros((P, 2, 2, P), np.float32)
    m_ts, m_st = np.zeros((P, 2, P), np.float32), np.zeros((P, 2, P), np.float32)
    same64, same16 = (s // 64) == (t // 64), (s // 16) == (t // 16)
    for d, strict in enumerate((s < t, s > t)):
        cm[:, d, 0], cm[:, d, 1] = same64 & strict, same64 & (strict | (s == t))
        m_st[:, d] = same16 & strict
        m_ts[:, d] = (same16 & strict).T
    a["chunk_masks"], a["mask16_ts"], a["mask16_st"] = cm, m_ts, m_st
    a["chunk_reset"] = np.tile((np.arange(T) % 64 != 0).astype(np.float32), (P, 1))
    freq = np.float32(10000.0) ** (-np.arange(0, 64, 2, dtype=np.float32) / np.float32(64))
    ang = (np.arange(T, dtype=np.float32)[:, None] * freq[None, :]).astype(np.float32).T
    rot = np.zeros((P, 2, T), np.float32)
    for r in range(4):
        rot[32 * r:32 * r + 32, 0] = np.cos(ang)
        rot[32 * r:32 * r + 32, 1] = np.sin(ang) * (1 if r % 2 else -1)
    a["rotary"] = rot
    return a


def kernel(**inputs):
    import concourse.bacc as bacc
    from concourse.bass_utils import run_bass_kernel_spmd
    nc = bacc.Bacc("TRN2", target_bir_lowering=False, num_devices=1)
    arrays = layout(inputs)
    ins = {k: nc.dram_tensor("in_" + k, v.shape, F32, kind="ExternalInput").ap() for k, v in arrays.items()}
    out = nc.dram_tensor("out", (P, DC, T), F32, kind="ExternalOutput").ap()
    build(nc, ins, out, BLOCKS)
    r = run_bass_kernel_spmd(nc, [{"in_" + k: v for k, v in arrays.items()}], core_ids=[0])
    y = r.results[0]["out"]
    return np.ascontiguousarray(y.transpose(1, 0, 2).reshape(D, T).T)[None]
```

```python
from contextlib import ExitStack

import numpy as np
import concourse.bass as bass
from concourse import mybir

F32 = mybir.dt.float32
F32R = mybir.dt.float32r
ACT = mybir.ActivationFunctionType
ALU = mybir.AluOpType
AX = mybir.AxisListType
P = 128
T = 256
TT = T // P
D = 2048
DC = D // P
EPS = 1e-6
GLA_HEADS, GLA_LEVELS = 4, 7
MEM_HEADS = 4
NEG = -1e30
BLOCKS = (1, 2, 3)
FF_ORDER = [(1, 0), (1, 1), (2, 0), (1, 2), (2, 1), (1, 3), (2, 2), (2, 3)]


def stream_plan(blocks):
    plan = []

    def add(name, units, kc=DC, cols=256):
        plan.append((name, units, kc, cols))
    if 1 in blocks:
        add("conv_a", 8); add("conv_b", 8); add("gla_q", 4); add("gla_k", 4); add("gla_v", 8)
        add("gate0", 8); add("conv_z", 8); add("alpha", 1, DC, 16); add("conv_out", 8)
        add("gate1", 8); add("gla_z", 8); add("gla_out", 8)
        add("gate2a", 4); add("mem_k", 2); add("mem_v", 2); add("mem_q", 2); add("gate2b", 4); add("mem_z", 2)
        add("mem_out", 8, 4); add("w_out", 8)
    if 2 in blocks:
        add("sa_q", 8); add("sa_k", 2); add("sa_v", 2); add("sa_qi", 2); add("sa_ki", 1, DC, 128); add("sa_wi", 1, DC, 8)
        add("sgu_u", 8); add("sgu_v", 8); add("gate_a", 8); add("gate_b", 8); add("w_out_2", 8)
        for part, c in FF_ORDER:
            add(f"ff{part}_{c}", 8)
    if 3 in blocks:
        add("rwkv_rk", 8); add("rwkv_v", 4); add("rwkv_da", 2, DC, 192)
        add("gate_rwkv", 8); add("z_rwkv", 4); add("mla_qkv_a", 4); add("mla_k_rope", 1); add("br_rwkv", 8, 8)
        add("mla_q_rope", 4, 4); add("mla_q_nope", 4, 4); add("mla_k_nope", 4, 4); add("mla_v", 4, 4)
        add("gate_mla", 8); add("z_mla", 4); add("br_mla", 8, 8); add("w_out_3", 8)
    return plan


VECS = [("ln_in_g", 16), ("mem_ln_g", 16), ("b_gate", 48), ("dw_b", 16), ("conv_ln_g", 16), ("conv_ln_b", 16),
        ("b_conv_out", 16), ("b_alpha", 8), ("gla_norm_g", 16), ("final_g", 16), ("dw_w", 16 * 31),
        ("g_pre_3", 16), ("mla_q_norm_3", 4), ("mla_kv_norm_3", 4), ("rwkv_mu_3", 28), ("rwkv_w0_f_3", 8), ("rwkv_w0_b_3", 8),
        ("rwkv_a0_f_3", 8), ("rwkv_a0_b_3", 8), ("rwkv_k_k_3", 8), ("rwkv_k_a_3", 8), ("rwkv_r_k_3", 8), ("rwkv_gn_g_3", 8),
        ("rwkv_gn_b_3", 8), ("g_post_3", 16), ("norm1_g_2", 16), ("norm2_g_2", 16), ("final_g_2", 16)]
VEC_AT = {}
_n = 0
for _name, _c in VECS:
    VEC_AT[_name] = _n
    _n += _c
NVEC = _n


class Stage:
    unit = 0
    gated = 0
    mids = 0
    made = 0
    splits = 0
    split_by = {}


def build(nc, ins, out, blocks):
    plan = stream_plan(blocks)
    units = [(name, u, kc, cols) for name, n, kc, cols in plan for u in range(n)]

    with ExitStack() as ctx:
        def sb(name, shape):
            return ctx.enter_context(nc.sbuf_tensor(name, shape, F32))

        def sem(name):
            return ctx.enter_context(nc.semaphore(name))

        def twin(name, shape):
            at = -(-nc.sbuf_base // 32) * 32
            return sb(name, shape), nc.alloc_sbuf_tensor_at(name + "_r", shape, F32R, offset=at)
        HALF = DC * 256 // 2
        ring, ring_lo = zip(*[twin(f"ring{i}", [P, HALF]) for i in range(4)])
        w_hi = [ctx.enter_context(nc.sbuf_tensor(f"w_hi{i}", [P, HALF // 2], F32R)) for i in range(2)]
        arena, arena_r = zip(*[twin(f"arena{i}", [P, DC, T]) for i in range(9)])
        Y, Tm = arena[2:4]
        tmp = [sb(f"act_tmp{i}", [P, 2, T]) for i in range(2)]
        tmp2 = [sb(f"dve_tmp{i}", [P, 2, T]) for i in range(2)]
        vecs = sb("vecs", [P, NVEC])
        ones = sb("ones", [P, P])
        ident = sb("ident", [P, P])
        stat = sb("stat", [P, 4, T])
        small = sb("small", [P, 64])
        psg = ctx.enter_context(nc.psum_tensor("ps_gemm", [P, 4, 512], F32))
        psa = ctx.enter_context(nc.psum_tensor("ps_aux", [P, 4, 512], F32))

        def vec(name, c):
            return vecs[:, bass.ds(c + VEC_AT[name], 1)]

        def pair(hi, lo, a=0, b=DC):
            return arena_r[hi][:, a:b, :], arena_r[lo][:, a:b, :]

        w_ready = [sem(f"w_ready{i}") for i in range(4)]
        hi_ready = sem("w_hi_ready")
        lo_ready = sem("w_lo_ready")
        hi_used = sem("w_hi_used")
        quarters_done = sem("quarters_done")
        split_in = sem("split_in")
        split_hi = sem("split_hi")
        split_done = sem("split_done")
        bank_free = sem("bank_free")
        act_ready = sem("act_ready")
        dve_mid = sem("dve_mid")
        const_in = sem("const_in")
        out_done = sem("out_done")
        st = Stage()

        def load_half(sp, g, h, src_index=None):
            name, u, kc, cols = units[g]
            ix = u if src_index is None else src_index
            n = kc * cols // 2
            slot = 2 * (g % 2) + h
            sp.dma_start(ring[slot][:, 0:n],
                         ins[name][bass.ds(ix, 1)].rearrange("a p n -> (a p) n")[:, h * n:(h + 1) * n]).then_inc(w_ready[slot], 16)

        def prefetch(sp, g0, n):
            g, end = g0 + 2, min(g0 + n + 2, len(units))
            while g < end:
                run = 1
                while g + run < end and units[g + run][0] == units[g][0]:
                    run += 1
                pairs = run // 2
                if pairs >= 2:
                    u0 = units[g][1]
                    with sp.Fori(0, pairs, 1) as i:
                        for j in range(2):
                            for h in range(2):
                                sp.wait_ge(quarters_done, 8 * i + (4 * (g + j) + 2 * h - 6))
                                load_half(sp, g + j, h, 2 * i + (u0 + j))
                    g += 2 * pairs
                    run -= 2 * pairs
                for _ in range(run):
                    for h in range(2):
                        sp.wait_ge(quarters_done, 4 * g + 2 * h - 6)
                        load_half(sp, g, h)
                    g += 1

        def quarter_of(g, q):
            n = units[g][2] * units[g][3] // 4
            return 2 * (g % 2) + q // 2, slice(q % 2 * n, (q % 2 + 1) * n), n, 4 * g + q

        def round_weights(act, i2, g, q):
            slot, part, size, n = quarter_of(g, q)
            act.wait_ge(w_ready[slot], 8 * i2 + 16 * (g // 2 + 1))
            if n >= 2:
                act.wait_ge(hi_used, 4 * i2 + (n - 1))
                act.wait_ge(lo_ready, 4 * i2 + (n - 1))
            nc.scalar.activation(w_hi[q % 2][:, 0:size], ring[slot][:, part], ACT.Copy).then_inc(hi_ready, 1)

        def rest_of_weights(dve, i2, g, q):
            slot, part, size, n = quarter_of(g, q)
            dve.wait_ge(hi_ready, 4 * i2 + (n + 1))
            nc.vector.tensor_tensor(ring_lo[slot][:, part], ring[slot][:, part], w_hi[q % 2][:, 0:size].bitcast(F32), ALU.subtract).then_inc(lo_ready, 1)

        def unit_work(eng, quarter, g0, i2, j, epilogue, split):
            more = g0 + j + 1 + (i2 if type(i2) is int else 0) < len(units)
            at, g = (0, g0 + j + i2) if type(i2) is int else (i2, g0 + j)
            quarter(eng, at, g, 2)
            quarter(eng, at, g, 3)
            if more:
                quarter(eng, at, g + 1, 0)
            epilogue(i2, j)
            if more:
                quarter(eng, at, g + 1, 1)
            split(i2, j)

        def all_units(eng, quarter, g0, n, epilogue, split):
            other = g0 + n >= len(units) or units[g0 + n][2:] != units[g0][2:]
            looped = n - 2 if other else n
            if looped >= 4:
                assert n % 2 == 0
                with eng.Fori(0, looped // 2, 1) as i:
                    for j in range(2):
                        unit_work(eng, quarter, g0, 2 * i, j, epilogue, split)
            else:
                looped = 0
            for u in range(looped, n):
                unit_work(eng, quarter, g0, u - u % 2, u % 2, epilogue, split)

        def pe_body(pe, g0, rhs, natural, fresh=None):
            name, _, kc, cols = units[g0]
            cw = 96 if cols == 192 else min(cols, P)
            r_hi, r_lo = rhs

            def body(i2, j):
                slot = (g0 + j) % 2
                pe.wait_ge(bank_free, i2 + (g0 + j + 1))
                for q in range(4):
                    ring_slot, part, _, n = quarter_of(g0 + j, q)
                    whi, wlo = w_hi[q % 2], ring_lo[ring_slot][:, part]

                    def sweep(passes, first, last):
                        for c in range(TT if natural else cols // cw):
                            bank = psg[:, 2 * slot + c, :]
                            for k in range(kc // 4):
                                kk = q * (kc // 4) + k
                                for m, (w, r) in enumerate(passes):
                                    start = first and q == 0 and k == 0 and m == 0
                                    stop = last and q == 3 and k == kc // 4 - 1
                                    if natural:
                                        mm = nc.tensor.matmul(bank[:, 0:cols], r[:, kk, c * P:(c + 1) * P],
                                                              w[:, k * cols:(k + 1) * cols], start=start, stop=stop)
                                    else:
                                        mm = nc.tensor.matmul(bank[0:cw, 0:T], w[:, k * cols + c * cw:k * cols + (c + 1) * cw],
                                                              r[:, kk, :], start=start, stop=stop)
                        return mm
                    if fresh is not None:
                        pe.wait_ge(split_done, fresh + q + 1)
                    pe.wait_ge(hi_ready, 4 * i2 + (n + 1))
                    sweep([(whi, r_hi), (whi, r_lo)], True, False).then_inc(hi_used, 1)
                    pe.wait_ge(lo_ready, 4 * i2 + (n + 1))
                    sweep([(wlo, r_hi)], False, True).then_inc(quarters_done, 1)
            return body

        ACT_ONLY = ("copy", "bias", "copy_small", "copy_narrow", "sig")
        DVE_ONLY = ("resid", "bias_mul", "mul_add")

        class Prod:

            def __init__(s, name, rhs, kind, dst=None, src=None, bias=None, scale=1.0, natural=False, at=0, after=False, rows=P, step=2, split=None, needs_loads=False, sums=None, also=None, before=None):
                s.g0 = st.unit
                assert units[s.g0][:2] == (name, 0), (units[s.g0], name)
                s.n = [x[1] for x in plan if x[0] == name][0]
                st.unit += s.n
                s.rhs, s.kind, s.dst, s.src, s.bias, s.scale, s.natural, s.at = rhs, kind, dst, src, bias, scale, natural, at
                s.after, s.rows, s.step = after, rows, step
                s.before = before
                s.also = also
                s.split, s.needs_loads = split, needs_loads
                s.split_before = st.split_by[after] if type(after) is str else st.splits
                s.act0, s.mid0 = st.gated, st.mids
                s.split0 = st.splits
                s.fresh = None
                if split:
                    st.splits += s.n
                st.split_by[name] = st.splits
                s.sums, s.sq0 = sums, norm_base[0]
                if sums is not None:
                    norm_base[0] += s.n
                    norm_base[1] += 1
                if kind not in ACT_ONLY + DVE_ONLY:
                    st.gated += s.n
                if kind in ("silu_mul", "gate_add", "mul_add"):
                    st.mids += s.n

            def sp(s, sp):
                prefetch(sp, s.g0, s.n)

            def pe(s, pe):
                if s.after:
                    pe.wait_ge(split_done, s.split_before)
                body = pe_body(pe, s.g0, s.rhs, s.natural)
                peeled = 2 if s.fresh is not None or s.sums is not None else 0
                looped = s.n - peeled if s.n >= 4 + peeled else 0
                if looped == 0:
                    peeled = s.n
                for u in range(peeled):
                    if u == 0 and s.fresh is not None:
                        pe_body(pe, s.g0, s.rhs, s.natural, s.fresh)(0, 0)
                    else:
                        body(u - u % 2, u % 2)
                if s.sums is not None:
                    s.sum_squares(pe, 0, 0, first=True)
                if looped:
                    assert looped % 2 == 0
                    with pe.Fori(peeled // 2, s.n // 2, 1) as i:
                        for j in range(2):
                            body(2 * i, j)
                            if s.sums is not None:
                                s.sum_squares(pe, 2 * i, j - 1)
                if s.sums is not None:
                    s.sum_squares(pe, 0, s.n - 1, last=True).then_inc(sums_done, 1)

            def sum_squares(s, pe, i2, j, first=False, last=False):
                pe.wait_ge(sq_ready, i2 + (s.sq0 + j + 1))
                for c in range(2):
                    mm = nc.tensor.matmul(psa[:, 0, 0:T], ones[:, :], s.sums[:, bass.ds(2 * i2 + (2 * j + c), 1), :].rearrange("p a t -> p (a t)"),
                                          start=first and c == 0, stop=last and c == 1)
                return mm

            def chunks(s, buf, i2, j):
                return buf[0:s.rows, bass.ds(s.step * i2 + (s.step * j + s.at), 2), :]

            def views(s, i2, j):
                slot = (s.g0 + j) % 2
                ps = psg[0:s.rows, 2 * slot:2 * slot + 2, 0:T]
                if s.kind == "copy_narrow":
                    return slot, psg[:, 2 * slot:2 * slot + 2, 0:s.dst.shape[2]], s.dst
                if s.natural:
                    d = s.dst[:, :, bass.ds(i2 * 256 + (j * 256 + s.at), 256)]
                elif s.kind != "copy_small":
                    d = s.chunks(s.dst, i2, j)
                else:
                    d = None
                return slot, ps, d

            def act(s, act):
                all_units(act, round_weights, s.g0, s.n, lambda i2, j: s.act_epilogue(act, i2, j), lambda i2, j: s.act_split(act, i2, j))

            def act_part(s, act, u, part):
                s.part(round_weights, s.act_epilogue, act, u, part)

            def dve_part(s, dve, u, part):
                s.part(rest_of_weights, s.dve_epilogue, dve, u, part)

            def part(s, quarter, epilogue, eng, u, part):
                g = s.g0 + u
                if part == 3:
                    epilogue(eng, u - u % 2, u % 2)
                if part < 2:
                    quarter(eng, 0, g, part + 2)
                elif g + 1 < len(units):
                    quarter(eng, 0, g + 1, part - 2)

            def act_unit(s, act, u):
                for part in range(4):
                    s.act_part(act, u, part)

            def dve_unit(s, dve, u):
                for part in range(4):
                    s.dve_part(dve, u, part)

            def pe_unit(s, pe, u):
                pe_body(pe, s.g0, s.rhs, s.natural)(u - u % 2, u % 2)

            def act_split(s, act, i2, j):
                if s.split:
                    act.wait_ge(bank_free, i2 + (s.g0 + j + 3))
                    nc.scalar.activation(s.chunks(s.split[0], i2, j), s.chunks(s.dst, i2, j), ACT.Copy).then_inc(split_hi, 1)

                if s.sums is not None:
                    act.wait_ge(bank_free, i2 + (s.g0 + j + 3))
                    nc.scalar.activation(s.chunks(s.sums, i2, j), s.chunks(s.dst, i2, j), ACT.Square).then_inc(sq_ready, 1)

            def dve_split(s, dve, i2, j):
                if s.split:
                    dve.wait_ge(split_hi, i2 + (s.split0 + j + 1))
                    hi, lo = (s.chunks(x, i2, j) for x in s.split)
                    nc.vector.tensor_tensor(lo, s.chunks(s.dst, i2, j), hi.bitcast(F32), ALU.subtract).then_inc(split_done, 1)

            def act_epilogue(s, act, i2, j):
                if s.kind in DVE_ONLY:
                    return
                slot, ps, d = s.views(i2, j)
                act.wait_ge(quarters_done, 4 * i2 + (4 * (s.g0 + j) + 4))
                if s.kind in ("copy", "copy_narrow"):
                    nc.scalar.activation(d, ps, ACT.Copy, scale=s.scale).then_inc(bank_free, 1)
                    return
                if s.kind == "copy_small":
                    nc.scalar.activation(s.dst, psg[0:s.dst.shape[0], 2 * slot, 0:T], ACT.Copy).then_inc(bank_free, 1)
                    return
                if s.kind in ("sig", "bias"):
                    for c in range(2):
                        o = s.dst[:, bass.ds(2 * i2 + (2 * j + c + s.at), 1), :].rearrange("p a t -> p (a t)")
                        a = nc.scalar.activation(o, ps[:, c, :], ACT.Sigmoid if s.kind == "sig" else ACT.Identity,
                                                 bias=vec(s.bias[0], 2 * i2 + (2 * j + c + s.bias[1])) if s.bias else 0.0)
                    a.then_inc(bank_free, 1)
                    return
                if s.also is not None:
                    nc.scalar.activation(s.chunks(s.also, i2, j), s.chunks(s.also, i2, j), ACT.Sigmoid)
                act.wait_ge(bank_free, i2 + (s.g0 + j + 1))
                if s.kind in ("gate_set", "gate_add") and s.bias:
                    for c in range(2):
                        a = nc.scalar.activation(tmp[slot][:, c, :], ps[:, c, :], ACT.Sigmoid,
                                                 bias=vec(s.bias[0], 2 * i2 + (2 * j + c + s.bias[1])))
                else:
                    f = {"sig_mul": ACT.Sigmoid, "silu": ACT.Sigmoid, "silu_mul": ACT.Sigmoid, "gate_set": ACT.Sigmoid, "gate_add": ACT.Sigmoid, "relu2": ACT.Relu}[s.kind]
                    a = nc.scalar.activation(tmp[slot][:, :, :], ps, f)
                a.then_inc(act_ready, 1)

            def dve(s, dve):
                if s.kind not in ACT_ONLY:
                    dve.wait_ge(bank_free, s.g0 + 2)
                all_units(dve, rest_of_weights, s.g0, s.n, lambda i2, j: s.dve_epilogue(dve, i2, j), lambda i2, j: s.dve_split(dve, i2, j))

            def dve_epilogue(s, dve, i2, j):
                if s.kind in ACT_ONLY:
                    return
                slot, ps, d = s.views(i2, j)
                if s.kind == "resid":
                    dve.wait_ge(quarters_done, 4 * i2 + (4 * (s.g0 + j) + 4))
                    nc.vector.tensor_tensor(d, ps, d, ALU.add).then_inc(bank_free, 1)
                    return
                if s.kind == "bias_mul":
                    dve.wait_ge(quarters_done, 4 * i2 + (4 * (s.g0 + j) + 4))
                    for c in range(2):
                        o = s.dst[:, bass.ds(2 * i2 + (2 * j + c), 1), :].rearrange("p a t -> p (a t)")
                        a = nc.vector.scalar_tensor_tensor(out=o, in0=ps[:, c, :], scalar=vec(s.bias, 2 * i2 + (2 * j + c)) if s.bias else 0.0,
                                                           in1=o, op0=ALU.add, op1=ALU.mult)
                    a.then_inc(bank_free, 1)
                    return
                if s.kind == "mul_add":
                    dve.wait_ge(quarters_done, 4 * i2 + (4 * (s.g0 + j) + 4))
                    nc.vector.tensor_tensor(tmp2[slot][:, :, :], ps, s.src[:, bass.ds(2 * i2 + 2 * j, 2), :], ALU.mult).then_inc(dve_mid, 1)
                    dve.wait_ge(dve_mid, i2 + (s.mid0 + j + 1))
                    nc.vector.tensor_tensor(d, tmp2[slot][:, :, :], d, ALU.add).then_inc(bank_free, 1)
                    return
                dve.wait_ge(act_ready, i2 + (s.act0 + j + 1))
                t = tmp[slot][:, :, :]
                if s.kind == "sig_mul":
                    last = nc.vector.tensor_tensor(d, t, d, ALU.mult)
                elif s.kind == "silu":
                    last = nc.vector.tensor_tensor(d, ps, t, ALU.mult)
                elif s.kind == "relu2":
                    last = nc.vector.tensor_tensor(d, t, t, ALU.mult)
                elif s.kind == "gate_set":
                    last = nc.vector.tensor_tensor(d, t, s.src[:, bass.ds(2 * i2 + 2 * j, 2), :], ALU.mult)
                else:
                    if s.kind == "silu_mul":
                        a = nc.vector.tensor_tensor(tmp2[slot][:, :, :], ps, t, ALU.mult)
                    else:
                        a = nc.vector.tensor_tensor(tmp2[slot][:, :, :], t, s.src[:, bass.ds(2 * i2 + 2 * j, 2), :], ALU.mult)
                    a.then_inc(dve_mid, 1)
                    dve.wait_ge(dve_mid, i2 + (s.mid0 + j + 1))
                    last = nc.vector.tensor_tensor(d, tmp2[slot][:, :, :], d,
                                                   ALU.mult if s.kind == "silu_mul" else ALU.add)
                last.then_inc(bank_free, 1)

        class Run:

            def __init__(s, *args, dve_body=None, loads=(), pre=None, dve_pre=None):
                s.prods = [Prod(*a[0], **a[1]) for a in args]
                s.dve_body, s.loads, s.pre, s.dve_pre = dve_body, loads, pre, dve_pre
                if loads:
                    (s.loaded,) = stage_sems("loaded")

            def sp(s, sp):
                for src, dst in s.loads:
                    sp.dma_start(dst, ins[src] if type(src) is str else src).then_inc(s.loaded, 16)
                for p in s.prods:
                    p.sp(sp)
                if s.loads:
                    sp.wait_ge(s.loaded, 16 * len(s.loads))

            def pe(s, pe):
                for p in s.prods:
                    p.pe(pe)

            def act(s, act):
                if s.pre:
                    s.pre.act(act)
                for p in s.prods:
                    p.act(act)

            def dve(s, dve):
                if s.pre:
                    s.pre.dve(dve)
                if s.dve_pre:
                    s.dve_pre(dve)
                if s.dve_body:
                    s.dve_body(dve, s.prods)
                    return
                for p in s.prods:
                    if p.needs_loads:
                        dve.wait_ge(s.loaded, 16 * len(s.loads))
                    if p.before:
                        dve.wait_ge(bank_free, p.g0 + 2)
                        p.before(dve)
                    p.dve(dve)

        def products(*args, **kw):
            run = Run(*args, **kw)
            with nc.Block() as block:
                @block.sync
                def _(sp):
                    run.sp(sp)

                @block.tensor
                def _(pe):
                    run.pe(pe)

                @block.scalar
                def _(act):
                    run.act(act)

                @block.vector
                def _(dve):
                    run.dve(dve)

        class Split:

            def __init__(s, groups, make, raw, hi, lo):
                s.groups, s.make, s.raw, s.hi, s.lo = groups, make, raw, hi, lo
                s.made0, s.split0 = st.made, st.splits
                st.made += groups
                st.splits += groups

            def act(s, act):
                for q in range(s.groups):
                    act.wait_ge(split_in, s.made0 + q + 1)
                    nc.scalar.activation(s.hi(q), s.raw(q), ACT.Copy).then_inc(split_hi, 1)

            def dve(s, dve):
                s.make(dve, 0).then_inc(split_in, 1)
                for q in range(s.groups):
                    if q + 1 < s.groups:
                        s.make(dve, q + 1).then_inc(split_in, 1)
                    dve.wait_ge(split_hi, s.split0 + q + 1)
                    nc.vector.tensor_tensor(s.lo(q), s.raw(q), s.hi(q).bitcast(F32), ALU.subtract).then_inc(split_done, 1)

        def G(*a, **k):
            return (a, k)

        nstage = [0]

        def stage_sems(*names):
            nstage[0] += 1
            return [sem(f"s{nstage[0]}_{n}") for n in names]

        def linker(eng, chain):
            count = [0]

            def link(x):
                count[0] += 1
                x.then_inc(chain, 1)
                eng.wait_ge(chain, count[0])
            return link

        def vcol(name, c):
            return vecs[:, VEC_AT[name] + c:VEC_AT[name] + c + 1]

        def flat(buf, a, b):
            return buf[:, a:b, :].rearrange("p c t -> p (c t)")

        sq_ready, sums_done, root_in, root_done, chain, normed = [
            sem("norm_" + n) for n in ("sq_ready", "sums_done", "root_in", "root_done", "dve_chain", "normed")]
        norm_base = [0] * 6

        def gained(dst, src, gain, c):
            return nc.vector.scalar_tensor_tensor(out=dst[:, c, :], in0=src[:, c, :], scalar=vcol(gain, c), in1=stat[:, 3, :], op0=ALU.mult, op1=ALU.mult)

        def rms(dve, link, sums, roots, n, ps=None, out=None):
            ps, out = (psa[:, 0, 0:T], stat[:, 3, :]) if ps is None else (ps, out)
            dve.wait_ge(sums_done, sums)
            nc.vector.tensor_scalar(out, ps, 1.0 / (n * P), EPS, ALU.mult, ALU.add).then_inc(root_in, 1)
            dve.wait_ge(root_done, roots)
            link(nc.vector.reciprocal(out, out))

        def root(act, n, out=None):
            out = stat[:, 3, :] if out is None else out
            act.wait_ge(root_in, n)
            nc.scalar.activation(out, out, ACT.Sqrt).then_inc(root_done, 1)

        def make_split(src, dst, n, gain, split, pick=lambda c: stat[:, 3, :]):
            def make(dve, q):
                for c in range(q * n // 4, (q + 1) * n // 4):
                    x = nc.vector.scalar_tensor_tensor(out=dst[:, c, :], in0=src[:, c, :], scalar=vcol(gain, c), in1=pick(c), op0=ALU.mult, op1=ALU.mult)
                return x
            part = lambda buf: (lambda q: buf[:, q * n // 4:(q + 1) * n // 4, :])
            return Split(4, make, part(dst), part(split[0]), part(split[1]))

        def counts(*more):
            for i, m in enumerate(more):
                norm_base[i] += m

        def chain_linker(dve, base, count):
            def link(x):
                count[0] += 1
                x.then_inc(chain, 1)
                dve.wait_ge(chain, base + count[0])
            return link

        def norm(src, dst, n, gain, scratch, groups=1, side=None, split=None, summed=False, then=(), **kw):
            b_sq, b_sums, b_in, b_root, b_chain, _ = norm_base
            tot = n * groups
            count = [0]
            first = st.unit == 0
            side = Prod(*side[0], **side[1]) if side else None
            inv = lambda c: stat[:, c // n if groups > 1 else 3, :]
            ps = psa[:, 0:2, :].rearrange("p b (k t) -> p (b k) t", k=2)[:, 0:groups, :] if groups > 1 else psa[:, 0, 0:T]
            out = stat[:, 0:groups, :] if groups > 1 else stat[:, 3, :]
            parts = make_split(src, dst, tot, gain, split, inv) if split else None
            run = Run(*then, **kw)
            if split and not side and then and groups == 1:
                run.prods[0].fresh = parts.split0
            pieces = 4 if not summed else 0
            x_in = stage_sems(*[f"x_in{q}" for q in range(4)]) if first else None
            with nc.Block() as block:
                @block.sync
                def _(sp):
                    if first:
                        for q in range(4):
                            sp.dma_start(src[:, 4 * q:4 * q + 4, :], ins["x_t"][:, 4 * q:4 * q + 4, :]).then_inc(x_in[q], 16)
                            if q == 0:
                                sp.dma_start(ones[:, :], ins["ones"]).then_inc(const_in, 16)
                        for h in range(2):
                            load_half(sp, 0, h)
                        sp.dma_start(vecs[:, :], ins["vecs"]).then_inc(const_in, 16)
                        sp.dma_start(ident[:, :], ins["ident"]).then_inc(const_in, 16)
                        for h in range(2):
                            load_half(sp, 1, h)
                        sp.wait_ge(const_in, 48)
                    if side:
                        side.sp(sp)
                    run.sp(sp)

                @block.scalar
                def _(act):
                    if first:
                        act.sem_inc(bank_free, 2)
                    for q in range(pieces):
                        if first:
                            act.wait_ge(x_in[q], 16)
                        a, b = q * tot // 4, (q + 1) * tot // 4
                        nc.scalar.activation(scratch[:, a:b, :], src[:, a:b, :], ACT.Square).then_inc(sq_ready, 1)
                    if first:
                        for q in range(2):
                            round_weights(act, 0, 0, q)
                    if side:
                        side.act_unit(act, 0)
                    root(act, b_in + 1, out)
                    if split:
                        parts.act(act)
                    for u in range(1, side.n if side else 0):
                        side.act_unit(act, u)
                    run.act(act)

                @block.tensor
                def _(pe):
                    if side:
                        side.pe_unit(pe, 0)
                    if first:
                        pe.wait_ge(const_in, 48)
                    for c in range(tot if pieces else 0):
                        pe.wait_ge(sq_ready, b_sq + c * 4 // tot + 1)
                        g = c // n
                        mm = nc.tensor.matmul(psa[:, g // 2, g % 2 * T:g % 2 * T + T], ones[:, :], scratch[:, c, :], start=c % n == 0, stop=c % n == n - 1)
                    if pieces:
                        mm.then_inc(sums_done, 1)
                    for u in range(1, side.n if side else 0):
                        side.pe_unit(pe, u)
                    run.pe(pe)

                @block.vector
                def _(dve):
                    link = chain_linker(dve, b_chain, count)
                    if side:
                        side.dve_unit(dve, 0)
                    if first:
                        for q in range(2):
                            rest_of_weights(dve, 0, 0, q)
                        dve.wait_ge(const_in, 48)
                    rms(dve, link, b_sums + (1 if pieces else 0), b_root + 1, n, ps, out)
                    if split:
                        parts.dve(dve)
                    else:
                        for c in range(tot):
                            x = nc.vector.scalar_tensor_tensor(out=dst[:, c, :], in0=src[:, c, :], scalar=vcol(gain, c), in1=inv(c), op0=ALU.mult, op1=ALU.mult)
                        link(x)
                    for u in range(1, side.n if side else 0):
                        side.dve_unit(dve, u)
                    run.dve(dve)
            counts(pieces, 1 if pieces else 0, 1, 1, count[0])

        def layer_norm_silu(buf, gain, bias, scratch, side, then, **kw):
            b_sq, b_sums, b_in, b_root, b_chain, b_norm = norm_base
            count = [0]
            side = Prod(*side[0], **side[1])
            run = Run(*then, **kw)
            assert side.n == DC // 2
            mean, var, sq = stat[:, 0, :], stat[:, 3, :], stat[:, 1, :]
            two = lambda ap: ap.rearrange("p (a t) -> p a t", a=1).broadcast_to([P, 2, T])
            with nc.Block() as block:
                @block.sync
                def _(sp):
                    side.sp(sp)
                    run.sp(sp)

                @block.scalar
                def _(act):
                    for q in range(4):
                        nc.scalar.activation(scratch[:, 4 * q:4 * q + 4, :], buf[:, 4 * q:4 * q + 4, :], ACT.Square).then_inc(sq_ready, 1)
                    side.act_part(act, 0, 0)
                    side.act_part(act, 0, 1)
                    side.act_part(act, 0, 2)
                    side.act_part(act, 0, 3)
                    root(act, b_in + 1)
                    for u in range(1, side.n):
                        side.act_part(act, u, 0)
                        act.wait_ge(normed, b_norm + u)
                        nc.scalar.activation(scratch[:, 2 * u - 2:2 * u, :], buf[:, 2 * u - 2:2 * u, :], ACT.Sigmoid).then_inc(root_done, 1)
                        for part in (1, 2, 3):
                            side.act_part(act, u, part)
                    act.wait_ge(normed, b_norm + side.n)
                    nc.scalar.activation(scratch[:, 14:16, :], buf[:, 14:16, :], ACT.Sigmoid).then_inc(root_done, 1)
                    run.act(act)

                @block.tensor
                def _(pe):
                    for c in range(DC):
                        nc.tensor.matmul(psa[:, 1, 0:T], ones[:, :], buf[:, c, :], start=c == 0, stop=c == DC - 1)
                    side.pe_unit(pe, 0)
                    for c in range(DC):
                        pe.wait_ge(sq_ready, b_sq + c // 4 + 1)
                        mm = nc.tensor.matmul(psa[:, 0, 0:T], ones[:, :], scratch[:, c, :], start=c == 0, stop=c == DC - 1)
                    mm.then_inc(sums_done, 1)
                    for u in range(1, side.n):
                        side.pe_unit(pe, u)
                    run.pe(pe)

                @block.vector
                def _(dve):
                    link = chain_linker(dve, b_chain, count)
                    v = nc.vector
                    side.dve_unit(dve, 0)
                    dve.wait_ge(sums_done, b_sums + 1)
                    link(v.tensor_scalar(mean, psa[:, 1, 0:T], 1.0 / D, None, ALU.mult))
                    link(v.tensor_tensor(sq, mean, mean, ALU.mult))
                    link(v.tensor_scalar(var, psa[:, 0, 0:T], 1.0 / D, EPS, ALU.mult, ALU.add))
                    v.tensor_tensor(var, var, sq, ALU.subtract).then_inc(root_in, 1)
                    dve.wait_ge(root_done, b_root + 1)
                    link(v.reciprocal(var, var))
                    link(v.tensor_tensor(mean, mean, var, ALU.mult))
                    for u in range(side.n):
                        x = buf[:, 2 * u:2 * u + 2, :]
                        link(v.tensor_tensor(x, x, two(var), ALU.mult))
                        if u + 1 < side.n:
                            side.dve_part(dve, u + 1, 0)
                        link(v.tensor_tensor(x, x, two(mean), ALU.subtract))
                        for c in (2 * u, 2 * u + 1):
                            y = v.tensor_scalar(buf[:, c, :], buf[:, c, :], vcol(gain, c), vcol(bias, c), ALU.mult, ALU.add)
                        y.then_inc(normed, 1)
                        if u + 1 < side.n:
                            for part in (1, 2, 3):
                                side.dve_part(dve, u + 1, part)
                        dve.wait_ge(root_done, b_root + u + 2)
                        y = v.tensor_tensor(x, x, scratch[:, 2 * u:2 * u + 2, :], ALU.mult)
                    link(y)
                    run.dve(dve)
            counts(4, 1, 1, 1 + side.n, count[0], side.n)

        def norm_twice(src, gain1, mid, spill, dst, gain2, scratch, split, then, **kw):
            _, b_sums, b_in, b_root, b_chain, b_norm = norm_base
            b_sq = norm_base[0]
            count = [0]
            parts = make_split(mid, dst, DC, gain2, split)
            run = Run(*then, **kw)
            run.prods[0].fresh = parts.split0
            (spilled,) = stage_sems("spilled")
            with nc.Block() as block:
                @block.sync
                def _(sp):
                    for q in range(4):
                        sp.wait_ge(normed, b_norm + q + 1)
                        sp.dma_start(spill[:, 4 * q:4 * q + 4, :], mid[:, 4 * q:4 * q + 4, :]).then_inc(spilled, 16)
                    run.sp(sp)
                    sp.wait_ge(spilled, 64)

                @block.scalar
                def _(act):
                    root(act, b_in + 1)
                    for q in range(4):
                        act.wait_ge(normed, b_norm + q + 1)
                        nc.scalar.activation(scratch[:, 4 * q:4 * q + 4, :], mid[:, 4 * q:4 * q + 4, :], ACT.Square).then_inc(sq_ready, 1)
                    root(act, b_in + 2)
                    parts.act(act)
                    run.act(act)

                @block.tensor
                def _(pe):
                    for c in range(DC):
                        pe.wait_ge(sq_ready, b_sq + c // 4 + 1)
                        mm = nc.tensor.matmul(psa[:, 1, 0:T], ones[:, :], scratch[:, c, :], start=c == 0, stop=c == DC - 1)
                    mm.then_inc(sums_done, 1)
                    run.pe(pe)

                @block.vector
                def _(dve):
                    link = chain_linker(dve, b_chain, count)
                    rms(dve, link, b_sums, b_root + 1, DC)
                    for c in range(DC):
                        x = gained(mid, src, gain1, c)
                        if c % 4 == 3:
                            x.then_inc(normed, 1)
                    rms(dve, link, b_sums + 1, b_root + 2, DC, psa[:, 1, 0:T], stat[:, 3, :])
                    parts.dve(dve)
                    run.dve(dve)
            counts(4, 1, 2, 2, count[0], 4)

        def last_norm(src, gain, dst, add=None):
            _, b_sums, b_in, b_root, b_chain, b_norm = norm_base
            count = [0]
            with nc.Block() as block:
                @block.sync
                def _(sp):
                    for q in range(4):
                        sp.wait_ge(normed, b_norm + q + 1)
                        sp.dma_start(out[:, 4 * q:4 * q + 4, :], dst[:, 4 * q:4 * q + 4, :]).then_inc(out_done, 16)
                    sp.wait_ge(out_done, 64)

                @block.scalar
                def _(act):
                    root(act, b_in + 1)

                @block.vector
                def _(dve):
                    link = chain_linker(dve, b_chain, count)
                    rms(dve, link, b_sums, b_root + 1, DC)
                    for q in range(4):
                        for c in range(4 * q, 4 * q + 4):
                            x = gained(dst, src, gain, c)
                        if add is not None:
                            link(x)
                            part = dst[:, 4 * q:4 * q + 4, :]
                            x = nc.vector.tensor_tensor(part, part, add[:, 4 * q:4 * q + 4, :], ALU.add)
                        x.then_inc(normed, 1)

        def attention(nh, qk, v, o, pbuf, ptbuf, mask=None, side=None):
            (qk_done, mx_done, exp_done, p_done, chain, tr_done, trc_done, o_done, oc_done) = stage_sems(
                "qk_done", "mx_done", "exp_done", "p_done", "dve_chain", "tr_done", "trc_done", "o_done", "oc_done")
            side = Prod(*side[0], **side[1]) if side else None
            m = side.n if side else 0
            share = [range(h * m // nh, (h + 1) * m // nh) for h in range(nh)]
            assert m <= nh
            with nc.Block() as block:
                @block.sync
                def _(sp):
                    if side:
                        side.sp(sp)

                @block.tensor
                def _(pe):
                    def scores(h):
                        if h >= 2:
                            pe.wait_ge(exp_done, h - 1)
                        mm = qk(h, psa[:, h % 2, :])
                        mm.then_inc(qk_done, 1)
                    scores(0)
                    for h in range(nh):
                        if h + 1 < nh:
                            scores(h + 1)
                        for u in share[h]:
                            side.pe_unit(pe, u)
                        pe.wait_ge(p_done, h + 1)
                        if h:
                            pe.wait_ge(trc_done, h)
                        for s in range(TT):
                            for t in range(TT):
                                mm = nc.tensor.transpose(psa[:, 2, s * T + t * P:s * T + (t + 1) * P],
                                                         pbuf[:, h % 2, t, s * P:(s + 1) * P], ident[:, :])
                        mm.then_inc(tr_done, 1)
                        pe.wait_ge(trc_done, h + 1)
                        if h:
                            pe.wait_ge(oc_done, h)
                        for s in range(TT):
                            mm = nc.tensor.matmul(psa[:, 3, 0:T], v(h, s), ptbuf[:, h % 2, s, :], start=s == 0, stop=s == TT - 1)
                        mm.then_inc(o_done, 1)

                @block.vector
                def _(dve):
                    count = [0]

                    def link(x):
                        count[0] += 1
                        x.then_inc(chain, 1)
                        dve.wait_ge(chain, count[0])

                    def maximum(h):
                        dve.wait_ge(qk_done, h + 1)
                        ps = psa[:, h % 2, :].rearrange("p (t s) -> p t s", t=TT)
                        src = ps
                        if mask is not None:
                            if h >= 2:
                                dve.wait_ge(tr_done, h - 1)
                            link(nc.vector.tensor_tensor(pbuf[:, h % 2, :, :], ps, mask, ALU.add))
                            src = pbuf[:, h % 2, :, :]
                        nc.vector.tensor_reduce(small[:, 4 * (h % 2):4 * (h % 2) + 2], src, AX.X, ALU.max, negate=True).then_inc(mx_done, 1)
                    maximum(0)
                    for h in range(nh):
                        if h + 1 < nh:
                            maximum(h + 1)
                        b = 8 + 4 * (h % 2)
                        dve.wait_ge(exp_done, h + 1)
                        link(nc.vector.reciprocal(small[:, b + 2:b + 4], small[:, b:b + 2]))
                        for t in range(TT):
                            x = nc.vector.tensor_scalar(pbuf[:, h % 2, t, :], pbuf[:, h % 2, t, :], small[:, b + 2 + t:b + 3 + t], None, ALU.mult)
                        x.then_inc(p_done, 1)
                        for u in share[h]:
                            side.dve_unit(dve, u)
                        dve.wait_ge(o_done, h + 1)
                        nc.vector.tensor_copy(o(h), psa[:, 3, 0:T]).then_inc(oc_done, 1)

                @block.scalar
                def _(act):
                    def exps(h):
                        act.wait_ge(mx_done, h + 1)
                        if h >= 2:
                            act.wait_ge(tr_done, h - 1)
                        for t in range(TT):
                            src = psa[:, h % 2, t * T:(t + 1) * T] if mask is None else pbuf[:, h % 2, t, :]
                            x = nc.scalar.activation(pbuf[:, h % 2, t, :], src, ACT.Exp, bias=small[:, 4 * (h % 2) + t:4 * (h % 2) + t + 1],
                                                     accum_out=small[:, 8 + 4 * (h % 2) + t:9 + 4 * (h % 2) + t])
                        x.then_inc(exp_done, 1)
                    exps(0)
                    for h in range(nh):
                        if h + 1 < nh:
                            exps(h + 1)
                        for u in share[h]:
                            side.act_unit(act, u)
                        act.wait_ge(tr_done, h + 1)
                        if h >= 2:
                            act.wait_ge(o_done, h - 1)
                        nc.scalar.activation(ptbuf[:, h % 2, :, :], psa[:, 2, :].rearrange("p (s t) -> p s t", s=TT), ACT.Copy).then_inc(trc_done, 1)

        S = arena
        H = pair(1, 0)
        state = {"x": ins["x_t"]}

        def enter(gain, then, **kw):
            split = (arena_r[1], arena_r[0])
            if st.unit == 0:
                norm(S[0], S[0], DC, gain, S[4], split=split, then=then, **kw)
            else:
                src, gain1 = state["left"]
                state["x"] = nc.dram_tensor(f"residual_{gain}", (P, DC, T), F32, kind="Internal").ap()
                norm_twice(src, gain1, S[8], state["x"], S[0], gain, S[4], split, then, **kw)

        def block_1(own):
            def sb(name, shape):
                return own.enter_context(nc.sbuf_tensor(name, shape, F32))
            masks = sb("level_masks", [P, 8, P])
            stt = sb("gla_scores", [P, 2, T])
            alpha_t, wal2 = S[4][0:16, 8, :], S[4][0:16, 12:16, :].rearrange("p c t -> p (c t)")
            U, CV = S[3], S[5]

            (conv_step,) = stage_sems("conv_step")
            K31 = 31

            def taps(dve, group, a, b):
                def ch(buf, cc, lo, hi):
                    return buf[:, bass.ds(4 * group + cc, 1), lo:hi].rearrange("p a t -> p (a t)")
                for n in range(a, b):
                    lag, cc = n // 4, n % 4
                    w = vecs[:, bass.ds(group * (4 * K31) + (VEC_AT["dw_w"] + cc * K31 + K31 - 1 - lag), 1)]
                    if lag == 0:
                        x = nc.vector.tensor_scalar(ch(CV, cc, 0, T), ch(U, cc, 0, T), w, vec("dw_b", 4 * group + cc), ALU.mult, ALU.add)
                    else:
                        dve.wait_ge(conv_step, group * (4 * K31) + (4 * (lag - 1) + cc + 1))
                        x = nc.vector.scalar_tensor_tensor(out=ch(CV, cc, lag, T), in0=ch(U, cc, 0, T - lag), scalar=w,
                                                           in1=ch(CV, cc, lag, T), op0=ALU.mult, op1=ALU.add)
                    x.then_inc(conv_step, 1)

            def first_taps(dve, prods):
                conv_a, conv_b = prods
                conv_a.dve(dve)
                dve.wait_ge(bank_free, conv_b.g0 + 2)
                for u in range(2):
                    conv_b.dve_unit(dve, u)
                dve.wait_ge(bank_free, conv_b.g0 + 2 + 2)
                n = 4 * (conv_b.n - 2)
                for u in range(2, conv_b.n):
                    for part in range(4):
                        conv_b.dve_part(dve, u, part)
                        i = 4 * (u - 2) + part
                        taps(dve, 0, i * 4 * K31 // n, (i + 1) * 4 * K31 // n)

            def other_taps(dve, prods):
                g0, rounds = prods[0].g0, DC // 4 - 1
                n = 4 * sum(p.n for p in prods) // rounds
                with dve.Fori(0, rounds, 1) as r:
                    for i in range(n):
                        rest_of_weights(dve, (n // 4) * r, g0 + (i + 2) // 4, (i + 2) % 4)
                        taps(dve, r + 1, i * 4 * K31 // n, (i + 1) * 4 * K31 // n)
            enter("ln_in_g", (G("conv_a", H, "copy", dst=U), G("conv_b", H, "sig_mul", dst=U)), dve_body=first_taps)
            QK, V = S[6], S[7]
            Vn = V[:, :, :].rearrange("p c t -> p (c t)").rearrange("p (t n) -> p t n", t=TT)
            products(G("gla_q", H, "copy", dst=QK, scale=1.0 / 16, step=4), G("gla_k", H, "copy", dst=QK, at=2, step=4),
                     G("gla_v", H, "copy", dst=Vn, natural=True), G("gate0", H, "sig", dst=Y, bias=("b_gate", 0)), dve_body=other_taps,
                     loads=(("level_masks", masks[:, :, :]), ("w_alpha2", wal2)))
            quarter = lambda buf: (lambda q: buf[:, 4 * q:4 * q + 4, :])
            gated = Split(4, lambda dve, q: nc.vector.tensor_tensor(quarter(CV)(q), quarter(CV)(q), quarter(U)(q), ALU.mult),
                          quarter(CV), quarter(arena_r[8]), quarter(arena_r[5]))
            layer_norm_silu(CV, "conv_ln_g", "conv_ln_b", S[8], G("conv_z", H, "silu", dst=U),
                            (G("alpha", H, "copy_small", dst=alpha_t), G("conv_out", pair(8, 5), "bias_mul", after=True, dst=Y, bias="b_conv_out")), pre=gated)

            gated_linear_attention(QK, Vn, alpha_t, wal2, masks, stt)
            O = QK
            norm(O, CV, 4, "gla_norm_g", S[8], groups=4,
                 then=(G("gla_z", H, "silu_mul", dst=CV, split=(arena_r[8], arena_r[5]), also=Tm),
                       G("gla_out", pair(8, 5), "mul_add", after=True, dst=Y, src=Tm)),
                 loads=(("mem_t", S[4][:, :, :]),))

            M, MH, MQ, MV = S[4], pair(5, 4), S[6], S[7]
            MVn = MV[:, 0:4, :].rearrange("p c t -> p (c t)").rearrange("p (t n) -> p t n", t=TT)
            norm(M, M, DC, "mem_ln_g", S[8], split=MH, side=G("gate2a", H, "sig", dst=Tm, bias=("b_gate", 32)),
                 then=(G("mem_k", MH, "copy", after=True, dst=MQ), G("mem_v", MH, "copy", dst=MVn, natural=True),
                       G("mem_q", H, "copy", dst=MQ, at=4, scale=float(128 ** -0.5))))

            def mem_qk(h, ps):
                for t in range(TT):
                    mm = nc.tensor.matmul(ps[:, t * T:(t + 1) * T], MQ[:, 4 + h, t * P:(t + 1) * P], MQ[:, h, :], start=True, stop=True)
                return mm
            PB = S[8][:, 0:4, :].rearrange("p (b t) s -> p b t s", b=2)
            PT = S[8][:, 4:8, :].rearrange("p (b t) s -> p b t s", b=2)
            attention(MEM_HEADS, mem_qk, lambda h, s: MVn[:, s, h * P:(h + 1) * P], lambda h: MQ[:, 8 + h, :], PB, PT,
                      side=G("gate2b", H, "sig", dst=Tm, at=8, bias=("b_gate", 40)))
            X = S[5]
            products(G("mem_z", H, "silu_mul", dst=MQ, at=8, split=(arena_r[8], arena_r[6])),
                     G("mem_out", pair(8, 6, 8, 12), "mul_add", after=True, dst=Y, src=Tm, split=(arena_r[4], arena_r[2])),
                     G("w_out", pair(4, 2), "resid", after=True, dst=X, needs_loads=True, sums=S[7]), loads=((state["x"], X[:, :, :]),))
            state["left"] = (X, "final_g")

        def gated_linear_attention(QK, Vn, alpha_t, wal2, masks, stt):
            B, LA, E, Q2, O = S[4], S[5], S[8], S[5], QK
            sc = [S[4][:, a:a + 4, :].rearrange("p c (k t) -> p (c k) t", k=2) for a in (8, 12)]
            side = Prod("gate1", H, "bias", dst=Tm, bias=("b_gate", 16))
            z_done, z_abs, z_log = stage_sems("z_done", "z_abs", "z_log")
            diff_ready, exp_ready, links, top_done, ops_ready, levels_done, scores_ready, o_done, o_used = stage_sems(
                "diff_ready", "exp_ready", "dve_links", "top_done", "ops_ready", "levels_done", "scores_ready", "o_done", "o_used")
            after = {0: 2, 1: 4, 2: 6}
            before = {1: 3, 2: 5, 3: 7}
            assert side.n == 8
            Ev = E[:, :, :].rearrange("p (l c) t -> p l (c t)", l=8)
            Q2v = Q2[:, :, :].rearrange("p (l c) t -> p l (c t)", l=8)
            with nc.Block() as block:
                @block.sync
                def _(sp):
                    side.sp(sp)

                @block.vector
                def _(dve):
                    link = linker(dve, links)
                    v = nc.vector

                    def differences(h, half):
                        bh = flat(B, 2 * h, 2 * h + 2)
                        for m in range(4 * half, 4 * half + 4):
                            n = 1 << m
                            bv = bh.rearrange("p (a k s) -> p a k s", k=2, s=n)
                            out = flat(E, 2 * m, 2 * m + 2).rearrange("p (a k s) -> p a k s", k=2, s=n)
                            r = bv[:, :, 0, n - 1:n].broadcast_to([P, T // n, n])
                            v.tensor_tensor(out[:, :, 0, :], r, bv[:, :, 0, :], ALU.subtract)
                            x = v.tensor_tensor(out[:, :, 1, :], bv[:, :, 1, :], r, ALU.subtract)
                        x.then_inc(diff_ready, 1)

                    def decay(h, step):
                        half, l = step // 4, 4 * (step // 4) + 2 * (step % 2)
                        out, a = (Ev, 4 * h + 2) if step % 4 > 1 else (Q2v, 4 * h)
                        if step % 4 == 0:
                            dve.wait_ge(exp_ready, 2 * h + half + 1)
                        x = flat(QK, a, a + 2).rearrange("p (a n) -> p a n", a=1).broadcast_to([P, 2, 2 * T])
                        x = v.tensor_tensor(out[:, l:l + 2, :], Ev[:, l:l + 2, :], x, ALU.mult)
                        if step % 4 == 1:
                            link(x)
                        if step % 4 == 3:
                            x.then_inc(ops_ready, 1)

                    def scores(h, t):
                        dve.wait_ge(levels_done, 2 * h + t + 1)
                        ps = psa[:, 2 * t:2 * t + 2, :].rearrange("p b (l t) -> p (b l) t", l=4)
                        link(v.tensor_tensor(sc[t], ps, masks[:, :, :], ALU.mult))
                        v.tensor_reduce(stt[:, t, t * P:(t + 1) * P], sc[t].rearrange("p l t -> p t l"), AX.X, ALU.add).then_inc(scores_ready, 1)

                    def output(h, c):
                        dve.wait_ge(o_done, 4 * h + c + 1)
                        v.tensor_copy(O[:, 4 * h + c, :], psa[:, 1 + 2 * (c % 2), 0:T]).then_inc(o_used, 1)

                    dve.wait_ge(z_done, 1)
                    for c in range(8):
                        x = v.tensor_scalar(B[:, c, :], psa[:, c // 2, (c % 2) * T:(c % 2 + 1) * T], vcol("b_alpha", c), None, ALU.add)
                    link(x)
                    v.scalar_tensor_tensor(out=LA[:, 0:8, :], in0=B[:, 0:8, :], scalar=-1.0, in1=B[:, 0:8, :], op0=ALU.mult, op1=ALU.min).then_inc(z_abs, 1)
                    side.dve_part(dve, 0, 0)
                    link(v.tensor_scalar(B[:, 0:8, :], B[:, 0:8, :], 0.0, 1.0 / 16, ALU.min, ALU.mult))
                    side.dve_part(dve, 0, 1)
                    dve.wait_ge(z_log, 2)
                    link(v.scalar_tensor_tensor(out=LA[:, 0:8, :], in0=LA[:, 8:16, :], scalar=-1.0 / 16, in1=B[:, 0:8, :], op0=ALU.mult, op1=ALU.add))
                    side.dve_part(dve, 0, 2)
                    for c in range(8):
                        x = v.tensor_tensor_scan(B[:, c, :], LA[:, c, :], LA[:, c, :], 0.0, ALU.add, ALU.bypass)
                    link(x)
                    side.dve_part(dve, 0, 3)
                    differences(0, 0)
                    side.dve_part(dve, 1, 0)
                    differences(0, 1)
                    side.dve_part(dve, 1, 1)
                    for step in range(8):
                        decay(0, step)
                        if step in (3, 7):
                            side.dve_part(dve, 1, 2 + step // 4)
                    for h in range(GLA_HEADS):
                        scores(h, 0)
                        scores(h, 1)
                        dve.wait_ge(top_done, h + 1)
                        v.tensor_copy(stt[:, 0, P:T], psa[:, 0, 0:P]).then_inc(scores_ready, 1)
                        if h in after:
                            u = after[h]
                            side.dve_part(dve, u, 0)
                            differences(h + 1, 0)
                            side.dve_part(dve, u, 1)
                            differences(h + 1, 1)
                            side.dve_part(dve, u, 2)
                            output(h, 0)
                            output(h, 1)
                            side.dve_part(dve, u, 3)
                            decay(h + 1, 0)
                            output(h, 2)
                            output(h, 3)
                            u = before[h + 1]
                            for step in (1, 2, 3):
                                decay(h + 1, step)
                            side.dve_part(dve, u, 0)
                            decay(h + 1, 4)
                            decay(h + 1, 5)
                            side.dve_part(dve, u, 1)
                            decay(h + 1, 6)
                            side.dve_part(dve, u, 2)
                            decay(h + 1, 7)
                            side.dve_part(dve, u, 3)
                        else:
                            for c in range(4):
                                output(h, c)

                @block.scalar
                def _(act):
                    def exponential(h, half):
                        act.wait_ge(diff_ready, 2 * h + half + 1)
                        nc.scalar.activation(E[:, 8 * half:8 * half + 8, :], E[:, 8 * half:8 * half + 8, :], ACT.Exp).then_inc(exp_ready, 1)
                    act.wait_ge(z_abs, 1)
                    nc.scalar.activation(LA[:, 0:8, :], LA[:, 0:8, :], ACT.Exp).then_inc(z_log, 1)
                    side.act_part(act, 0, 0)
                    act.wait_ge(z_log, 1)
                    nc.scalar.activation(LA[:, 8:16, :], LA[:, 0:8, :], ACT.Ln, bias=1.0).then_inc(z_log, 1)
                    side.act_part(act, 0, 1)
                    side.act_part(act, 0, 2)
                    side.act_part(act, 0, 3)
                    side.act_part(act, 1, 0)
                    exponential(0, 0)
                    side.act_part(act, 1, 1)
                    exponential(0, 1)
                    side.act_part(act, 1, 2)
                    side.act_part(act, 1, 3)
                    for h in after:
                        u = after[h]
                        side.act_part(act, u, 0)
                        side.act_part(act, u, 1)
                        exponential(h + 1, 0)
                        side.act_part(act, u, 2)
                        side.act_part(act, u, 3)
                        exponential(h + 1, 1)
                        side.act_unit(act, before[h + 1])

                @block.tensor
                def _(pe):
                    for c in range(8):
                        mm = nc.tensor.matmul(psa[:, c // 2, (c % 2) * T:(c % 2 + 1) * T], wal2[:, c * P:(c + 1) * P],
                                              alpha_t, start=True, stop=True)
                    mm.then_inc(z_done, 1)
                    side.pe_unit(pe, 0)
                    side.pe_unit(pe, 1)
                    for h in range(GLA_HEADS):
                        if h in before:
                            side.pe_unit(pe, before[h])
                        for t in range(TT):
                            tk = slice(t * P, (t + 1) * P)
                            for l in range(8):
                                if t == 0 and l % 4 == 0:
                                    pe.wait_ge(ops_ready, 2 * h + l // 4 + 1)
                                    if h and l == 4:
                                        pe.wait_ge(o_used, 4 * h)
                                for c in range(2):
                                    kk = E[:, 2 * l + c, tk] if l < GLA_LEVELS else QK[:, 4 * h + 2 + c, tk]
                                    qq = Q2[:, 2 * l + c, tk] if l < GLA_LEVELS else QK[:, 4 * h + c, tk]
                                    mm = nc.tensor.matmul(psa[:, 2 * t + l // 4, (l % 4) * P:(l % 4 + 1) * P], kk, qq, start=c == 0, stop=c == 1)
                            mm.then_inc(levels_done, 1)
                        pe.wait_ge(scores_ready, 3 * h + 1)
                        for c in range(2):
                            mm = nc.tensor.matmul(psa[:, 0, 0:P], E[:, 14 + c, 0:P], Q2[:, 14 + c, P:T], start=c == 0, stop=c == 1)
                        mm.then_inc(top_done, 1)
                        if h in after:
                            side.pe_unit(pe, after[h])
                        pe.wait_ge(scores_ready, 3 * h + 3)
                        for c in range(4):
                            if c > 1:
                                pe.wait_ge(o_used, 4 * h + c - 1)
                            col, bank = (4 * h + c) * P, psa[:, 1 + 2 * (c % 2), :]
                            nc.tensor.matmul(bank[:, 0:T], Vn[:, 0, col:col + P], stt[:, 0, :], start=True, stop=False)
                            nc.tensor.matmul(bank[:, P:T], Vn[:, 1, col:col + P], stt[:, 1, P:T], start=False, stop=True).then_inc(o_done, 1)

        def block_3(own):
            with ExitStack() as rwkv_mem:
                rwkv(rwkv_mem)
            with ExitStack() as mla_mem:
                mla(mla_mem)
            X = S[6]
            products(G("w_out_3", pair(5, 8), "copy", dst=Tm, sums=S[4]), loads=((state["x"], X[:, :, :]),))
            last_norm(Tm, "g_post_3", S[0], add=X)
            state.pop("left", None)

        NC8 = 8
        CH = 64
        NCH = T // CH

        def rwkv(own):
            def sb(name, shape):
                return own.enter_context(nc.sbuf_tensor(name, shape, F32))
            RK, VD, LW, AA = S[2], S[3], S[4], S[5]
            spill_g = nc.dram_tensor("gate_rwkv_spill", (P, DC, T), F32, kind="Internal").ap()
            spill_h = [nc.dram_tensor("normed_" + n, (P, DC, T), F32, kind="Internal").ap() for n in ("hi", "lo")]
            blk = sb("head_ones", [P, P])
            masks64 = sb("chunk_masks", [P, 2, 2, P])
            m16_ts = sb("mask16_ts", [P, 2, P])
            m16_st = sb("mask16_st", [P, 2, P])
            reset = sb("chunk_reset", [P, T])
            enter("g_pre_3", (G("rwkv_rk", H, "copy", dst=RK), G("rwkv_v", H, "copy", dst=VD),
                     G("rwkv_da", H, "copy", dst=AA, at=12, rows=96)),
                     loads=(("head_ones", blk[:, :]), ("rwkv_w2", S[7][0:96, :, :]), ("chunk_masks", masks64[:, :, :, :]),
                            ("mask16_ts", m16_ts[:, :, :]), ("mask16_st", m16_st[:, :, :]), ("chunk_reset", reset[:, :])))

            TS, KK, W2 = S[8], VD[:, 8:16, :], S[7][0:96, :, :].rearrange("p c t -> p (c t)")
            side = Prod("gate_rwkv", H, "sig", dst=S[6])
            steps, tanh_in, tanh_out, low_done, low_used, kk_in, kk_squared, kk_sums, kk_root, h_stored = stage_sems(
                "dve_steps", "tanh_in", "tanh_out", "lowrank_done", "lowrank_used", "kk_ready", "kk_squared", "kk_sums", "kk_root", "h_stored")
            with nc.Block() as block:
                @block.sync
                def _(sp):
                    sp.dma_start(spill_h[0], arena_r[1][:, :, :].bitcast(F32)).then_inc(h_stored, 16)
                    sp.dma_start(spill_h[1][:, 8:16, :], arena_r[0][:, 8:16, :].bitcast(F32)).then_inc(h_stored, 16)
                    side.sp(sp)
                    sp.wait_ge(h_stored, 32)

                @block.vector
                def _(dve):
                    link = linker(dve, steps)
                    v = nc.vector
                    parts = [0]

                    def beside():
                        if parts[0] < 4 * side.n:
                            side.dve_part(dve, parts[0] // 4, parts[0] % 4)
                            parts[0] += 1

                    def shift(buf, rows, a, b, mu):
                        x = buf[0:rows, a:b, :]
                        y = TS[0:rows, 0:b - a, :]
                        v.tensor_tensor(y[:, :, 1:T - 1], x[:, :, 0:T - 2], x[:, :, 2:T], ALU.add)
                        beside()
                        v.tensor_copy(y[:, :, 0:1], x[:, :, 1:2])
                        link(v.tensor_copy(y[:, :, T - 1:T], x[:, :, T - 2:T - 1]))
                        link(v.scalar_tensor_tensor(out=y, in0=y, scalar=0.5, in1=x, op0=ALU.mult, op1=ALU.subtract))
                        beside()
                        for c in range(b - a):
                            z = v.scalar_tensor_tensor(out=x[:, c, :], in0=y[:, c, :], scalar=vcol("rwkv_mu_3", mu + c)[0:rows, :],
                                                       in1=x[:, c, :], op0=ALU.mult, op1=ALU.add)
                        return z
                    shift(AA, 96, 12, 16, 24).then_inc(tanh_in, 1)
                    dve.wait_ge(tanh_in, 1)
                    beside()
                    link(shift(RK, P, 8, 16, 8))
                    beside()
                    for c in range(NC8):
                        x = v.tensor_scalar(KK[:, c, :], RK[:, 8 + c, :], vcol("rwkv_k_k_3", c), None, ALU.mult)
                    x.then_inc(kk_in, 1)
                    beside()
                    link(shift(RK, P, 0, 8, 0))
                    beside()
                    link(shift(VD, P, 0, 8, 16))
                    beside()
                    for a in (0, 8):
                        dve.wait_ge(low_used, a + 8)
                        v.tensor_scalar(LW[:, a:a + 8, :], LW[:, a:a + 8, :], -float(np.exp(-0.5)), None, ALU.mult)
                        beside()
                    while parts[0] < 4 * 6:
                        beside()
                    norms = TS[:, 8:16, :]
                    dve.wait_ge(kk_root, 1)
                    link(v.tensor_scalar(norms, norms, 1e-12, None, ALU.max))
                    beside()
                    link(v.reciprocal(norms, norms))
                    beside()
                    v.tensor_tensor(KK, KK, norms, ALU.mult)
                    while parts[0] < 4 * side.n:
                        beside()

                @block.scalar
                def _(act):
                    side.act_part(act, 0, 0)
                    side.act_part(act, 0, 1)
                    act.wait_ge(tanh_in, 1)
                    nc.scalar.activation(AA[0:96, 12:14, :], AA[0:96, 12:14, :], ACT.Tanh).then_inc(tanh_out, 1)
                    side.act_part(act, 0, 2)
                    side.act_part(act, 0, 3)
                    for j in range(4):
                        side.act_part(act, j + 1, 0)
                        for c in range(8):
                            act.wait_ge(low_done, 8 * j + c + 1)
                            nc.scalar.activation((LW if j < 2 else AA)[:, (j % 2) * 8 + c, :], psa[:, c % 4, c // 4 * T:(c // 4 + 1) * T], ACT.Sigmoid,
                                                 bias=vcol(("rwkv_w0_f_3", "rwkv_w0_b_3", "rwkv_a0_f_3", "rwkv_a0_b_3")[j], c)).then_inc(low_used, 1)
                        for part in (1, 2, 3):
                            side.act_part(act, j + 1, part)
                        if j == 2:
                            act.wait_ge(kk_in, 1)
                            nc.scalar.activation(TS[:, 8:16, :], KK, ACT.Square).then_inc(kk_squared, 1)
                    side.act_part(act, 5, 0)
                    act.wait_ge(kk_sums, 1)
                    nc.scalar.activation(flat(TS, 8, 16).rearrange("p (k b t) -> p k b t", k=2, b=4), psa[:, :, :].rearrange("p b (k t) -> p k b t", k=2), ACT.Sqrt).then_inc(kk_root, 1)
                    for part in (1, 2, 3):
                        side.act_part(act, 5, part)
                    side.act_unit(act, 6)
                    side.act_unit(act, 7)

                @block.tensor
                def _(pe):
                    side.pe_unit(pe, 0)
                    pe.wait_ge(tanh_out, 1)
                    for j in range(4):
                        if j:
                            pe.wait_ge(low_used, 8 * j)
                        for c in range(8):
                            nc.tensor.matmul(psa[:, c % 4, c // 4 * T:(c // 4 + 1) * T], W2[:, j * 1024 + c * P:j * 1024 + (c + 1) * P],
                                             AA[0:96, 12 + j, :], start=True, stop=True).then_inc(low_done, 1)
                        side.pe_unit(pe, j + 1)
                    pe.wait_ge(low_used, 32)
                    pe.wait_ge(kk_squared, 1)
                    for c in range(NC8):
                        mm = nc.tensor.matmul(psa[:, c % 4, c // 4 * T:(c // 4 + 1) * T], blk[:, :], TS[:, 8 + c, :], start=True, stop=True)
                    mm.then_inc(kk_sums, 1)
                    for u in range(5, side.n):
                        side.pe_unit(pe, u)

            with ExitStack() as scan_mem:
                rwkv_scan(scan_mem, RK, VD, LW, AA, (masks64, m16_ts, m16_st, reset), spill_g)
            rwkv_out(own, blk, RK, VD, LW, AA, spill_h, spill_g)

        def rwkv_scan(own, RK, VD, LW, AA, scan_masks, spill_g):
            def sb(name, shape):
                return own.enter_context(nc.sbuf_tensor(name, shape, F32))
            pool = {0: [[S[6], 0], [S[1], 0]], 1: [[S[7], 0], [S[8], 0]]}

            def carve(d, n):
                for slot in pool[d]:
                    if slot[1] + n <= DC * T:
                        slot[1] += n
                        return slot[0][:, :, :].rearrange("p c t -> p (c t)")[:, slot[1] - n:slot[1]]
                raise AssertionError("arena is full")
            masks64, m16_ts, m16_st, reset = scan_masks

            def quad(ap):
                return ap.rearrange("p (i n) -> p i n", i=4)

            def per4(mask):
                return mask.rearrange("p (a n) -> p a n", a=1).broadcast_to([P, 4, mask.shape[-1]])

            class Dir:
                pass
            dirs = []
            for d in range(2):
                q = Dir()
                q.bank = [(psg, psa)[d][:, b, :] for b in range(4)]
                q.two = [(psg, psa)[d][:, 2 * b:2 * b + 2, :].rearrange("p b n -> p (b n)") for b in range(2)]
                q.M1 = carve(d, 1024).rearrange("p (i k t) -> p i k t", i=4, k=2)
                q.M2 = carve(d, 1024).rearrange("p (i k t) -> p i k t", i=4, k=2)
                q.SQ0 = carve(d, 1024).rearrange("p (k i t) -> p k i t", k=2, i=4)
                q.SQ1 = carve(d, 1024).rearrange("p (k i t) -> p k i t", k=2, i=4)
                q.RT = quad(carve(d, 512))
                q.B = [quad(carve(d, 512)) for _ in range(2)]
                q.TT = quad(carve(d, 512))
                q.AR = carve(d, 512).rearrange("p (t k n) -> p t k n", t=2, k=2)
                q.bk = carve(d, 512).rearrange("p (k n) -> p k n", k=2)
                q.bkp = tmp2[d][:, :, :]
                q.tok = flat(S[0], 8 + 4 * d, 12 + 4 * d).rearrange("p (k t n) -> p k t n", k=4, t=2)
                q.EX = carve(d, 1024).rearrange("p (k n) -> p k n", k=4) if d else stat
                q.GC = sb(f"gc{d}", [P, NCH])
                q.t1 = q.EX[:, 2, :]
                q.W1T = tmp[d][:, 1, :].rearrange("p (t n) -> p t n", t=2)
                q.Z = tmp[d][:, 0, :].rearrange("p (i n) -> p i n", i=4)
                q.W2 = q.bk[:, 0, :].rearrange("p (h t n) -> p h t n", h=2, t=2)
                q.U = q.W2
                q.S = carve(0, 256).rearrange("p (k n) -> p k n", k=NCH)
                q.ka, q.kf = tmp[d][:, 0, :], tmp[d][:, 1, :]
                q.order = range(NCH) if d == 0 else range(NCH - 1, -1, -1)
                dirs.append(q)
            prep_in, prep_exp, chain, y_done, y_copied, started, passed = stage_sems("exponents", "exponentials", "dve_chain", "y_done", "y_copied", "states_zero", "waits_passed")
            prepared = stage_sems("prepared0", "prepared1")
            pe_step = stage_sems("pe_step0", "pe_step1")
            act_step = stage_sems("act_step0", "act_step1")
            dve_step = stage_sems("dve_step0", "dve_step1")
            inst = [(hp, t) for hp in range(2) for t in range(TT)]

            STEPS = [("tok", 1, 1), ("gram", 0, 1), ("d2", 1, 0), ("d4", 1, 1), ("d8", 1, 1), ("b8", 0, 1), ("t16", 1, 0),
                     ("n1", 1, 0), ("n2", 1, 0), ("cz", 1, 1), ("tt", 0, 1), ("w", 1, 0)]
            for k in range(NCH):
                STEPS.append((("u", k), 0, 1))
                if k < NCH - 1:
                    STEPS.append((("s", k), 0, 1))
            NS = len(STEPS)
            NA = sum(x[1] for x in STEPS)
            ND = sum(x[2] for x in STEPS)

            def seen(n, col):
                return sum(x[col] for x in STEPS[:n])

            def rows(hp):
                return slice(CH * hp, CH * hp + CH)

            def pe_emit(q, name):
                b0, b1, b2, b3 = q.bank
                mm = nc.tensor.matmul
                tr = nc.tensor.transpose

                def four(bank, lhs, rhs):
                    for i in range(4):
                        x = mm(bank[:, i * P:(i + 1) * P], lhs[:, i, :], rhs[:, i, :], start=True, stop=True)
                    return x
                Dm, DT, E2, E2T = q.SQ0[:, 0], q.SQ0[:, 1], q.SQ1[:, 0], q.SQ1[:, 1]
                if name == "tok":
                    for t in range(TT):
                        tk = slice(t * P, (t + 1) * P)
                        tr(b0[:, tk], q.AR[:, t, 0, :], ident[:, :])
                        tr(b0[:, T + t * P:T + (t + 1) * P], q.bkp[:, 0, tk], ident[:, :])
                        tr(b1[:, tk], q.bkp[:, 1, tk], ident[:, :])
                        tr(b1[:, T + t * P:T + (t + 1) * P], vc_buf[:, tk], ident[:, :])
                    for i, (hp, t) in enumerate(inst):
                        x = mm(q.bank[2 + hp][:, t * P:(t + 1) * P], q.AR[rows(hp), t, 0, :], q.bk[rows(hp), 0, t * P:(t + 1) * P], start=True, stop=True)
                elif name == "gram":
                    for k in range(2):
                        for i, (hp, t) in enumerate(inst):
                            x = mm(q.two[k][:, i * T:(i + 1) * T], q.bk[rows(hp), k, t * P:(t + 1) * P],
                                   q.AR[rows(hp), t, :, :].rearrange("p k n -> p (k n)"), start=True, stop=True)
                elif name == "d2":
                    four(b0, DT, Dm)
                    x = four(b1, Dm, DT)
                elif name == "d4":
                    four(b0, E2T, E2)
                    four(b1, E2, E2T)
                    x = four(b2, E2, q.B[0])
                elif name == "d8":
                    four(b0, DT, Dm)
                    x = four(b2, Dm, q.B[1])
                elif name == "b8":
                    x = four(b2, E2, q.B[0])
                elif name == "t16":
                    for i in range(4):
                        x = tr(b0[:, i * P:(i + 1) * P], q.B[1][:, i, :], ident[:, :])
                elif name == "n1":
                    four(b0, q.RT, E2T)
                    x = four(b1, E2T, q.RT)
                elif name == "n2":
                    x = four(b0, DT, Dm)
                elif name == "cz":
                    four(b2, E2, q.B[1])
                    for i, (hp, t) in enumerate(inst):
                        x = mm(b3[:, i * CH:(i + 1) * CH], q.M2[:, i, 0, :], q.tok[:, 3, t, CH * hp:CH * hp + CH], start=True, stop=True)
                elif name == "tt":
                    x = four(b2, Dm, q.B[0])
                elif name == "w":
                    for i, (hp, t) in enumerate(inst):
                        mm(b0[rows(hp), t * P:(t + 1) * P], q.tok[:, 0, t, CH * hp:CH * hp + CH], q.TT[:, i, :], start=True, stop=True)
                        x = mm(b1[:, i * CH:(i + 1) * CH], q.TT[:, i, :], q.Z[:, i, :], start=True, stop=True)
                elif name[0] == "u":
                    c = q.order[name[1]]
                    half = rows(c % 2)
                    for hp in range(2):
                        x = mm(q.bank[hp][half, 0:CH], q.W1T[rows(hp), c // 2, CH * (c % 2):CH * (c % 2) + CH],
                               q.S[rows(hp), name[1], :], start=True, stop=True)
                elif name[0] == "s":
                    c = q.order[name[1]]
                    half = rows(c % 2)
                    for hp in range(2):
                        mm(b2[rows(hp), 0:CH], q.tok[half, 1, c // 2, CH * hp:CH * hp + CH], q.U[half, hp, c // 2, :], start=True, stop=False)
                        x = mm(b2[rows(hp), 0:CH], q.tok[half, 2, c // 2, CH * hp:CH * hp + CH],
                               q.tok[half, 3, c // 2, CH * hp:CH * hp + CH], start=False, stop=True)
                return x

            def act_emit(q, name):
                cp = lambda o, i: nc.scalar.activation(o, i, ACT.Copy)
                if name == "tok":
                    return cp(q.tok, q.two[0].rearrange("p (k t n) -> p k t n", k=4, t=2))
                if name in ("d2", "n1", "d4"):
                    src = q.two[0].rearrange("p (k i t) -> p k i t", k=2, i=4)
                    return cp(q.SQ1 if name == "d2" else q.SQ0, src)
                if name in ("d8", "n2"):
                    return cp(q.SQ1[:, 0], quad(q.bank[0]))
                if name == "t16":
                    return cp(q.SQ1[:, 1], quad(q.bank[0]))
                if name == "cz":
                    return cp(q.Z, quad(q.bank[3][:, 0:T]))
                if name == "w":
                    cp(q.W1T, q.bank[0][:, 0:T].rearrange("p (t n) -> p t n", t=2))
                    return cp(q.W2, q.bank[1][:, 0:T].rearrange("p (h t n) -> p h t n", h=2, t=2))

            def dve_emit(dve, d, q, name, link):
                tt = nc.vector.tensor_tensor
                b2 = quad(q.bank[2])
                if name == "tok":
                    dve.wait_ge(stored, 16)
                    four = lambda ap: ap.rearrange("p (h t) n -> p h t n", h=2)
                    grams = q.two[1].rearrange("p (h x) -> p h x", h=2)[:, :, 0:T].rearrange("p h (t n) -> p h t n", t=TT)
                    return tt(four(q.SQ0[:, 0]), grams, four(per4(m16_ts[:, d, :])), ALU.mult)
                if name == "gram":
                    m = masks64[:, d, :, :].rearrange("p k t -> p (k t)")
                    for k, M in ((1, q.M2), (0, q.M1)):
                        x = tt(M.rearrange("p i k t -> p i (k t)"), q.two[k].rearrange("p (i n) -> p i n", i=4), per4(m), ALU.mult)
                    link(x)
                    link(tt(q.SQ0[:, 1], q.M1[:, :, 0, :], per4(m16_st[:, d, :]), ALU.mult))
                    tt(q.RT, q.M1[:, :, 0, :], q.SQ0[:, 1], ALU.subtract)
                    return tt(q.B[0], q.SQ0[:, 1], per4(ident[:, :]), ALU.add)
                if name == "d4":
                    return tt(q.B[1], b2, q.B[0], ALU.add)
                if name == "d8":
                    return tt(q.B[0], b2, q.B[1], ALU.add)
                if name == "b8":
                    return tt(q.B[1], b2, q.B[0], ALU.add)
                if name == "cz":
                    return tt(q.B[0], b2, q.B[1], ALU.add)
                if name == "tt":
                    return tt(q.TT, b2, q.B[0], ALU.add)
                c = q.order[name[1]]
                if name[0] == "u":
                    half = rows(c % 2)
                    return tt(q.U[half, :, c // 2, :], q.two[0].rearrange("p (h x) -> p h x", h=2)[half, :, 0:CH], q.W2[half, :, c // 2, :], ALU.add)
                return nc.vector.scalar_tensor_tensor(out=q.S[:, name[1] + 1, :], in0=q.S[:, name[1], :], scalar=q.GC[:, c:c + 1],
                                                      in1=q.bank[2][:, 0:CH], op0=ALU.mult, op1=ALU.add)

            vc_buf = carve(0, T)
            NCHAIN = 2 * (4 + 3 + 2)
            (stored,) = stage_sems("gate_stored")
            with nc.Block() as block:
                @block.sync
                def _(sp):
                    sp.dma_start(spill_g, S[6][:, :, :]).then_inc(stored, 16)
                    sp.wait_ge(stored, 16)

                @block.tensor
                def _(pe):
                    pe.wait_ge(started, 1)
                    with pe.Fori(0, NC8, 1) as it:
                        for n, (name, _, _) in enumerate(STEPS):
                            for d, q in enumerate(dirs):
                                if n == 0:
                                    pe.wait_ge(prepared[d], it + 1)
                                else:
                                    pe.wait_ge(act_step[d], it * NA + seen(n, 1))
                                if seen(n, 2):
                                    pe.wait_ge(dve_step[d], it * ND + seen(n, 2))
                                if name[0] in ("u", "s"):
                                    pe.sem_inc(passed, 1)
                                pe_emit(q, name).then_inc(pe_step[d], 1)
                        for d in range(2):
                            pe.wait_ge(dve_step[d], it * ND + ND)
                        yb = dirs[0].bank[3]
                        for i, (hp, t) in enumerate(inst):
                            y = yb[rows(hp), t * P:(t + 1) * P]
                            for d, q in enumerate(dirs):
                                nc.tensor.matmul(y, q.tok[:, 3, t, CH * hp:CH * hp + CH], q.M2[:, i, 1, :], start=d == 0, stop=False)
                                nc.tensor.matmul(y, q.U[:, hp, t, :], q.M1[:, i, 1, :], start=False, stop=False)
                                for k in range(NCH):
                                    c = q.order[k]
                                    if c // 2 == t:
                                        mm = nc.tensor.matmul(yb[rows(hp), c * CH:(c + 1) * CH], q.S[rows(hp), k, :],
                                                              q.AR[rows(hp), t, 1, CH * (c % 2):CH * (c % 2) + CH],
                                                              start=False, stop=d == 1 and k == max(kk for kk in range(NCH) if q.order[kk] // 2 == t))
                        mm.then_inc(y_done, 1)

                @block.scalar
                def _(act):
                    act.sem_inc(y_copied, 1)
                    with act.Fori(0, NC8, 1) as it:
                        for d, q in enumerate(dirs):
                            act.wait_ge(prep_in, 2 * it + (d + 1))
                            nc.scalar.activation(q.EX[:, 3, :], q.EX[:, 0, :], ACT.Exp, scale=-1.0).then_inc(prep_exp, 1)
                            act.wait_ge(prep_exp, it * 6 + (3 * d + 1))
                            nc.scalar.activation(q.EX[:, 0:3, :], q.EX[:, 0:3, :], ACT.Exp).then_inc(prep_exp, 1)
                            nc.scalar.activation(q.GC[:, :], q.GC[:, :], ACT.Exp).then_inc(prep_exp, 1)
                        for n, (name, a, _) in enumerate(STEPS):
                            if a:
                                for d, q in enumerate(dirs):
                                    act.wait_ge(pe_step[d], it * NS + (n + 1))
                                    act_emit(q, name).then_inc(act_step[d], 1)
                        act.wait_ge(y_done, it + 1)
                        nc.scalar.activation(LW[:, bass.ds(it, 1), :].rearrange("p a t -> p (a t)"), dirs[0].bank[3][:, 0:T], ACT.Copy).then_inc(y_copied, 1)

                @block.vector
                def _(dve):
                    for d, q in enumerate(dirs):
                        x = nc.vector.memset(q.S[:, 0, :], 0.0)
                    nc.vector.memset(small[:, :], 0.0).then_inc(started, 1)
                    dve.wait_ge(started, 1)
                    v = nc.vector
                    with dve.Fori(0, NC8, 1) as it:
                        count = [0]

                        def link(x):
                            count[0] += 1
                            x.then_inc(chain, 1)
                            dve.wait_ge(chain, it * NCHAIN + count[0])

                        def pair(buf, off):
                            return buf[:, bass.ds(it + off, 1), :].rearrange("p a t -> p (a t)")
                        v.tensor_copy(vc_buf[:, :], pair(VD, 0))
                        for d, q in enumerate(dirs):
                            lw = pair(LW, 8 * d)
                            by = lambda ap: ap.rearrange("p (c n) -> p c n", c=NCH)
                            link(v.tensor_tensor_scan(q.ka, reset[:, :], lw, 0.0, ALU.mult, ALU.add))
                            tot = by(q.ka)[:, :, CH - 1:CH]
                            incl, excl, tail = q.EX[:, 0, :], q.EX[:, 1, :], q.EX[:, 2, :]
                            link(v.tensor_tensor(by(excl if d else tail), tot.broadcast_to([P, NCH, CH]), by(q.ka), ALU.subtract))
                            link(v.tensor_tensor(tail if d else excl, q.ka, lw, ALU.subtract))
                            if d:
                                link(v.tensor_tensor(incl, excl, lw, ALU.add))
                            else:
                                link(v.tensor_copy(incl, q.ka))
                            v.tensor_copy(q.GC[:, :], q.ka.rearrange("p (c n) -> p c n", c=NCH)[:, :, CH - 1]).then_inc(prep_in, 1)
                        for d, q in enumerate(dirs):
                            aa = pair(AA, 8 * d)
                            link(v.tensor_tensor(q.ka, pair(VD, 8), aa, ALU.mult))
                            link(v.tensor_scalar(q.kf, aa, 1.0, vecs[:, bass.ds(it + VEC_AT["rwkv_k_a_3"], 1)], ALU.subtract, ALU.mult))
                            link(v.scalar_tensor_tensor(out=q.kf, in0=q.kf, scalar=1.0, in1=pair(RK, 8), op0=ALU.add, op1=ALU.mult))
                            dve.wait_ge(prep_exp, it * 6 + (3 * d + 3))
                            til = lambda ap: ap.rearrange("p (t n) -> p t n", t=TT)
                            dve.wait_ge(y_copied, it + 1)
                            v.scalar_tensor_tensor(out=q.AR[:, :, 0, :], in0=til(pair(VD, 8)), scalar=-1.0, in1=til(q.EX[:, 1, :]), op0=ALU.mult, op1=ALU.mult)
                            v.tensor_tensor(q.AR[:, :, 1, :], til(pair(RK, 0)), til(q.EX[:, 0, :]), ALU.mult)
                            v.tensor_tensor(q.bk[:, 0, :], q.ka, q.EX[:, 3, :], ALU.mult)
                            v.tensor_tensor(q.bk[:, 1, :], q.kf, q.EX[:, 3, :], ALU.mult)
                            v.tensor_tensor(q.bkp[:, 0, :], q.ka, q.EX[:, 2, :], ALU.mult)
                            v.tensor_tensor(q.bkp[:, 1, :], q.kf, q.EX[:, 2, :], ALU.mult).then_inc(prepared[d], 1)
                        for n, (name, _, a) in enumerate(STEPS):
                            if a:
                                for d, q in enumerate(dirs):
                                    dve.wait_ge(pe_step[d], it * NS + (n + 1))
                                    dve_emit(dve, d, q, name, link).then_inc(dve_step[d], 1)
                        assert count[0] == NCHAIN

        def rwkv_out(own, blk, RK, VD, LW, AA, spill_h, spill_g):
            YR, G6, G7 = LW, S[6], S[7]
            side = Prod("z_rwkv", H, "silu", dst=S[7], at=8)
            side2 = Prod("mla_qkv_a", H, "copy", dst=RK)
            out = Split(4, lambda dve, q: nc.vector.tensor_tensor(YR[:, 2 * q:2 * q + 2, :], G6[:, 2 * q:2 * q + 2, :], S[7][:, 8 + 2 * q:10 + 2 * q, :], ALU.mult),
                        *[(lambda q, x=x: x[:, 2 * q:2 * q + 2, :]) for x in (YR, arena_r[5], arena_r[4])])
            run = Run(G("mla_k_rope", H, "copy", dst=RK, at=8), G("br_rwkv", pair(5, 4, 0, 8), "bias_mul", after=True, dst=S[8]), pre=out)
            a_in, a_out, p1, p2, steps, back, again = stage_sems("act_in", "act_out", "pe_done", "pe_used", "dve_steps", "h_back", "h_again")
            (gate_back,) = stage_sems("gate_back")
            with nc.Block() as block:
                @block.sync
                def _(sp):
                    for a, b, k in ((0, 8, 1), (8, 16, 1), (8, 16, 0)):
                        sp.dma_start(S[k][:, a:b, :], spill_h[1 - k][:, a:b, :]).then_inc(back, 16)
                    sp.dma_start(S[8][:, :, :], spill_g).then_inc(gate_back, 16)
                    side.sp(sp)
                    side2.sp(sp)
                    run.sp(sp)

                @block.vector
                def _(dve):
                    link = linker(dve, steps)
                    v = nc.vector
                    link(v.tensor_tensor(AA[:, 0:8, :], AA[:, 0:8, :], AA[:, 8:16, :], ALU.add))
                    for c in range(NC8):
                        x = v.tensor_scalar(AA[:, c, :], AA[:, c, :], 2.0, vcol("rwkv_k_a_3", c), ALU.subtract, ALU.mult)
                    link(x)
                    link(v.scalar_tensor_tensor(out=AA[:, 0:8, :], in0=AA[:, 0:8, :], scalar=2.0, in1=RK[:, 8:16, :], op0=ALU.add, op1=ALU.mult))
                    for c in range(NC8):
                        x = v.scalar_tensor_tensor(out=AA[:, c, :], in0=AA[:, c, :], scalar=vcol("rwkv_r_k_3", c), in1=RK[:, c, :], op0=ALU.mult, op1=ALU.mult)
                    x.then_inc(a_in, 1)
                    side.dve_unit(dve, 0)
                    side.dve_unit(dve, 1)
                    for c in range(NC8):
                        dve.wait_ge(p1, 2 * c + 2)
                        v.scalar_tensor_tensor(out=G6[:, c, :], in0=psa[:, 2 * (c % 2), 0:T], scalar=-1.0 / 64, in1=YR[:, c, :], op0=ALU.mult, op1=ALU.add)
                        v.tensor_tensor(G7[:, c, :], psa[:, 2 * (c % 2) + 1, 0:T], VD[:, c, :], ALU.mult).then_inc(p2, 1)
                    side.dve_unit(dve, 2)
                    for c in range(NC8):
                        dve.wait_ge(p1, 16 + c + 1)
                        v.tensor_scalar(G6[:, 8 + c, :], psa[:, c % 4, 0:T], 1.0 / 64, 64e-5, ALU.mult, ALU.add).then_inc(p2, 1)
                    dve.wait_ge(a_out, 2)
                    link(v.reciprocal(G6[:, 8:16, :], G6[:, 8:16, :]))
                    side.dve_unit(dve, 3)
                    link(v.tensor_tensor(G6[:, 0:8, :], G6[:, 0:8, :], G6[:, 8:16, :], ALU.mult))
                    side2.dve_unit(dve, 0)
                    for c in range(NC8):
                        x = v.tensor_scalar(G6[:, c, :], G6[:, c, :], vcol("rwkv_gn_g_3", c), vcol("rwkv_gn_b_3", c), ALU.mult, ALU.add)
                    link(x)
                    side2.dve_unit(dve, 1)
                    link(v.tensor_tensor(G6[:, 0:8, :], G6[:, 0:8, :], G7[:, 0:8, :], ALU.add))
                    side2.dve_unit(dve, 2)
                    side2.dve_unit(dve, 3)
                    dve.wait_ge(gate_back, 16)
                    run.dve(dve)

                @block.tensor
                def _(pe):
                    pe.wait_ge(again, 2)
                    side.pe_unit(pe, 0)
                    side.pe_unit(pe, 1)
                    pe.wait_ge(a_in, 1)
                    for c in range(NC8):
                        if c >= 2:
                            pe.wait_ge(p2, c - 1)
                        nc.tensor.matmul(psa[:, 2 * (c % 2), 0:T], blk[:, :], YR[:, c, :], start=True, stop=True).then_inc(p1, 1)
                        nc.tensor.matmul(psa[:, 2 * (c % 2) + 1, 0:T], blk[:, :], AA[:, c, :], start=True, stop=True).then_inc(p1, 1)
                    side.pe_unit(pe, 2)
                    pe.wait_ge(a_out, 1)
                    for c in range(NC8):
                        if c >= 4:
                            pe.wait_ge(p2, 8 + c - 3)
                        nc.tensor.matmul(psa[:, c % 4, 0:T], blk[:, :], AA[:, 8 + c, :], start=True, stop=True).then_inc(p1, 1)
                    side.pe_unit(pe, 3)
                    for u in range(side2.n):
                        side2.pe_unit(pe, u)
                    run.pe(pe)

                @block.scalar
                def _(act):
                    act.wait_ge(back, 48)
                    nc.scalar.activation(arena_r[1][:, :, :], S[1][:, :, :], ACT.Copy).then_inc(again, 1)
                    nc.scalar.activation(arena_r[0][:, 8:16, :], S[0][:, 8:16, :], ACT.Copy).then_inc(again, 1)
                    side.act_unit(act, 0)
                    side.act_unit(act, 1)
                    act.wait_ge(p2, NC8)
                    nc.scalar.activation(AA[:, 8:16, :], G6[:, 0:8, :], ACT.Square).then_inc(a_out, 1)
                    side.act_unit(act, 2)
                    act.wait_ge(p2, 2 * NC8)
                    nc.scalar.activation(G6[:, 8:16, :], G6[:, 8:16, :], ACT.Sqrt).then_inc(a_out, 1)
                    side.act_unit(act, 3)
                    for u in range(side2.n):
                        side2.act_unit(act, u)
                    run.act(act)

        def mla(own):
            QA, QN, RO = S[2], S[5], S[6]
            rot = S[7][:, 8:10, :]
            OA = S[3]
            QL, KL = pair(3, 2, 0, 4), pair(3, 2, 4, 8)
            VN = RO[:, 8:16, :].rearrange("p c t -> p (c t)").rearrange("p (t n) -> p t n", t=TT)
            scale = float((128 + 64) ** -0.5)
            (steps,) = stage_sems("dve_steps")

            def rotate(dve):
                link = linker(dve, steps)

                def table(k, n):
                    return rot[:, k:k + 1, :].broadcast_to([P, n, T])
                for a, n, buf in ((0, 4, RO), (8, 1, QA)):
                    x, y = buf[:, a:a + n, :], buf[:, a + n:a + 2 * n, :]
                    nc.vector.tensor_tensor(x, x, table(0, n), ALU.mult)
                    link(nc.vector.tensor_tensor(y, y, table(1, n), ALU.mult))
                    link(nc.vector.tensor_tensor(x, x, y, ALU.add))
            norm(QA, QA, 4, "mla_q_norm_3", S[7], groups=2, split=(arena_r[3], arena_r[2]),
                 then=(G("mla_q_rope", QL, "copy", after=True, dst=RO, scale=scale), G("mla_q_nope", QL, "copy", dst=QN, scale=scale),
                       G("mla_k_nope", KL, "copy", dst=QN, at=8, needs_loads=True, before=rotate), G("mla_v", KL, "copy", dst=VN, natural=True)),
                 loads=(("rotary", rot),))

            def qk(h, ps):
                half = slice(64 * (h % 2), 64 * (h % 2) + 64)
                for t in range(TT):
                    tk = slice(t * P, (t + 1) * P)
                    nc.tensor.matmul(ps[:, t * T:(t + 1) * T], QN[:, h, tk], QN[:, 8 + h, :], start=True, stop=False)
                    mm = nc.tensor.matmul(ps[:, t * T:(t + 1) * T], RO[half, h // 2, tk], QA[half, 8, :], start=False, stop=True)
                return mm
            PB = S[4][:, 0:4, :].rearrange("p (b t) s -> p b t s", b=2)
            PT = S[4][:, 4:8, :].rearrange("p (b t) s -> p b t s", b=2)
            attention(8, qk, lambda h, s: VN[:, s, h * P:(h + 1) * P], lambda h: OA[:, h, :], PB, PT,
                      side=G("gate_mla", H, "sig", dst=S[7]))
            products(G("z_mla", H, "silu_mul", dst=OA, split=(arena_r[4], arena_r[3])),
                     G("br_mla", pair(4, 3), "mul_add", after=True, dst=S[8], src=S[7], split=(arena_r[5], arena_r[8])))

        IH, NH, NKV, TOPK, RB = 8, 16, 4, 64, 32

        def block_2(own):
            tri = own.enter_context(nc.sbuf_tensor("causal_t", [P, P], F32))
            with ExitStack() as attn_mem:
                sparse_attention(attn_mem, tri)
            X = S[6]
            sgu(tri, X)
            steps = []
            for part, c in FF_ORDER:
                F, hi = 2 + c % 2, 7 + c % 2
                if part == 1:
                    steps.append(G(f"ff1_{c}", pair(1, 5), "relu2", dst=S[F], split=(arena_r[hi], arena_r[F])))
                else:
                    steps.append(G(f"ff2_{c}", pair(hi, F), "resid", after=f"ff1_{c}", dst=X, sums=S[4] if c == 3 else None))
            norm(X, S[5], DC, "norm2_g_2", S[4], split=(arena_r[1], arena_r[5]), summed=True, then=steps)
            state["left"] = (X, "final_g_2")

        def sparse_attention(own, tri):
            def sb(name, shape):
                return own.enter_context(nc.sbuf_tensor(name, shape, F32))
            Q, KI, V4 = S[2], S[3], S[3]
            wi = sb("index_weights", [P, TT, IH])
            onehot = flat(S[7][0:RB], 8, 10)
            rel = sb("rel_bias_sb", [RB, NH])
            exch = sb("exchange", [P, P])
            bvec = flat(S[7][0:NH], 10, 12)
            causal = sb("causal", [P, 2, TT, T])
            VN = V4[:, 12:16, :].rearrange("p c t -> p (c t)").rearrange("p (t n) -> p t n", t=TT)
            enter("norm1_g_2", (G("sa_q", H, "copy", dst=Q, scale=float(128 ** -0.5)), G("sa_k", H, "copy", dst=KI),
                     G("sa_v", H, "copy", dst=VN, natural=True), G("sa_qi", H, "copy", dst=KI, at=4),
                     G("sa_ki", H, "copy_small", dst=KI[:, 8, :]), G("sa_wi", H, "copy_narrow", dst=wi[:, :, :], natural=True)),
                     loads=(("bucket_onehot", onehot), ("rel_bias", rel[:, :]), ("exchange", exch[:, :]),
                            ("causal", causal[:, :, :, :]), ("causal_t", tri[:, :])))

            RBs = [S[5], S[6]]
            RBv = [r[:, 0:12, :].rearrange("p c t -> p (c t)").rearrange("p (h z) -> p h z", h=8) for r in RBs]
            scratch = nc.dram_tensor("bias_scratch", (NH, 512), F32, kind="Internal").ap()
            pe_b, act_b, dma_b = stage_sems("bias_done", "bias_copied", "bias_moved")
            idx_done, relu_done, steps, scaled = stage_sems("index_done", "relu_done", "dve_steps", "scaled")
            RL = S[7][:, 0:2, :]
            SC = S[7][:, 2:4, :]
            WK = S[7][:, 4:6, :]
            MK = S[8][:, 8:10, :]
            m8 = small[:, 16:32]
            side = Prod("sgu_u", H, "copy", dst=S[4])
            with nc.Block() as block:
                @block.sync
                def _(sp):
                    side.sp(sp)
                    sp.wait_ge(act_b, 1)
                    sp.dma_start(scratch, bvec).then_inc(dma_b, 16)
                    sp.wait_ge(dma_b, 16)
                    for k in range(2):
                        src = bass.AP(tensor=scratch.tensor, offset=scratch.offset + 8 * k * 512, ap=[[1, P], [512, 8], [1, 384]])
                        sp.dma_start(RBv[k], src).then_inc(dma_b, 16)
                    sp.wait_ge(dma_b, 48)

                @block.tensor
                def _(pe):
                    nc.tensor.matmul(psa[0:NH, 3, :], rel[:, :], onehot, start=True, stop=True).then_inc(pe_b, 1)
                    for t in range(TT):
                        for h in range(IH):
                            n = IH * t + h
                            if n == 3:
                                pe.wait_ge(act_b, 1)
                            if n in (4, 10):
                                side.pe_unit(pe, n // 10)
                            if n >= 4:
                                pe.wait_ge(relu_done, n - 3)
                            half = slice(64 * (h % 2), 64 * (h % 2) + 64)
                            nc.tensor.matmul(psa[:, n % 4, 0:T], KI[half, 4 + h // 2, t * P:(t + 1) * P], KI[half, 8, :],
                                             start=True, stop=True).then_inc(idx_done, 1)

                    for u in range(2, side.n):
                        side.pe_unit(pe, u)

                @block.scalar
                def _(act):
                    act.wait_ge(pe_b, 1)
                    nc.scalar.activation(bvec, psa[0:NH, 3, :], ACT.Copy).then_inc(act_b, 1)
                    for n in range(TT * IH):
                        act.wait_ge(idx_done, n + 1)
                        if n >= 2:
                            act.wait_ge(scaled, n)
                        nc.scalar.activation(RL[:, n % 2, :], psa[:, n % 4, 0:T], ACT.Relu).then_inc(relu_done, 1)
                        if n in (3, 9):
                            side.act_unit(act, n // 9)
                    for u in range(2, side.n):
                        side.act_unit(act, u)

                @block.vector
                def _(dve):
                    link = linker(dve, steps)
                    v = nc.vector
                    v.tensor_scalar(wi[:, :, :], wi[:, :, :], float(IH ** -0.5 * 64 ** -0.5), None, ALU.mult).then_inc(scaled, 1)
                    dve.wait_ge(scaled, 1)
                    for t in range(TT):
                        for h in range(IH):
                            n = IH * t + h
                            dve.wait_ge(relu_done, n + 1)
                            dve.wait_ge(scaled, n + 1)
                            w = wi[:, t, h:h + 1]
                            if h == 0:
                                v.tensor_scalar(SC[:, t, :], RL[:, n % 2, :], w, None, ALU.mult).then_inc(scaled, 1)
                            else:
                                v.scalar_tensor_tensor(out=SC[:, t, :], in0=RL[:, n % 2, :], scalar=w, in1=SC[:, t, :],
                                                       op0=ALU.mult, op1=ALU.add).then_inc(scaled, 1)
                            if n in (3, 9):
                                side.dve_unit(dve, n // 9)
                    dve.wait_ge(scaled, TT * IH + 1)
                    link(v.tensor_tensor(SC, SC, causal[:, 1, :, :], ALU.add))
                    for r in range(TOPK // 8):
                        src = SC if r == 0 else WK
                        for t in range(TT):
                            x = v.max(m8[:, 8 * t:8 * t + 8], src[:, t, :])
                        link(x)
                        for t in range(TT):
                            x = v.match_replace(out=WK[:, t, :], in_to_replace=m8[:, 8 * t:8 * t + 8], in_values=src[:, t, :], imm_value=-3e38)
                        link(x)
                        if r % 2:
                            side.dve_unit(dve, 2 + r // 2)
                    link(v.tensor_tensor(WK, WK, SC, ALU.is_equal))
                    link(v.tensor_scalar(WK, WK, -1.0, 1.0, ALU.mult, ALU.add))
                    link(v.tensor_tensor(WK, WK, causal[:, 0, :, :], ALU.mult))
                    link(v.tensor_scalar(MK, WK, 1.0, -NEG, ALU.subtract, ALU.mult))
                    for u in range(6, side.n):
                        side.dve_unit(dve, u)

            def qk(h, ps):
                for t in range(TT):
                    nc.tensor.matmul(ps[:, t * T:(t + 1) * T], Q[:, h, t * P:(t + 1) * P], KI[:, h // (NH // NKV), :], start=True, stop=False)
                    off = P * (1 - t)
                    mm = nc.tensor.matmul(ps[:, t * T:(t + 1) * T], exch[:, :], RBv[h // 8][:, h % 8, off:off + T], start=False, stop=True)
                return mm
            PB = S[8][:, 0:4, :].rearrange("p (b t) s -> p b t s", b=2)
            PT = S[8][:, 4:8, :].rearrange("p (b t) s -> p b t s", b=2)
            attention(NH, qk, lambda h, s: VN[:, s, (h // (NH // NKV)) * P:(h // (NH // NKV) + 1) * P], lambda h: Q[:, h, :], PB, PT, mask=MK,
                      side=G("sgu_v", H, "copy", natural=True, dst=flat(S[7], 0, DC).rearrange("p (t n) -> p t n", t=TT)))

        def sgu(ones_tri, X):
            U, VS, M5, S6, GB, WB = S[4], S[7], S[5], S[6], S[3], S[8]
            VN = VS[:, :, :].rearrange("p c t -> p (c t)").rearrange("p (t n) -> p t n", t=TT)
            gb = flat(GB, 0, DC).rearrange("p (k n) -> p k n", k=2)
            ws = flat(WB, 0, 8).rearrange("p (g t) -> p g t", g=16)
            bs = flat(WB, 8, 16).rearrange("p (g t) -> p g t", g=16)
            tri_t = ones_tri
            cub, sig, steps, ln_in, ln_out, mix, mixed, sq = stage_sems("cubes", "sigmoids", "dve_steps", "ln_in", "ln_sums", "mix_done", "mixed", "root")
            (loaded,) = stage_sems("loaded")
            side = Prod("gate_a", H, "sig", dst=S6)
            with nc.Block() as block:
                @block.sync
                def _(sp):
                    for k, name in enumerate(("sgu_g", "sgu_b")):
                        sp.dma_start(gb[:, k, :], ins[name].broadcast_to([P, D])).then_inc(loaded, 16)
                    sp.dma_start(ws, ins["sgu_w"]).then_inc(loaded, 16)
                    sp.dma_start(bs, ins["sgu_bias"].broadcast_to([P, D]).rearrange("p (g t) -> p g t", g=16)).then_inc(loaded, 16)
                    side.sp(sp)
                    sp.wait_ge(loaded, 64)

                @block.vector
                def _(dve):
                    link = linker(dve, steps)
                    v = nc.vector
                    for k, x in enumerate((VS, U)):
                        x, tm = x[:, :, :], M5[:, :, :]
                        link(v.tensor_tensor(tm, x, x, ALU.mult))
                        link(v.tensor_scalar(tm, tm, 0.044715, 1.0, ALU.mult, ALU.add))
                        v.tensor_tensor(tm, tm, x, ALU.mult).then_inc(cub, 1)
                        if k:
                            side.dve_unit(dve, 1)
                        dve.wait_ge(sig, k + 1)
                        v.tensor_tensor(x, x, tm, ALU.mult).then_inc(ln_in, 1)
                        dve.wait_ge(ln_in, k + 1)
                        side.dve_unit(dve, 2 * k)
                    dve.wait_ge(ln_out, 4)
                    mean, sums = small[:, 32:34], small[:, 34:36]
                    link(v.tensor_scalar(small[:, 32:36], small[:, 32:36], 1.0 / D, None, ALU.mult))
                    link(v.tensor_tensor(small[:, 36:38], mean, mean, ALU.mult))
                    link(v.tensor_tensor(sums, sums, small[:, 36:38], ALU.subtract))
                    v.tensor_scalar(sums, sums, EPS, None, ALU.add).then_inc(ln_in, 1)
                    dve.wait_ge(sq, 1)
                    link(v.reciprocal(sums, sums))
                    dve.wait_ge(loaded, 64)
                    for t in range(TT):
                        x = v.tensor_scalar(VN[:, t, :], VN[:, t, :], small[:, 32 + t:33 + t], small[:, 34 + t:35 + t], ALU.subtract, ALU.mult)
                    link(x)
                    gk = lambda k: gb[:, k:k + 1, :].broadcast_to([P, TT, D])
                    link(v.tensor_tensor(VN, VN, gk(0), ALU.mult))
                    side.dve_unit(dve, 3)
                    v.tensor_tensor(VN, VN, gk(1), ALU.add)
                    v.tensor_tensor(ws, ws, tri_t[:, :].rearrange("p (a t) -> p a t", a=1).broadcast_to([P, 16, P]), ALU.mult).then_inc(ln_in, 1)
                    for g in range(16):
                        if g and g % 4 == 0:
                            side.dve_unit(dve, 3 + g // 4)
                        dve.wait_ge(mix, g + 1)
                        b = bs[:, g:g + 1, :].broadcast_to([P, TT, P])
                        v.tensor_tensor(M5[:, g, :].rearrange("p (c t) -> p c t", c=TT), psa[:, g % 4, 0:T].rearrange("p (c t) -> p c t", c=TT), b, ALU.add).then_inc(mixed, 1)
                    side.dve_unit(dve, side.n - 1)

                @block.scalar
                def _(act):
                    def gate(k):
                        act.wait_ge(cub, k + 1)
                        nc.scalar.activation(M5[:, :, :], M5[:, :, :], ACT.Sigmoid, scale=float(2 * np.sqrt(2 / np.pi))).then_inc(sig, 1)
                    gate(0)
                    side.act_unit(act, 0)
                    act.wait_ge(ln_in, 1)
                    for t in range(TT):
                        junk = psa[:, :, :].rearrange("p b n -> p (b n)")
                        if t:
                            act.wait_ge(ln_out, 2)
                        nc.scalar.activation(junk, VN[:, t, :], ACT.Copy, accum_out=small[:, 32 + t:33 + t]).then_inc(ln_out, 1)
                        if t == 0:
                            side.act_unit(act, 1)
                        act.wait_ge(ln_out, 2 * t + 1)
                        nc.scalar.activation(junk, VN[:, t, :], ACT.Square, accum_out=small[:, 34 + t:35 + t]).then_inc(ln_out, 1)
                    gate(1)
                    side.act_unit(act, 2)
                    act.wait_ge(ln_in, 3)
                    nc.scalar.activation(small[:, 34:36], small[:, 34:36], ACT.Sqrt).then_inc(sq, 1)
                    for u in range(3, side.n):
                        side.act_unit(act, u)

                @block.tensor
                def _(pe):
                    for u in range(4):
                        side.pe_unit(pe, u)
                    pe.wait_ge(ln_in, 4)
                    for g in range(16):
                        if g >= 4:
                            pe.wait_ge(mixed, g - 3)
                        for c in range(TT):
                            mm = nc.tensor.matmul(psa[:, g % 4, c * P:(c + 1) * P], VN[:, c, g * P:(g + 1) * P], ws[:, g, :], start=True, stop=True)
                        mm.then_inc(mix, 1)
                        if g % 4 == 3:
                            side.pe_unit(pe, 4 + g // 4)
            (gated,) = stage_sems("gated")

            def gate_branches(dve):
                v.tensor_tensor(M5[:, :, :], M5[:, :, :], U[:, :, :], ALU.mult).then_inc(gated, 1)
                v.tensor_tensor(S[2][:, :, :], S[2][:, :, :], S6[:, :, :], ALU.mult).then_inc(gated, 1)
                dve.wait_ge(gated, 2)
            v = nc.vector
            products(G("gate_b", H, "gate_add", dst=S[2], src=M5, split=(arena_r[3], arena_r[2])), dve_pre=gate_branches)
            products(G("w_out_2", pair(3, 2), "resid", dst=X, needs_loads=True, sums=S[4]), loads=((state["x"], X[:, :, :]),))

        for n, part in ((1, block_1), (2, block_2), (3, block_3)):
            if n in blocks:
                with ExitStack() as own:
                    part(own)

        if "left" in state:
            last_norm(*state["left"], S[0])


def to_units(w, cols=256):
    w = np.asarray(w)
    k, n = w.shape
    return np.ascontiguousarray(w.reshape(k // P, P, n // cols, cols).transpose(2, 1, 0, 3).reshape(n // cols, P, k // P * cols))


def channel_major(x):
    return np.ascontiguousarray(np.asarray(x).T.reshape(-1, P, x.shape[0]).transpose(1, 0, 2))


def per_channel(v):
    return np.asarray(v).reshape(-1, P).T


def layout(i):
    a = {}
    w = np.asarray(i["w_in"])[0]
    sizes = [("conv_a", 2048), ("conv_b", 2048), ("conv_z", 2048), ("gla_q", 1024), ("gla_k", 1024), ("gla_v", 2048),
             ("gla_z", 2048), ("alpha", 16), ("mem_q", 512), ("mem_z", 512), ("gate0", 2048), ("gate1", 2048), ("gate2", 2048)]
    at = 0
    for name, n in sizes:
        a[name] = to_units(w[:, at:at + n], min(n, 256))
        at += n
    a["gate2a"], a["gate2b"] = a["gate2"][:4], a.pop("gate2")[4:]
    a["conv_out"] = to_units(i["w_conv_out"][0])
    a["gla_out"] = to_units(i["w_gla_out"][0])
    a["mem_k"] = to_units(i["w_mem_kv"][0][:, :512])
    a["mem_v"] = to_units(i["w_mem_kv"][0][:, 512:])
    a["mem_out"] = to_units(i["w_mem_out"][0])
    a["w_out"] = to_units(i["w_out"][0])
    a["x_t"] = channel_major(np.asarray(i["x"])[0])
    a["mem_t"] = channel_major(np.asarray(i["mem"])[0])
    a["w_alpha2"] = np.ascontiguousarray(np.asarray(i["w_alpha2"])[0])
    cols = []
    for name, c in VECS:
        v = np.asarray(i[name])
        if name == "dw_w":
            cols.append(v[0].reshape(31, DC, P).transpose(2, 1, 0).reshape(P, -1))
        elif name == "rwkv_mu_3":
            cols.append(per_channel(v[:3072]))
            cols.append(np.concatenate([v[3072:].reshape(4, 96), np.zeros((4, 32), v.dtype)], 1).T)
        else:
            cols.append(per_channel(v))
    a["vecs"] = np.ascontiguousarray(np.concatenate(cols, 1))
    w = np.asarray(i["w_in_2"])[0]
    for name, lo, hi in (("sa_q", 0, 2048), ("sa_k", 2048, 2560), ("sa_v", 2560, 3072), ("sa_qi", 3072, 3584),
                         ("sgu_u", 3656, 5704), ("sgu_v", 5704, 7752), ("gate_a", 7752, 9800), ("gate_b", 9800, 11848)):
        a[name] = to_units(w[:, lo:hi])
    a["sa_ki"] = to_units(np.concatenate([w[:, 3584:3648]] * 2, 1), 128)
    a["sa_wi"] = to_units(w[:, 3648:3656], 8)
    a["w_out_2"] = to_units(i["w_out_2"][0])
    w1, w2 = np.asarray(i["w_ff1_2"])[0], np.asarray(i["w_ff2_2"])[0]
    for c in range(4):
        a[f"ff1_{c}"] = to_units(w1[:, c * D:(c + 1) * D])
        a[f"ff2_{c}"] = to_units(w2[c * D:(c + 1) * D])
    a["rel_bias"] = np.asarray(i["rel_bias_2"])
    a["sgu_g"], a["sgu_b"] = np.asarray(i["sgu_ln_g_2"]), np.asarray(i["sgu_ln_b_2"])
    a["sgu_w"] = np.ascontiguousarray(np.asarray(i["sgu_w_2"])[0].transpose(2, 0, 1))
    a["sgu_bias"] = np.asarray(i["sgu_b_2"]).reshape(1, D)
    w = np.asarray(i["w_in_3"])
    for name, lo, hi in (("rwkv_rk", 1088, 3136), ("rwkv_v", 3136, 4160), ("z_mla", 4544, 5568), ("z_rwkv", 5568, 6592),
                         ("gate_mla", 6592, 8640), ("gate_rwkv", 8640, 10688), ("mla_qkv_a", 0, 1024)):
        a[name] = to_units(w[:, lo:hi])
    a["rwkv_da"] = to_units(w[:, 4160:4544], 192)
    kr, krs = w[:, 1024:1088], np.concatenate([w[:, 1056:1088], w[:, 1024:1056]], 1)
    a["mla_k_rope"] = to_units(np.concatenate([kr, kr, krs, krs], 1))
    wq = np.asarray(i["mla_wq_b_3"]).reshape(512, 8, 192)
    a["mla_q_nope"] = to_units(wq[:, :, :128].reshape(512, 1024))
    a["mla_q_rope"] = to_units(np.concatenate([wq[:, :, 128:].reshape(512, 512),
                                               np.concatenate([wq[:, :, 160:], wq[:, :, 128:160]], 2).reshape(512, 512)], 1))
    wkv = np.asarray(i["mla_wkv_b_3"]).reshape(512, 8, 256)
    a["mla_k_nope"] = to_units(wkv[:, :, :128].reshape(512, 1024))
    a["mla_v"] = to_units(wkv[:, :, 128:].reshape(512, 1024))
    a["br_mla"] = to_units(i["w_br_mla_3"])
    a["br_rwkv"] = to_units(i["w_br_rwkv_3"])
    a["w_out_3"] = to_units(i["w_out_3"])
    a["rwkv_w2"] = np.ascontiguousarray(np.stack([np.asarray(i[n]) for n in ("rwkv_w2_f_3", "rwkv_w2_b_3", "rwkv_a2_f_3", "rwkv_a2_b_3")], 1)
                                        .reshape(96, DC, T))
    a["ones"] = np.ones((P, P), np.float32)
    a["ident"] = np.eye(P, dtype=np.float32)
    s, t = np.arange(P)[:, None], np.arange(P)[None, :]
    m = np.zeros((P, 8, P), np.float32)
    for l in range(GLA_LEVELS):
        m[:, l] = ((s >> (l + 1)) == (t >> (l + 1))) & (((s >> l) & 1) == 0) & (((t >> l) & 1) == 1)
    m[:, 7] = s == t
    a["level_masks"] = m
    a["exchange"] = (s + t == P - 1).astype(np.float32)
    a["causal_t"] = (s <= t).astype(np.float32)
    key, query = np.arange(T)[None, None, :], (np.arange(TT)[None, :, None] * P + np.arange(P)[:, None, None])
    a["causal"] = np.stack([key <= query, np.where(key <= query, 0, NEG)], 1).astype(np.float32)
    dist = np.maximum(T - 1 - np.arange(512), 0)
    large = 16 + (np.log(np.maximum(dist, 1).astype(np.float32) / np.float32(16)) / np.float32(np.log(8.0)) * np.float32(16)).astype(np.int32)
    bucket = np.where(dist < 16, dist, np.minimum(large, 31))
    a["bucket_onehot"] = (np.arange(32)[:, None] == bucket[None, :]).astype(np.float32)
    a["head_ones"] = ((s // 64) == (t // 64)).astype(np.float32)
    cm = np.zeros((P, 2, 2, P), np.float32)
    m_ts, m_st = np.zeros((P, 2, P), np.float32), np.zeros((P, 2, P), np.float32)
    same64, same16 = (s // 64) == (t // 64), (s // 16) == (t // 16)
    for d, strict in enumerate((s < t, s > t)):
        cm[:, d, 0], cm[:, d, 1] = same64 & strict, same64 & (strict | (s == t))
        m_st[:, d] = same16 & strict
        m_ts[:, d] = (same16 & strict).T
    a["chunk_masks"], a["mask16_ts"], a["mask16_st"] = cm, m_ts, m_st
    a["chunk_reset"] = np.tile((np.arange(T) % 64 != 0).astype(np.float32), (P, 1))
    freq = np.float32(10000.0) ** (-np.arange(0, 64, 2, dtype=np.float32) / np.float32(64))
    ang = (np.arange(T, dtype=np.float32)[:, None] * freq[None, :]).astype(np.float32).T
    rot = np.zeros((P, 2, T), np.float32)
    for r in range(4):
        rot[32 * r:32 * r + 32, 0] = np.cos(ang)
        rot[32 * r:32 * r + 32, 1] = np.sin(ang) * (1 if r % 2 else -1)
    a["rotary"] = rot
    return a


def kernel(**inputs):
    import concourse.bacc as bacc
    from concourse.bass_utils import run_bass_kernel_spmd
    nc = bacc.Bacc("TRN2", target_bir_lowering=False, num_devices=1)
    arrays = layout(inputs)
    ins = {k: nc.dram_tensor("in_" + k, v.shape, F32, kind="ExternalInput").ap() for k, v in arrays.items()}
    out = nc.dram_tensor("out", (P, DC, T), F32, kind="ExternalOutput").ap()
    build(nc, ins, out, BLOCKS)
    r = run_bass_kernel_spmd(nc, [{"in_" + k: v for k, v in arrays.items()}], core_ids=[0])
    y = r.results[0]["out"]
    return np.ascontiguousarray(y.transpose(1, 0, 2).reshape(D, T).T)[None]
```
